# Optimizing a Trainium2 kernel written in Bass

```python
import jax, jax.numpy as jnp
from jax import lax
import numpy as np
import math

D_MODEL = 1024
BATCH = 1
SEQ = 256
DEPTH = 1

N_HEADS = 8
HEAD_DIM = 64
ATTN_WIDTH = N_HEADS * HEAD_DIM
KV_RANK = 128
IDX_HEADS = 8
IDX_DIM = 64
TOPK_MAX = 256
Q_BLOCK = 128
CHUNK = 128
GMLP_GROUPS = 4
GMLP_GROUP_DIM = 128
GMLP_WIDTH = GMLP_GROUPS * GMLP_GROUP_DIM
NUM_BUCKETS = 32
MAX_DISTANCE = 128
N_GROUPS = 4
EXPERTS_PER_GROUP = 8
N_EXPERTS = N_GROUPS * EXPERTS_PER_GROUP
TOP_K_INNER = 2
D_FF_EXPERT = 256
EPS = 1e-6
IN_SIZES = (ATTN_WIDTH, KV_RANK, IDX_HEADS * IDX_DIM, IDX_DIM, IDX_HEADS, GMLP_WIDTH, GMLP_WIDTH, D_MODEL, D_MODEL)
IN_COLS = ATTN_WIDTH + KV_RANK + IDX_HEADS * IDX_DIM + IDX_DIM + IDX_HEADS + 2 * GMLP_WIDTH + 2 * D_MODEL


def rms_norm(x, g):
    xf = x.astype(jnp.float32)
    y = xf * lax.rsqrt(jnp.mean(xf * xf, axis=-1, keepdims=True) + EPS)
    return y.astype(x.dtype) * g

def layer_norm(x, g, b):
    xf = x.astype(jnp.float32)
    mu = jnp.mean(xf, axis=-1, keepdims=True)
    var = jnp.mean(jnp.square(xf - mu), axis=-1, keepdims=True)
    return ((xf - mu) * lax.rsqrt(var + EPS)).astype(x.dtype) * g + b

def t5_bucket(n):
    max_exact = NUM_BUCKETS // 2
    nf = jnp.maximum(n, 1).astype(jnp.float32)
    large = max_exact + (jnp.log(nf / max_exact) / np.float32(np.log(MAX_DISTANCE / max_exact)) * (NUM_BUCKETS - max_exact)).astype(jnp.int32)
    large = jnp.minimum(large, NUM_BUCKETS - 1)
    return jnp.where(n < max_exact, n, large)

def sparse_attention(q_lat, q_idx, w_idx, c_kv, k_idx, rel_bias):
    B, T = c_kv.shape[:2]
    nb = T // Q_BLOCK
    topk = min(TOPK_MAX, T // 4)
    scale = HEAD_DIM ** -0.5
    s_pos = jnp.arange(T, dtype=jnp.int32)

    def to_blocks(a):
        return jnp.moveaxis(a.reshape((B, nb, Q_BLOCK) + a.shape[2:]), 1, 0)

    def block(args):
        blk, ql, qi, wi = args
        t_pos = blk * Q_BLOCK + jnp.arange(Q_BLOCK, dtype=jnp.int32)
        rel = jax.nn.relu(jnp.einsum('bqhd,bsd->bqhs', qi, k_idx))
        index = jnp.einsum('bqhs,bqh->bqs', rel, wi)
        causal = s_pos[None, :] <= t_pos[:, None]
        index = jnp.where(causal[None], index, -jnp.inf)
        _, sel = lax.top_k(index, topk)
        c_sel = jax.vmap(lambda c, i: c[i])(c_kv, sel)
        dist = t_pos[None, :, None] - sel
        valid = dist >= 0
        bias = rel_bias[t5_bucket(jnp.maximum(dist, 0))]
        scores = jnp.einsum('bqhr,bqkr->bqhk', ql, c_sel).astype(jnp.float32) * scale
        scores = scores + jnp.transpose(bias, (0, 1, 3, 2)).astype(jnp.float32)
        scores = jnp.where(valid[:, :, None, :], scores, -jnp.inf)
        p = jax.nn.softmax(scores, axis=-1).astype(c_sel.dtype)
        return jnp.einsum('bqhk,bqkr->bqhr', p, c_sel)

    out = lax.map(block, (jnp.arange(nb, dtype=jnp.int32), to_blocks(q_lat), to_blocks(q_idx), to_blocks(w_idx)))
    return jnp.moveaxis(out, 0, 1).reshape(B, T, N_HEADS, KV_RANK)

def chunked_gmlp(u, v, ln_g, ln_b, w_s, b_s):
    B, T = u.shape[:2]
    u = jax.nn.gelu(u)
    v = layer_norm(jax.nn.gelu(v), ln_g, ln_b)
    vc = v.reshape(B, T // CHUNK, CHUNK, GMLP_GROUPS, GMLP_GROUP_DIM)
    mask = jnp.tril(jnp.ones((CHUNK, CHUNK), dtype=bool))
    ws = jnp.where(mask[None], w_s, 0.0)
    s = jnp.einsum('gij,bcjge->bcige', ws, vc) + jnp.transpose(b_s)[None, None, :, :, None]
    return u * s.reshape(B, T, GMLP_WIDTH)

def hier_moe(h, rg_w, rg_b, re_w, re_b, w_gate, w_up, w_down):
    N = h.shape[0]
    gp = jax.nn.softmax((h @ rg_w + rg_b).astype(jnp.float32), axis=-1)
    g_w, g_idx = lax.top_k(gp, 1)
    el = (h @ re_w + re_b).reshape(N, N_GROUPS, EXPERTS_PER_GROUP)
    el = jnp.take_along_axis(el, g_idx[:, :, None], axis=1)[:, 0]
    ep = jax.nn.softmax(el.astype(jnp.float32), axis=-1)
    e_w, e_idx = lax.top_k(ep, TOP_K_INNER)
    e_w = g_w * e_w / jnp.sum(e_w, axis=-1, keepdims=True)
    eid = g_idx * EXPERTS_PER_GROUP + e_idx
    comb = jnp.sum(jax.nn.one_hot(eid, N_EXPERTS, dtype=jnp.float32) * e_w[..., None], axis=1).astype(h.dtype)
    y = jnp.zeros_like(h)
    for e in range(N_EXPERTS):
        he = jax.nn.silu(h @ w_gate[e]) * (h @ w_up[e])
        y = y + comb[:, e:e + 1] * (he @ w_down[e])
    return y

def first_inputs(seed: int = 0) -> dict:
    key = jax.random.key(seed)
    ks = jax.random.split(key, 24)

    def nrm(k, shape, s):
        return jax.random.normal(k, shape, jnp.float32) * s

    return {
        "x": nrm(ks[0], (BATCH, SEQ, D_MODEL), 1.0),
        "w_in": nrm(ks[1], (DEPTH, D_MODEL, IN_COLS), D_MODEL ** -0.5),
        "kv_norm_g": 1.0 + nrm(ks[2], (DEPTH, KV_RANK), 0.01),
        "w_uk": nrm(ks[3], (DEPTH, KV_RANK, N_HEADS, HEAD_DIM), KV_RANK ** -0.5),
        "w_uv": nrm(ks[4], (DEPTH, KV_RANK, N_HEADS, HEAD_DIM), KV_RANK ** -0.5),
        "rel_bias": nrm(ks[5], (NUM_BUCKETS, N_HEADS), 0.5),
        "ln_v_g": 1.0 + nrm(ks[6], (DEPTH, GMLP_WIDTH), 0.01),
        "ln_v_b": nrm(ks[7], (DEPTH, GMLP_WIDTH), 0.01),
        "w_spatial": nrm(ks[8], (DEPTH, GMLP_GROUPS, CHUNK, CHUNK), CHUNK ** -0.5),
        "b_spatial": 1.0 + nrm(ks[9], (DEPTH, GMLP_GROUPS, CHUNK), 0.01),
        "w_proj_a": nrm(ks[10], (DEPTH, ATTN_WIDTH, D_MODEL), ATTN_WIDTH ** -0.5),
        "w_proj_b": nrm(ks[11], (DEPTH, GMLP_WIDTH, D_MODEL), GMLP_WIDTH ** -0.5),
        "w_out": nrm(ks[12], (DEPTH, D_MODEL, D_MODEL), D_MODEL ** -0.5),
        "norm1_g": 1.0 + nrm(ks[13], (DEPTH, D_MODEL), 0.01),
        "norm2_g": 1.0 + nrm(ks[14], (DEPTH, D_MODEL), 0.01),
        "router_group_w": nrm(ks[15], (DEPTH, D_MODEL, N_GROUPS), D_MODEL ** -0.5),
        "router_group_b": nrm(ks[16], (DEPTH, N_GROUPS), 0.01),
        "router_expert_w": nrm(ks[17], (DEPTH, D_MODEL, N_EXPERTS), D_MODEL ** -0.5),
        "router_expert_b": nrm(ks[18], (DEPTH, N_EXPERTS), 0.01),
        "w_gate": nrm(ks[19], (DEPTH, N_EXPERTS, D_MODEL, D_FF_EXPERT), D_MODEL ** -0.5),
        "w_up": nrm(ks[20], (DEPTH, N_EXPERTS, D_MODEL, D_FF_EXPERT), D_MODEL ** -0.5),
        "w_down": nrm(ks[21], (DEPTH, N_EXPERTS, D_FF_EXPERT, D_MODEL), D_FF_EXPERT ** -0.5),
        "final_norm_g": 1.0 + nrm(ks[22], (D_MODEL,), 0.01),
    }

def first_block(x, w_in, kv_norm_g, w_uk, w_uv, rel_bias, ln_v_g, ln_v_b, w_spatial, b_spatial, w_proj_a, w_proj_b, w_out, norm1_g, norm2_g, router_group_w, router_group_b, router_expert_w, router_expert_b, w_gate, w_up, w_down, final_norm_g):
    B, T, D = x.shape
    splits = [int(c) for c in np.cumsum(IN_SIZES)[:-1]]
    idx_scale = (IDX_HEADS ** -0.5) * (IDX_DIM ** -0.5)
    for l in range(DEPTH):
        h = rms_norm(x, norm1_g[l])
        proj = h @ w_in[l]
        q, ckv, qi, ki, wi, u, v, ga, gb = jnp.split(proj, splits, axis=-1)
        q = q.reshape(B, T, N_HEADS, HEAD_DIM)
        c_kv = rms_norm(ckv, kv_norm_g[l])
        q_lat = jnp.einsum('bthd,rhd->bthr', q, w_uk[l])
        q_idx = qi.reshape(B, T, IDX_HEADS, IDX_DIM)
        w_idx = wi * idx_scale
        o_lat = sparse_attention(q_lat, q_idx, w_idx, c_kv, ki, rel_bias)
        o_a = jnp.einsum('bthr,rhd->bthd', o_lat, w_uv[l]).reshape(B, T, ATTN_WIDTH)
        y_a = o_a @ w_proj_a[l]
        y_b = chunked_gmlp(u, v, ln_v_g[l], ln_v_b[l], w_spatial[l], b_spatial[l]) @ w_proj_b[l]
        merged = jax.nn.sigmoid(ga) * y_a + jax.nn.sigmoid(gb) * y_b
        x = x + merged @ w_out[l]
        h2 = rms_norm(x, norm2_g[l]).reshape(B * T, D)
        y = hier_moe(h2, router_group_w[l], router_group_b[l], router_expert_w[l], router_expert_b[l], w_gate[l], w_up[l], w_down[l])
        x = x + y.reshape(B, T, D)
    return rms_norm(x, final_norm_g)


DEPTH_2 = 2

D_RG = D_MODEL
RG_HEADS = 8
RG_HEAD_DIM = D_RG // RG_HEADS
D_ML = D_MODEL
ML_HEADS = 4
ML_HEAD_DIM = D_ML // ML_HEADS
D_MIX = D_RG + D_ML
D_IN = 2 * D_RG + 3 * D_ML
CONV_WIDTH = 4
RG_C = 8.0
ML_CHUNK = 128


def rms_norm_2(x, g):
    x32 = x.astype(jnp.float32)
    y = x32 * lax.rsqrt(jnp.mean(x32 * x32, axis=-1, keepdims=True) + EPS)
    return (y * g.astype(jnp.float32)).astype(x.dtype)

def causal_depthwise_conv(x, w, b):
    ch = x.shape[-1]
    y = lax.conv_general_dilated(
        x, w[:, None, :].astype(x.dtype), window_strides=(1,),
        padding=[(CONV_WIDTH - 1, 0)], dimension_numbers=("NWC", "WIO", "NWC"),
        feature_group_count=ch)
    return y + b.astype(x.dtype)

def block_diag(x, w):
    h, dh, dout = w.shape
    xb = x.reshape(x.shape[:-1] + (h, dh))
    return jnp.einsum("bshd,hde->bshe", xb, w).reshape(x.shape[:-1] + (h * dout,))

def rglru(x, w_a, b_a, w_x, b_x, lam):
    r = jax.nn.sigmoid(block_diag(x, w_a) + b_a).astype(jnp.float32)
    i = jax.nn.sigmoid(block_diag(x, w_x) + b_x).astype(jnp.float32)
    log_a = -RG_C * r * jax.nn.softplus(-lam.astype(jnp.float32))
    a = jnp.exp(log_a)
    u = jnp.sqrt(-jnp.expm1(2.0 * log_a)) * (i * x.astype(jnp.float32))

    def combine(lhs, rhs):
        a1, b1 = lhs
        a2, b2 = rhs
        return a1 * a2, a2 * b1 + b2

    _, h = lax.associative_scan(combine, (a, u), axis=1)
    return h.astype(x.dtype)

def mlstm_chunkwise(q, k, v, log_i, log_f):
    bsz, s_len, nh, dh = q.shape
    nc = s_len // ML_CHUNK

    def to_chunks(t):
        return t.reshape(bsz, nc, ML_CHUNK, nh, dh).transpose(1, 0, 3, 2, 4)

    def gate_chunks(t):
        return t.reshape(bsz, nc, ML_CHUNK, nh).transpose(1, 0, 3, 2)

    causal = jnp.tril(jnp.ones((ML_CHUNK, ML_CHUNK), dtype=bool))

    def step(carry, xs):
        c_st, n_st, m_st = carry
        qc, kc, vc, li, lf = xs
        b = jnp.cumsum(lf, axis=-1)
        b_last = b[..., -1]
        d = jnp.where(causal, b[..., :, None] - b[..., None, :] + li[..., None, :], -jnp.inf)
        m_inter = b + m_st[..., None]
        m_t = jnp.maximum(m_inter, jnp.max(d, axis=-1))
        w_intra = jnp.exp(d - m_t[..., None])
        w_inter = jnp.exp(m_inter - m_t)
        s = jnp.einsum("bhtk,bhsk->bhts", qc, kc) * w_intra
        num = (jnp.einsum("bhts,bhsv->bhtv", s, vc)
               + w_inter[..., None] * jnp.einsum("bhtk,bhkv->bhtv", qc, c_st))
        den = jnp.sum(s, axis=-1) + w_inter * jnp.einsum("bhtk,bhk->bht", qc, n_st)
        h = num / jnp.maximum(jnp.abs(den), jnp.exp(-m_t))[..., None]
        g = b_last[..., None] - b + li
        m_new = jnp.maximum(b_last + m_st, jnp.max(g, axis=-1))
        w_state = jnp.exp(g - m_new[..., None])
        decay = jnp.exp(b_last + m_st - m_new)
        kw = kc * w_state[..., None]
        c_new = decay[..., None, None] * c_st + jnp.einsum("bhsk,bhsv->bhkv", kw, vc)
        n_new = decay[..., None] * n_st + jnp.sum(kw, axis=2)
        return (c_new, n_new, m_new), h

    init = (jnp.zeros((bsz, nh, dh, dh), jnp.float32),
            jnp.zeros((bsz, nh, dh), jnp.float32),
            jnp.zeros((bsz, nh), jnp.float32))
    _, h = lax.scan(step, init, (to_chunks(q), to_chunks(k), to_chunks(v),
                                 gate_chunks(log_i), gate_chunks(log_f)))
    return h.transpose(1, 0, 3, 2, 4).reshape(bsz, s_len, nh, dh)

def mlstm_branch(xm, o_pre, conv_w, conv_b, w_q, w_k, w_v, w_if, b_if, head_g):
    bsz, s_len, _ = xm.shape
    xc = jax.nn.silu(causal_depthwise_conv(xm, conv_w, conv_b))
    q = block_diag(xc, w_q)
    k = block_diag(xc, w_k)
    v = block_diag(xm, w_v)
    gates = (jnp.concatenate([q, k, v], axis=-1) @ w_if + b_if).astype(jnp.float32)
    log_i = gates[..., :ML_HEADS]
    log_f = jax.nn.log_sigmoid(gates[..., ML_HEADS:])

    def heads(t):
        return t.reshape(bsz, s_len, ML_HEADS, ML_HEAD_DIM).astype(jnp.float32)

    cell = mlstm_chunkwise(heads(q), heads(k) * (ML_HEAD_DIM ** -0.5), heads(v), log_i, log_f)
    h = jax.nn.sigmoid(heads(o_pre)) * cell
    h = h * lax.rsqrt(jnp.mean(h * h, axis=-1, keepdims=True) + EPS)
    return (h.reshape(bsz, s_len, D_ML) * head_g.astype(jnp.float32)).astype(xm.dtype)

def second_inputs(seed: int = 0) -> dict:
    key = jax.random.key(seed)
    ks = jax.random.split(key, 24)
    f32 = jnp.float32

    def nrm(k, shape, scale):
        return jax.random.normal(k, shape, f32) * scale

    x = jax.random.normal(ks[0], (BATCH, SEQ, D_MODEL), f32)
    c = jax.random.normal(ks[1], (BATCH, D_MODEL), f32)
    norm_g = 1.0 + nrm(ks[2], (DEPTH_2, D_MODEL), 0.02)
    w_ada = nrm(ks[3], (DEPTH_2, D_MODEL, 3 * D_MODEL), 0.3 * D_MODEL ** -0.5)
    b_ada = nrm(ks[4], (DEPTH_2, 3 * D_MODEL), 0.02)
    w_in = nrm(ks[5], (DEPTH_2, D_MODEL, D_IN), D_MODEL ** -0.5)
    rg_conv_w = nrm(ks[6], (DEPTH_2, CONV_WIDTH, D_RG), CONV_WIDTH ** -0.5)
    rg_conv_b = nrm(ks[7], (DEPTH_2, D_RG), 0.02)
    rg_w_a = nrm(ks[8], (DEPTH_2, RG_HEADS, RG_HEAD_DIM, RG_HEAD_DIM), RG_HEAD_DIM ** -0.5)
    rg_b_a = nrm(ks[9], (DEPTH_2, D_RG), 0.02)
    rg_w_x = nrm(ks[10], (DEPTH_2, RG_HEADS, RG_HEAD_DIM, RG_HEAD_DIM), RG_HEAD_DIM ** -0.5)
    rg_b_x = nrm(ks[11], (DEPTH_2, D_RG), 0.02)
    a_c = jax.random.uniform(ks[12], (DEPTH_2, D_RG), f32, 0.9, 0.999)
    a0 = a_c ** (1.0 / RG_C)
    rg_lambda = jnp.log(a0) - jnp.log1p(-a0)
    ml_conv_w = nrm(ks[13], (DEPTH_2, CONV_WIDTH, D_ML), CONV_WIDTH ** -0.5)
    ml_conv_b = nrm(ks[14], (DEPTH_2, D_ML), 0.02)
    ml_w_q = nrm(ks[15], (DEPTH_2, ML_HEADS, ML_HEAD_DIM, ML_HEAD_DIM), ML_HEAD_DIM ** -0.5)
    ml_w_k = nrm(ks[16], (DEPTH_2, ML_HEADS, ML_HEAD_DIM, ML_HEAD_DIM), ML_HEAD_DIM ** -0.5)
    ml_w_v = nrm(ks[17], (DEPTH_2, ML_HEADS, ML_HEAD_DIM, ML_HEAD_DIM), ML_HEAD_DIM ** -0.5)
    ml_w_if = nrm(ks[18], (DEPTH_2, 3 * D_ML, 2 * ML_HEADS), 0.1 * (3 * D_ML) ** -0.5)
    b_i = nrm(ks[19], (DEPTH_2, ML_HEADS), 0.1) - 1.0
    b_f = jnp.linspace(3.0, 6.0, ML_HEADS, dtype=f32)[None, :] + nrm(ks[20], (DEPTH_2, ML_HEADS), 0.1)
    ml_b_if = jnp.concatenate([b_i, b_f], axis=-1)
    ml_norm_g = 1.0 + nrm(ks[21], (DEPTH_2, D_ML), 0.02)
    w_out = nrm(ks[22], (DEPTH_2, D_MIX, D_MODEL), D_MIX ** -0.5)
    final_g = 1.0 + nrm(ks[23], (D_MODEL,), 0.02)
    return {"x": x, "c": c, "norm_g": norm_g, "w_ada": w_ada, "b_ada": b_ada,
            "w_in": w_in, "rg_conv_w": rg_conv_w, "rg_conv_b": rg_conv_b,
            "rg_w_a": rg_w_a, "rg_b_a": rg_b_a, "rg_w_x": rg_w_x, "rg_b_x": rg_b_x,
            "rg_lambda": rg_lambda, "ml_conv_w": ml_conv_w, "ml_conv_b": ml_conv_b,
            "ml_w_q": ml_w_q, "ml_w_k": ml_w_k, "ml_w_v": ml_w_v, "ml_w_if": ml_w_if,
            "ml_b_if": ml_b_if, "ml_norm_g": ml_norm_g, "w_out": w_out, "final_g": final_g}

def second_block(x, c, norm_g, w_ada, b_ada, w_in, rg_conv_w, rg_conv_b, rg_w_a, rg_b_a,
              rg_w_x, rg_b_x, rg_lambda, ml_conv_w, ml_conv_b, ml_w_q, ml_w_k, ml_w_v,
              ml_w_if, ml_b_if, ml_norm_g, w_out, final_g):
    split_pts = [D_RG, 2 * D_RG, 2 * D_RG + D_ML, 2 * D_RG + 2 * D_ML]
    c_act = jax.nn.silu(c)
    for l in range(DEPTH_2):
        mod = c_act @ w_ada[l] + b_ada[l]
        shift, scale, gate = jnp.split(mod, 3, axis=-1)
        h = rms_norm_2(x, norm_g[l]) * (1.0 + scale[:, None, :]) + shift[:, None, :]
        u = h @ w_in[l]
        rg_x, rg_z, ml_x, ml_o, ml_z = jnp.split(u, split_pts, axis=-1)
        y_rg = rglru(causal_depthwise_conv(rg_x, rg_conv_w[l], rg_conv_b[l]),
                     rg_w_a[l], rg_b_a[l], rg_w_x[l], rg_b_x[l], rg_lambda[l]) * jax.nn.silu(rg_z)
        y_ml = mlstm_branch(ml_x, ml_o, ml_conv_w[l], ml_conv_b[l], ml_w_q[l], ml_w_k[l],
                            ml_w_v[l], ml_w_if[l], ml_b_if[l], ml_norm_g[l]) * jax.nn.silu(ml_z)
        y = jnp.concatenate([y_rg, y_ml], axis=-1) @ w_out[l]
        x = x + gate[:, None, :] * y
    return rms_norm_2(x, final_g)


def setup_inputs(seed=0):
    out = dict(first_inputs(seed))
    for name, value in second_inputs(seed + 1).items():
        if name != "x":
            out[name + "_2"] = value
    return out


def reference(
    x, w_in, kv_norm_g, w_uk, w_uv, rel_bias, ln_v_g, ln_v_b, w_spatial, b_spatial, w_proj_a,
    w_proj_b, w_out, norm1_g, norm2_g, router_group_w, router_group_b, router_expert_w,
    router_expert_b, w_gate, w_up, w_down, final_norm_g, c_2, norm_g_2, w_ada_2, b_ada_2,
    w_in_2, rg_conv_w_2, rg_conv_b_2, rg_w_a_2, rg_b_a_2, rg_w_x_2, rg_b_x_2, rg_lambda_2,
    ml_conv_w_2, ml_conv_b_2, ml_w_q_2, ml_w_k_2, ml_w_v_2, ml_w_if_2, ml_b_if_2, ml_norm_g_2,
    w_out_2, final_g_2,
):
    x = first_block(
        x, w_in, kv_norm_g, w_uk, w_uv, rel_bias, ln_v_g, ln_v_b, w_spatial, b_spatial,
        w_proj_a, w_proj_b, w_out, norm1_g, norm2_g, router_group_w, router_group_b,
        router_expert_w, router_expert_b, w_gate, w_up, w_down, final_norm_g,
    )
    return second_block(
        x, c_2, norm_g_2, w_ada_2, b_ada_2, w_in_2, rg_conv_w_2, rg_conv_b_2, rg_w_a_2,
        rg_b_a_2, rg_w_x_2, rg_b_x_2, rg_lambda_2, ml_conv_w_2, ml_conv_b_2, ml_w_q_2, ml_w_k_2,
        ml_w_v_2, ml_w_if_2, ml_b_if_2, ml_norm_g_2, w_out_2, final_g_2,
    )


_drawn_inputs = setup_inputs


def setup_inputs(seed=0):
    import zlib

    import numpy as np

    out = dict(_drawn_inputs(seed))
    spreads = {}
    factors = {'kv_norm_g': 4.859,
     'ln_v_g': 8.0,
     'ln_v_b': 8.0,
     'b_spatial': 8.0,
     'norm2_g': 3.461,
     'router_group_b': 3.947,
     'router_expert_b': 3.647,
     'final_norm_g': 5.505,
     'norm_g_2': 8.0,
     'rg_conv_b_2': 6.334,
     'rg_w_a_2': 3.06,
     'rg_b_a_2': 8.0,
     'rg_b_x_2': 8.0,
     'ml_conv_b_2': 8.0,
     'ml_w_if_2': 8.0,
     'ml_norm_g_2': 8.0,
     'final_g_2': 2.854}
    for name, (base, spread) in spreads.items():
        noise = np.random.default_rng([zlib.crc32(name.encode()), seed]).standard_normal(out[name].shape)
        drawn = base * np.exp(spread * noise) if base else spread * noise
        out[name] = __import__('jax').numpy.asarray(drawn.astype(out[name].dtype))
    for name, factor in factors.items():
        out[name] = (out[name] * factor).astype(out[name].dtype)
    return out
```

```python
from contextlib import ExitStack

import numpy as np
import concourse.bass as bass
from concourse import mybir

F32 = mybir.dt.float32
ALU = mybir.AluOpType
ACT = mybir.ActivationFunctionType
AX = mybir.AxisListType

P = 128
T = 256
TT = T // P
D = 1024
KB = D // P
HEADS, HD = 8, 64
RANK = 128
TOPK = min(256, T // 4)
BUCKETS = 32
GROUPS, GDIM = 4, 128
EG, EPG = 4, 8
EXPERTS = EG * EPG
FF = 256
EPS = 1e-6
LAYERS = 2
MLH, MLD = 4, 256
TAPS = 4
PAD = TAPS - 1
XW = T + 4
VW = MLD + 1
CW = 256
RING = 6
BIG = 1e30
MASKED, TAKEN = -1e38, -3e38
SCALE = HD ** -0.5
IDX_SCALE = (8 ** -0.5) * (64 ** -0.5)
C_Q, C_CKV, C_QI, C_KI, C_WI, C_U, C_V, C_GA, C_GB = 0, 512, 640, 1152, 1216, 1224, 1736, 2248, 3272
V_NORM, V_ADA, V_RCW, V_MCW, V_RCB, V_BA, V_BX, V_LAM = 0, 8, 32, 64, 96, 104, 112, 120
LOG1P = [1.0 / k for k in (17, 15, 13, 11, 9, 7, 5, 3)]


class Banks:

    def __init__(self, banks, done, free):
        self.banks, self.done, self.free = banks, done, free
        self.put, self.got, self.names = 0, 0, {}

    def acquire(self, pe, name=None):
        n = self.put
        self.put += 1
        self.names[name] = n + 1
        if n >= len(self.banks):
            pe.wait_ge(self.free, n + 1 - len(self.banks))
        return self.banks[n % len(self.banks)]

    def take(self, eng):
        n = self.got
        self.got += 1
        eng.wait_ge(self.done, n + 1)
        return self.banks[n % len(self.banks)]

    def upto(self, name):
        return self.names[name]


class Chain:

    def __init__(self, eng, sem):
        self.eng, self.sem, self.count = eng, sem, {}

    def __call__(self, ins, sem=None):
        sem = sem or self.sem
        n = self.count.get(sem.name, 0) + 1
        self.count[sem.name] = n
        ins.then_inc(sem, 1)
        self.eng.wait_ge(sem, n)


def build(nc, a, out):
    with ExitStack() as ctx:
        def sb(name, shape):
            return ctx.enter_context(nc.sbuf_tensor(name, shape, F32))

        def sem(name):
            return ctx.enter_context(nc.semaphore(name))

        psum = [ctx.enter_context(nc.psum_tensor(f"bank{i}", [P, 512], F32)) for i in range(8)]

        ring = [sb(f"ring{i}", [P, KB * CW]) for i in range(RING)]
        x = sb("x", [P, TT, D])
        hT = sb("hT", [P, KB, T])
        tmp = sb("tmp", [P, 2048])
        rxp = sb("rxp", [P, KB * XW])
        mxp = sb("mxp", [P, KB * XW])
        s0, s1, s2, s3, s4 = (sb(f"s{i}", [P, MLH * 2 * VW]) for i in range(5))
        z0, z1, s5, s6, s7 = (sb(n, [P, 2048]) for n in ("z0", "z1", "s5", "s6", "s7"))
        vaug_t = sb("vaug", [P, TT * MLH * VW])
        w4 = sb("w4", [P, 1024])
        gateB = sb("gateB", [P, D])
        oth_t = sb("oth", [P, 2048])
        ident = sb("ident", [P, P])
        anti = sb("anti", [P, P])
        later = sb("later", [P, P])
        ones = sb("ones", [1, P])
        onesr = sb("onesr", [MLH, P])
        sel4 = sb("sel4", [MLH, MLH, P])
        rowsA = sb("rowsA", [32, P])
        colA = sb("colA", [P, 32])
        rowsL = sb("rowsL", [P, LAYERS, P])
        rowsM = sb("rowsM", [16, LAYERS, P])
        colL = sb("colL", [P, LAYERS, P])
        colM = sb("colM", [P, LAYERS, 16])
        small = sb("small", [P, 64])
        rt_b = sb("rt_b", [1, EG + EXPERTS])
        wif = sb("wif", [P, LAYERS, 24, 8])
        bif = sb("bif", [MLH, LAYERS, 2])
        csil = sb("csil", [P, KB])
        modc = sb("modc", [P, 16])
        gs = sb("gs", [P, KB])
        n4 = sb("n4", [P, 2, KB])
        lam = sb("lam", [P, 5, LAYERS, KB])
        hb = sb("hb", [P, LAYERS, 2 * KB])
        gnat = sb("gnat", [P, TT, 8])
        rsc = sb("rsc", [MLH, 4])
        cols = sb("cols", [P, 4, MLH])
        logit = sb("logit", [P, TT, EG + EXPERTS])
        comb = sb("comb", [P, TT, EXPERTS])
        rt = sb("rt", [P, 128])
        desc = sb("desc", [P, EPG])
        m8 = sb("m8", [P, 8])

        lneg, labs, lsp, ly, lt = (lam[:, i, :, :] for i in range(5))
        squares = s7[:, :].rearrange("p (t d) -> p t d", t=TT)

        xn = tmp[:, :].rearrange("p (t d) -> p t d", t=TT)
        qT = s0[:, 0:1024].rearrange("p (b t) -> p b t", b=4)
        qiT = s0[:, 1024:2048].rearrange("p (b t) -> p b t", b=4)
        kvT = s1[:, 0:1024].rearrange("p (b t) -> p b t", b=4)
        vnat = s1[:, 1024:2048].rearrange("p (s c) -> p s c", s=TT)
        biasT = s2[:, 0:2048].rearrange("p (h j) -> p h j", h=HEADS)
        idx = s3[:, 0:512].rearrange("p (t s) -> p t s", t=TT)
        maskb = s3[:, 512:1024].rearrange("p (t s) -> p t s", t=TT)
        relu = s3[:, 1024:1536].rearrange("p (b s) -> p b s", b=2)
        sc = s3[:, 1536:2048].rearrange("p (t s) -> p t s", t=TT)
        prob = [[tmp[:, 384 * i:384 * i + P], tmp[:, 384 * i + P:384 * i + 3 * P]] for i in range(2)]
        pT = s4[:, 0:768].rearrange("p (b s q) -> p b s q", b=2, s=3)
        kiT = s4[:, 768:1024]
        cT = s4[:, 1024:1280]
        ckv = s4[:, 1280:1536].rearrange("p (t r) -> p t r", t=TT)
        wi = s4[:, 1536:1552].rearrange("p (t h) -> p t h", t=TT)
        vst = s4[:, 1552:1568]
        bkt = s4[0:BUCKETS, 1568:2056]
        tga = z0[:, :].rearrange("p (b t) -> p b t", b=KB)
        tgb = z1[:, :].rearrange("p (b t) -> p b t", b=KB)
        guT = s5[:, 0:1024].rearrange("p (b t) -> p b t", b=GROUPS)
        gv = s5[:, 1024:2048].rearrange("p (t c) -> p t c", t=TT)
        gmT = s6[:, 0:1024].rearrange("p (b t) -> p b t", b=GROUPS)
        oaT = s6[:, 1024:2048].rearrange("p (b t) -> p b t", b=4)
        mgT = s7[:, :].rearrange("p (b t) -> p b t", b=KB)
        mtmp = vaug_t[:, 0:512].rearrange("p (b t) -> p b t", b=2)
        reltab = vaug_t[0:BUCKETS, 512:1024]
        relw = vaug_t[0:BUCKETS, 1024:1032]
        relrow = vaug_t[0:HEADS, 1032:1544]
        wuk = w4[:, 0:512]
        wuv = w4[:, 512:1024]
        lng = gateB[:, 0:512]
        lnb = gateB[:, 512:1024]
        wsn = oth_t[:, 0:512].rearrange("p (g j) -> p g j", g=GROUPS)
        wsT = oth_t[:, 512:1024].rearrange("p (g j) -> p g j", g=GROUPS)
        bsp = rxp[0:1, 0:512]
        wi_w = mxp[:, 0:64].rearrange("p (k n) -> p k n", k=KB)
        rt_w = mxp[:, 64:64 + KB * (EG + EXPERTS)].rearrange("p (k n) -> p k n", k=KB)
        heT = s5[:, 0:1024].rearrange("p (e b t) -> p e b t", e=2, b=2)
        thg = s5[:, 1024:2048].rearrange("p (e n) -> p e n", e=2)
        sg = s6[:, 0:512]
        gfin = gateB
        rxv = rxp[:, :].rearrange("p (b t) -> p b t", b=KB)
        mxv = mxp[:, :].rearrange("p (b t) -> p b t", b=KB)

        def v8(s):
            return s[:, 0:2048].rearrange("p (b t) -> p b t", b=KB)
        rxc, thr, thi, aa, tl = v8(s0), v8(s1), v8(s2), v8(s3), v8(s4)
        zr, zm = v8(z0), v8(z1)
        mc, mqT, mkT = v8(s5), v8(s6), v8(s7)
        mth = v8(tmp)
        mvT = v8(s3)
        rows = s2[0:MLH, 0:8 * T].rearrange("p (r t) -> p r t", r=8)
        adab = z1[0:1, 0:D]
        cBC = v8(z0)[:, :, 0:P]
        ebuf = tmp[:, 256:512].rearrange("p (b t) -> p b t", b=2)
        stb = tmp[:, 512:768].rearrange("p (b t) -> p b t", b=2)
        hn = tmp[:, 768:768 + VW]
        inter = tmp[:, 1032:1032 + 2 * VW].rearrange("p (b c) -> p b c", b=2)
        vaug = vaug_t[:, :].rearrange("p (t h c) -> p t h c", t=TT, h=MLH)
        knat = w4[:, :].rearrange("p (h c) -> p h c", h=MLH)
        caug = s0[:, :].rearrange("p (h k c) -> p h k c", h=MLH, k=2)
        oth = oth_t[:, :].rearrange("p (t c) -> p t c", t=TT)
        hh = s3[:, 0:2048].rearrange("p (t c) -> p t c", t=TT)
        ymT = v8(s4)

        relscr = nc.dram_tensor("rel_scratch", (HEADS, 512), F32)
        relscr_ap = relscr.ap() if hasattr(relscr, "ap") else relscr

        diag = bass.AP(relscr_ap.tensor, 0, [[1, P], [512, HEADS], [1, T]])

        def bcast(ap, n):
            return bass.AP(ap.tensor, ap.offset, [[0, P], [1, n]])

        A = Banks(psum[0:4], sem("a_done"), sem("a_free"))
        B = Banks(psum[4:8], sem("b_done"), sem("b_free"))
        slot_full = [sem(f"slot_full{i}") for i in range(RING)]
        chunk_used = sem("chunk_used")
        s_act, s_dve, s_pool = sem("act_step"), sem("dve_step"), sem("pool_step")
        S = {n: sem(n) for n in (
            "x_loaded", "rows_loaded", "small_loaded", "attn_loaded", "rel_loaded", "const_ready", "rowsL_loaded",
            "ssq_ready", "root_wanted", "root_ready", "xn_ready", "relrow_ready", "relrow_stored", "bias_loaded",
            "relu_used", "idx_ready", "idx_masked", "sel_ready", "mask_ready", "sc_ready", "p_ready",
            "prob_ready", "cT_wanted", "ws_masked", "vln_ready", "mg_ready", "cbc_ready", "csil_ready", "gate_b_loaded",
            "exp_wanted", "exp_ready", "comb_ready", "tanh_gate", "silu_ready", "he_ready", "gu_done",
            "gate_done", "down_done", "down_out", "gfin_loaded", "x_stored", "mod_ready", "conv_ready", "rg_gate", "rg_root_wanted",
            "rg_root", "mconv_ready", "mtanh_ready", "mc_ready", "pads_ready", "lf_wanted", "lf_ready",
            "row_wanted", "row_ready", "kw_ready", "hh_ready", "hq_ready", "y_ready",
            "adab_loaded", "layer_done", "sp_wanted", "sp_ready", "csil_wanted", "csil_tanh", "hT_ready", "ln_loaded",
            "z_used", "rg_done", "oth_ready", "ckv_ready", "rstd_used", "hb_ready")}

        def cols_of(w, c, n=CW):
            return w[:, c:c + n].rearrange("(k p) c -> p k c", p=P)

        w_in = a["w_in"][0]
        chunks = []
        def add(*parts):
            chunks.append(parts)
        full = lambda t: t[:, :].rearrange("p (k c) -> p k c", k=KB)
        def colpart(lo, n):
            return lambda t: full(t)[:, :, lo:lo + n]
        add((colpart(0, 128), cols_of(w_in, C_CKV, 128)), (colpart(128, 64), cols_of(w_in, C_KI, 64)),
            (colpart(192, 64), cols_of(w_in, C_KI, 64)))
        for c in (C_Q, C_QI, C_U, C_V):
            for j in range(2):
                add((full, cols_of(w_in, c + j * CW)))
        for c in (C_GA, C_GB):
            for j in range(4):
                add((full, cols_of(w_in, c + j * CW)))
        for j in range(4):
            add((lambda t: full(t)[:, 0:4, :], cols_of(a["w_proj_a"][0], j * CW)),
                (lambda t: full(t)[:, 4:8, :], cols_of(a["w_proj_b"][0], j * CW)))
        for j in range(4):
            add((full, cols_of(a["w_out"][0], j * CW)))
        first_expert_chunk = len(chunks)
        assert first_expert_chunk == 25
        NB1 = first_expert_chunk
        tail = []
        def addt(*parts):
            tail.append(parts)
        for l in range(LAYERS):
            for j in range(12):
                addt((full, cols_of(a["w_ada_2"][l], j * CW)))
            wi2 = a["w_in_2"][l]
            for j in range(4):
                addt((full, cols_of(wi2, j * CW)))
            addt((colpart(0, 128), a["rg_w_a_2"][l].rearrange("h d e -> d h e")),
                 (colpart(128, 128), a["rg_w_x_2"][l].rearrange("h d e -> d h e")))
            for c in (D, 2 * D):
                for j in range(4):
                    addt((full, cols_of(wi2, c + j * CW)))
            for n in ("ml_w_q_2", "ml_w_k_2", "ml_w_v_2"):
                addt((full, a[n][l].rearrange("h (k p) e -> p (h k) e", p=P)))
            for c in (3 * D, 4 * D):
                for j in range(4):
                    addt((full, cols_of(wi2, c + j * CW)))
            for j in range(4):
                for kh in range(2):
                    addt((full, cols_of(a["w_out_2"][l][kh * D:(kh + 1) * D, :], j * CW)))
        E0 = NB1
        L0 = NB1 + 3 * EXPERTS

        block = ctx.enter_context(nc.Block())

        nparts = [len(c) for c in chunks] + [1] * (3 * EXPERTS) + [len(c) for c in tail]
        fill_value, filled = [], [0] * RING
        for n, k in enumerate(nparts):
            filled[n % RING] += 16 * k
            fill_value.append(filled[n % RING])

        chunk_free = []

        @block.tensor
        def _(pe):
            state = {"n": 0, "free": 0}

            def chunk(k=None):
                n = state["n"]
                state["n"] += 1
                pe.wait_ge(slot_full[n % RING], fill_value[n])
                return ring[n % RING]

            def tr(dst, src, k=P):
                return pe.transpose(dst, src, ident[0:k, 0:k])

            def transpose_x(ready, tag):
                pe.wait_ge(S["xn_ready"], ready)
                for kb in range(KB):
                    b = B.acquire(pe, f"hT{tag}{kb}")
                    for tt in range(TT):
                        m = tr(b[:, tt * P:(tt + 1) * P], xn[:, tt, kb * P:(kb + 1) * P])
                    m.then_inc(B.done, 1)

            def projT(w, m, rhs, pool, name=None, nk=KB, k0=0):
                b = pool.acquire(pe, name)
                for kb in range(nk):
                    mm = pe.matmul(b[:, 0:T], w[:, (k0 + kb) * CW + m * P:(k0 + kb) * CW + (m + 1) * P], rhs[:, kb, :],
                                   start=(kb == 0), stop=(kb == nk - 1))
                mm.then_inc(pool.done, 1)
                return mm

            def used(pool=A, mm=None):
                if mm is None:
                    chunk_free.append((pool.done, pool.put))
                else:
                    state["free"] += 1
                    mm.then_inc(chunk_used, 1)
                    chunk_free.append((chunk_used, state["free"]))

            pe.wait_ge(S["const_ready"], 1)
            pe.wait_ge(S["rows_loaded"], 16 * 5)
            b = B.acquire(pe, "colA")
            tr(b[:, 0:25], rowsA[0:25, :], 25).then_inc(B.done, 1)
            pe.wait_ge(S["rel_loaded"], 32)
            b = B.acquire(pe, "relrow")
            pe.matmul(b[0:HEADS, :], relw, reltab, start=True, stop=True).then_inc(B.done, 1)
            pe.wait_ge(S["rowsL_loaded"], 16 * 20)
            for l in range(LAYERS):
                b = B.acquire(pe, f"colL{l}")
                tr(b[:, 0:P], rowsL[:, l, :])
                tr(b[:, P:P + 16], rowsM[:, l, :], 16).then_inc(B.done, 1)

            transpose_x(1, "A")
            pe.wait_ge(B.free, B.upto("hTA7"))

            w = chunk()
            wv = full(w)
            for tt in range(TT):
                b = A.acquire(pe, f"ckv{tt}")
                for kb in range(KB):
                    mm = pe.matmul(b[:, 0:RANK], hT[:, kb, tt * P:(tt + 1) * P], wv[:, kb, 0:RANK],
                                   start=(kb == 0), stop=(kb == KB - 1))
                mm.then_inc(A.done, 1)
            projT(w, 1, hT, A, "kiT")
            used()
            pe.wait_ge(S["small_loaded"], 16 * 5)
            b = A.acquire(pe, "wi")
            for tt in range(TT):
                for kb in range(KB):
                    mm = pe.matmul(b[:, tt * 8:tt * 8 + 8], hT[:, kb, tt * P:(tt + 1) * P], wi_w[:, kb, :],
                                   start=(kb == 0), stop=(kb == KB - 1))
            mm.then_inc(A.done, 1)
            for name in ("q", "qi"):
                for j in range(2):
                    w = chunk()
                    for m in range(2):
                        projT(w, m, hT, A, f"{name}{2 * j + m}")
                    used()
            pe.wait_ge(A.free, A.upto("qi3"))
            for tt in range(TT):
                ns = (tt + 1) * P
                for h in range(HEADS):
                    o = (h % 2) * 64
                    b = A.acquire(pe, f"idx{tt}{h}")
                    pe.matmul(b[:, 0:ns], qiT[o:o + 64, h // 2, tt * P:(tt + 1) * P], kiT[o:o + 64, 0:ns],
                              start=True, stop=True).then_inc(A.done, 1)
            pe.wait_ge(S["ckv_ready"], 1)
            b = B.acquire(pe, "cT")
            for tt in range(TT):
                mm = tr(b[:, tt * P:(tt + 1) * P], ckv[:, tt, :])
            mm.then_inc(B.done, 1)
            pe.wait_ge(B.free, B.upto("cT"))
            pe.wait_ge(S["attn_loaded"], 32)
            for m in range(4):
                b = A.acquire(pe, f"K{m}")
                pe.matmul(b[:, 0:T], wuk[:, m * P:(m + 1) * P], cT, start=True, stop=True).then_inc(A.done, 1)
            for tt in range(TT):
                b = A.acquire(pe, f"V{tt}")
                pe.matmul(b[:, :], cT[:, tt * P:(tt + 1) * P], wuv, start=True, stop=True).then_inc(A.done, 1)
            for j in range(2):
                w = chunk()
                for m in range(2):
                    projT(w, m, hT, A, f"u{2 * j + m}")
                used()
            for j in range(2):
                w = full(chunk())
                for tt in range(TT):
                    b = A.acquire(pe, f"v{j}{tt}")
                    for kb in range(KB):
                        mm = pe.matmul(b[:, 0:CW], hT[:, kb, tt * P:(tt + 1) * P], w[:, kb, :],
                                       start=(kb == 0), stop=(kb == KB - 1))
                    mm.then_inc(A.done, 1)
                used()
            pe.wait_ge(S["ws_masked"], 1)
            b = A.acquire(pe, "wsT")
            for g in range(GROUPS):
                mm = tr(b[:, g * P:(g + 1) * P], wsn[:, g, :])
            mm.then_inc(A.done, 1)

            gate_jobs = [(j, m) for j in range(8) for m in range(2)]
            gst = {}

            def gate_job():
                if not gate_jobs:
                    return
                j, m = gate_jobs.pop(0)
                if m == 0:
                    gst["w"] = chunk()
                projT(gst["w"], m, hT, A, f"g{2 * j + m}")
                if m == 1:
                    used()

            for h in range(HEADS + 1):
                gate_job()
                if h < HEADS:
                    o = (h % 2) * 64
                    for tt in range(TT):
                        ns = (tt + 1) * P
                        b = B.acquire(pe, f"S{h}{tt}")
                        if (h, tt) == (0, 0):
                            pe.wait_ge(S["bias_loaded"], 16)
                        pe.matmul(b[:, 0:ns], anti[:, :], biasT[:, h, T - ns:T], start=True, stop=False)
                        pe.matmul(b[:, 0:ns], qT[o:o + 64, h // 2, tt * P:(tt + 1) * P], kvT[o:o + 64, h // 2, 0:ns],
                                  start=False, stop=True).then_inc(B.done, 1)
                gate_job()
                if h >= 1:
                    g = h - 1
                    o = (g % 2) * 64
                    pe.wait_ge(S["prob_ready"], 2 * g + 2)
                    b = A.acquire(pe, f"pT{g}")
                    pn = prob[g % 2]
                    tr(b[:, 0:P], pn[0][:, 0:P])
                    tr(b[:, P:2 * P], pn[1][:, 0:P])
                    tr(b[:, 2 * P:3 * P], pn[1][:, P:2 * P]).then_inc(A.done, 1)
                    pe.wait_ge(A.free, A.upto(f"pT{g}"))
                    b = A.acquire(pe, f"o{g}")
                    pe.matmul(b[o:o + 64, 0:P], vnat[:, 0, g * HD:(g + 1) * HD], pT[:, g % 2, 0, :],
                              start=True, stop=True)
                    for st in range(2):
                        mm = pe.matmul(b[o:o + 64, P:2 * P], vnat[:, st, g * HD:(g + 1) * HD], pT[:, g % 2, 1 + st, :],
                                       start=(st == 0), stop=(st == 1))
                    mm.then_inc(A.done, 1)
            assert not gate_jobs
            pe.wait_ge(S["vln_ready"], 1)
            pe.wait_ge(S["ln_loaded"], 48)
            pe.wait_ge(A.free, A.upto("wsT"))
            for g in range(GROUPS):
                b = B.acquire(pe, f"gm{g}")
                for c in range(TT):
                    pe.matmul(b[:, c * P:(c + 1) * P], ones[0:1, :], bsp[0:1, g * P:(g + 1) * P], start=True, stop=False)
                    mm = pe.matmul(b[:, c * P:(c + 1) * P], gv[:, c, g * P:(g + 1) * P], wsT[:, g, :],
                                   start=False, stop=True)
                mm.then_inc(B.done, 1)
            pe.wait_ge(B.free, B.upto("gm3"))
            pe.wait_ge(A.free, A.upto("o7"))
            for j in range(4):
                w = chunk()
                for m in range(2):
                    projT(w, m, oaT, B, f"ya{2 * j + m}", 4, 0)
                    projT(w, m, gmT, B, f"yb{2 * j + m}", 4, 4)
                used(B)
            pe.wait_ge(S["mg_ready"], KB)
            for j in range(4):
                w = full(chunk())
                for tt in range(TT):
                    b = B.acquire(pe, f"xo{j}{tt}")
                    for kb in range(KB):
                        mm = pe.matmul(b[:, 0:CW], mgT[:, kb, tt * P:(tt + 1) * P], w[:, kb, :],
                                       start=(kb == 0), stop=(kb == KB - 1))
                    mm.then_inc(B.done, 1)
                used(B)

            transpose_x(2, "B")
            pe.wait_ge(B.free, B.upto("hTB7"))
            b = B.acquire(pe, "router")
            NR = EG + EXPERTS
            for tt in range(TT):
                for kb in range(KB):
                    pe.matmul(b[:, tt * NR:(tt + 1) * NR], hT[:, kb, tt * P:(tt + 1) * P], rt_w[:, kb, :],
                              start=(kb == 0), stop=False)
                mm = pe.matmul(b[:, tt * NR:(tt + 1) * NR], ones[0:1, :], rt_b[0:1, :], start=False, stop=True)
            mm.then_inc(B.done, 1)
            pe.wait_ge(B.free, B.upto("router"))
            pe.wait_ge(A.free, A.put)

            def gate_up(e, par, wg, wu):
                if not isinstance(e, int) or e >= 2:
                    pe.wait_ge(S["he_ready"], e - 1)
                for w, bank, done in ((wg, psum[par], S["gate_done"]), (wu, psum[2 + par], S["gu_done"])):
                    pe.wait_ge(slot_full[w[0]], w[1])
                    wt = ring[w[0]]
                    for m in range(2):
                        for kb in range(KB):
                            mm = pe.matmul(bank[:, m * T:(m + 1) * T], wt[:, kb * CW + m * P:kb * CW + (m + 1) * P],
                                           hT[:, kb, :], start=(kb == 0), stop=(kb == KB - 1))
                    mm.then_inc(done, 1)

            def down(e, par, wd):
                pe.wait_ge(S["he_ready"], e + 1)
                if not isinstance(e, int) or e >= 1:
                    pe.wait_ge(S["down_out"], e * 4)
                pe.wait_ge(slot_full[wd[0]], wd[1])
                wt = ring[wd[0]][:, :].rearrange("p (k c) -> p k c", k=2)
                for tt in range(TT):
                    for hf in range(2):
                        for k in range(2):
                            mm = pe.matmul(psum[4 + 2 * tt + hf][:, :], heT[:, par, k, tt * P:(tt + 1) * P],
                                           wt[:, k, hf * 512:(hf + 1) * 512], start=(k == 0), stop=(k == 1))
                        mm.then_inc(S["down_done"], 1)

            def at(n):
                return n % RING, fill_value[n]

            def at_i(n0, i):
                return n0 % RING, i * 16 + fill_value[n0]

            gate_up(0, 0, at(E0), at(E0 + 1))
            for e in range(2):
                n = E0 + 2 + 3 * e
                gate_up(e + 1, (e + 1) % 2, at(n), at(n + 1))
                down(e, e, at(n + 2))
            with pe.Fori(1, (EXPERTS - 2) // 2) as i:
                for j in range(2):
                    n0 = E0 + 2 + 3 * j
                    gate_up(i * 2 + (j + 1), (j + 1) % 2, at_i(n0, i), at_i(n0 + 1, i))
                    down(i * 2 + j, j, at_i(n0 + 2, i))
            n0 = E0 + 2 + 3 * (EXPERTS - 2)
            gate_up(EXPERTS - 1, 1, at(n0), at(n0 + 1))
            down(EXPERTS - 2, 0, at(n0 + 2))
            down(EXPERTS - 1, 1, at(n0 + 3))
            state["n"] = L0
            G, U, Dn = (lambda e: (S["gate_done"], e + 1)), (lambda e: (S["gu_done"], e + 1)), \
                (lambda e: (S["down_done"], 4 * e + 4))
            chunk_free.extend([G(0), U(0)])
            for e in range(EXPERTS - 1):
                chunk_free.extend([G(e + 1), U(e + 1), Dn(e)])
            chunk_free.append(Dn(EXPERTS - 1))
            assert len(chunk_free) == L0
            pe.wait_ge(S["down_out"], 4 * EXPERTS)

            for l in range(LAYERS):
                pe.wait_ge(S["csil_ready"], 1)
                b = A.acquire(pe, f"mod{l}")
                for j in range(8):
                    w = chunk()
                    for m in range(2):
                        c = 2 * j + m
                        for kb in range(KB):
                            mm = pe.matmul(b[:, c:c + 1], w[:, kb * CW + m * P:kb * CW + (m + 1) * P],
                                           csil[:, kb:kb + 1], start=(kb == 0), stop=(kb == KB - 1))
                    if j < 7:
                        used(mm=mm)
                mm.then_inc(A.done, 1)
                used()
                pe.wait_ge(S["cbc_ready"], l + 1)
                pe.wait_ge(S["adab_loaded"], 16 * (l + 1))
                for j in range(4):
                    w = full(chunk())
                    b = A.acquire(pe, f"gate{l}{j}")
                    for kb in range(KB):
                        pe.matmul(b[:, 0:CW], cBC[:, kb, :], w[:, kb, :], start=(kb == 0), stop=False)
                    pe.matmul(b[:, 0:CW], ones[0:1, :], adab[0:1, j * CW:(j + 1) * CW], start=False,
                              stop=True).then_inc(A.done, 1)
                    used()
                transpose_x(3 + l, f"L{l}")
                pe.wait_ge(B.free, B.upto(f"hTL{l}7"))
                for j in range(4):
                    w = chunk()
                    for m in range(2):
                        projT(w, m, hT, A, f"rx{l}{2 * j + m}")
                    used()
                w = full(chunk())
                for h in range(KB):
                    pe.wait_ge(S["conv_ready"], l * KB + h + 1)
                    b = A.acquire(pe, f"ri{l}{h}")
                    pe.matmul(b[:, 0:T], w[:, h, 0:P], rxc[:, h, :], start=True, stop=True)
                    pe.matmul(b[:, T:2 * T], w[:, h, P:2 * P], rxc[:, h, :], start=True, stop=True).then_inc(A.done, 1)
                used()
                for name in ("rz", "mx"):
                    for j in range(4):
                        w = chunk()
                        for m in range(2):
                            projT(w, m, hT, A, f"{name}{l}{2 * j + m}")
                        used()
                wq = full(chunk())
                pe.wait_ge(S["mc_ready"], l * KB + KB)

                def headT(w, src, name):
                    for h in range(MLH):
                        b = A.acquire(pe, f"{name}{l}{h}")
                        for m in range(2):
                            for k in range(2):
                                mm = pe.matmul(b[:, m * T:(m + 1) * T], w[:, 2 * h + k, m * P:(m + 1) * P],
                                               src(2 * h + k), start=(k == 0), stop=(k == 1))
                        mm.then_inc(A.done, 1)
                headT(wq, lambda k: mc[:, k, :], "mq")
                used()
                wk = full(chunk())
                headT(wk, lambda k: mc[:, k, :], "mk")
                for hp in range(2):
                    b = A.acquire(pe, f"kn{l}{hp}")
                    for h in range(2):
                        for k in range(2):
                            mm = pe.matmul(b[:, h * MLD:(h + 1) * MLD], mc[:, 2 * (2 * hp + h) + k, 0:P],
                                           wk[:, 2 * (2 * hp + h) + k, :], start=(k == 0), stop=(k == 1))
                    mm.then_inc(A.done, 1)
                used()
                wv2 = full(chunk())
                headT(wv2, lambda k: mxv[:, k, PAD:PAD + T], "mv")
                for tt in range(TT):
                    for hp in range(2):
                        b = A.acquire(pe, f"vn{l}{tt}{hp}")
                        for h in range(2):
                            for k in range(2):
                                kk = 2 * (2 * hp + h) + k
                                mm = pe.matmul(b[:, h * MLD:(h + 1) * MLD],
                                               mxv[:, kk, PAD + tt * P:PAD + (tt + 1) * P],
                                               wv2[:, kk, :], start=(k == 0), stop=(k == 1))
                        mm.then_inc(A.done, 1)
                used()
                pe.wait_ge(A.free, A.upto(f"mv{l}3"))
                pe.wait_ge(S["gate_b_loaded"], 16 * 3 * LAYERS)
                b = A.acquire(pe, f"gt{l}")
                for tt in range(TT):
                    for k in range(24):
                        src = (mqT, mkT, mvT)[k // 8]
                        mm = pe.matmul(b[:, tt * 8:tt * 8 + 8], src[:, k % 8, tt * P:(tt + 1) * P], wif[:, l, k, :],
                                       start=(k == 0), stop=(k == 23))
                mm.then_inc(A.done, 1)
                pe.wait_ge(A.free, A.upto(f"gt{l}"))
                b = B.acquire(pe, f"gr{l}")
                for g in range(2):
                    for tt in range(TT):
                        mm = tr(b[0:MLH, g * T + tt * P:g * T + (tt + 1) * P], gnat[:, tt, g * 4:g * 4 + 4])
                mm.then_inc(B.done, 1)
                for j in range(4):
                    w = full(chunk())
                    for tt in range(TT):
                        b = A.acquire(pe, f"mo{l}{j}{tt}")
                        for kb in range(KB):
                            mm = pe.matmul(b[:, 0:CW], hT[:, kb, tt * P:(tt + 1) * P], w[:, kb, :],
                                           start=(kb == 0), stop=(kb == KB - 1))
                        mm.then_inc(A.done, 1)
                    used()
                for j in range(4):
                    w = chunk()
                    for m in range(2):
                        projT(w, m, hT, A, f"mz{l}{2 * j + m}")
                    used()
                pe.wait_ge(S["row_ready"], 3 * (l + 1))
                b = B.acquire(pe, f"cols{l}")
                for n, (r, o) in enumerate(((6, 0), (6, P), (2, 0), (2, P))):
                    mm = tr(b[:, n * MLH:(n + 1) * MLH], rows[:, r, o:o + P], MLH)
                mm.then_inc(B.done, 1)
                for c in range(TT):
                    for h in range(MLH):
                        b = A.acquire(pe, f"E{l}{c}{h}")
                        pe.matmul(b[:, 0:P], rows[:, 3, c * P:(c + 1) * P], sel4[:, h, :], start=True, stop=False)
                        pe.matmul(b[:, 0:P], sel4[:, h, :], rows[:, 5, c * P:(c + 1) * P], start=False, stop=False)
                        pe.matmul(b[:, 0:P], ident[:, :], later[:, :], start=False, stop=True).then_inc(A.done, 1)
                        b = B.acquire(pe, f"St{l}{c}{h}")
                        for k in range(2):
                            mm = pe.matmul(b[:, 0:P], mkT[:, 2 * h + k, c * P:(c + 1) * P],
                                           mqT[:, 2 * h + k, c * P:(c + 1) * P], start=(k == 0), stop=(k == 1))
                        mm.then_inc(B.done, 1)
                        if c == 1:
                            b = A.acquire(pe, f"in{l}{h}")
                            for k in range(2):
                                mm = pe.matmul(b[:, 0:VW], mqT[:, 2 * h + k, P:2 * P], caug[:, h, k, :],
                                               start=(k == 0), stop=(k == 1))
                            mm.then_inc(A.done, 1)
                        pe.wait_ge(B.free, B.upto(f"St{l}{c}{h}"))
                        b = B.acquire(pe, f"nm{l}{c}{h}")
                        pe.matmul(b[:, 0:VW], stb[:, h % 2, :], vaug[:, c, h, :], start=True, stop=True) \
                            .then_inc(B.done, 1)
                    if c == 0:
                        pe.wait_ge(S["kw_ready"], MLH * (l + 1))
                        pe.wait_ge(S["rg_done"], l + 1)
                        for h in range(MLH):
                            for k in range(2):
                                b = A.acquire(pe, f"C{l}{h}{k}")
                                pe.matmul(b[:, 0:VW], knat[:, h, k * P:(k + 1) * P], vaug[:, 0, h, :],
                                          start=True, stop=True).then_inc(A.done, 1)
                        pe.wait_ge(A.free, A.upto(f"C{l}31"))
                pe.wait_ge(S["hq_ready"], l + 1)
                for m in range(KB):
                    b = B.acquire(pe, f"ym{l}{m}")
                    for tt in range(TT):
                        mm = tr(b[:, tt * P:(tt + 1) * P], hh[:, tt, m * P:(m + 1) * P])
                    mm.then_inc(B.done, 1)
                pe.wait_ge(B.free, B.upto(f"ym{l}7"))
                for j in range(4):
                    bb = [B.acquire(pe, f"xo{l}{j}{tt}") for tt in range(TT)]
                    for kh, yT in ((0, thr), (1, ymT)):
                        w = full(chunk())
                        for tt in range(TT):
                            for kb in range(KB):
                                mm = pe.matmul(bb[tt][:, 0:CW], yT[:, kb, tt * P:(tt + 1) * P], w[:, kb, :],
                                               start=(kh == 0 and kb == 0), stop=(kh == 1 and kb == KB - 1))
                            if kh == 1:
                                mm.then_inc(B.done, 1)
                        if kh == 1:
                            used(B)
                        else:
                            used(mm=mm)
            assert state["n"] == len(nparts), state

        @block.sync
        def _(sp):
            sp.dma_start(x[:, 0, :], a["x"][0, 0:P, :]).then_inc(S["x_loaded"], 16)
            sp.dma_start(x[:, 1, :], a["x"][0, P:T, :]).then_inc(S["x_loaded"], 16)

            def load(n, parts):
                if n >= RING:
                    sp.wait_ge(*chunk_free[n - RING])
                for dst, src in parts:
                    sp.dma_start(dst(ring[n % RING]), src).then_inc(slot_full[n % RING], 16)

            for n, parts in enumerate(chunks):
                load(n, parts)

            def expert_part(e, kind):
                k = 2 if kind == "w_down" else KB
                return (lambda t: t[:, :].rearrange("p (k c) -> p k c", k=k),
                        a[kind][0, e].rearrange("(k p) c -> p k c", p=P))

            load(E0, [expert_part(0, "w_gate")])
            load(E0 + 1, [expert_part(0, "w_up")])
            for e in range(2):
                n = E0 + 2 + 3 * e
                load(n, [expert_part(e + 1, "w_gate")])
                load(n + 1, [expert_part(e + 1, "w_up")])
                load(n + 2, [expert_part(e, "w_down")])
            with sp.Fori(1, (EXPERTS - 2) // 2) as i:
                for j in range(2):
                    e = i * 2 + j
                    for k, (kind, which, (used_sem, used_value)) in enumerate((
                            ("w_gate", i * 2 + (j + 1), (S["gate_done"], i * 2 + j)),
                            ("w_up", i * 2 + (j + 1), (S["gu_done"], i * 2 + j)),
                            ("w_down", e, (S["down_done"], i * 8 + (4 * j - 4))))):
                        n0 = E0 + 2 + 3 * j + k
                        sp.wait_ge(used_sem, used_value)
                        dst, src = expert_part(which, kind)
                        sp.dma_start(dst(ring[n0 % RING]), src).then_inc(slot_full[n0 % RING], 16)
            n = E0 + 2 + 3 * (EXPERTS - 2)
            load(n, [expert_part(EXPERTS - 1, "w_gate")])
            load(n + 1, [expert_part(EXPERTS - 1, "w_up")])
            load(n + 2, [expert_part(EXPERTS - 2, "w_down")])
            load(n + 3, [expert_part(EXPERTS - 1, "w_down")])

            for n, parts in enumerate(tail):
                load(L0 + n, parts)
            for tt in range(TT):
                sp.wait_ge(S["layer_done"], LAYERS + tt + 1)
                sp.dma_start(out[0, tt * P:(tt + 1) * P, :], xn[:, tt, :]).then_inc(S["x_stored"], 16)
            sp.wait_ge(S["x_stored"], 32)

        @block.scalar
        def _(act):
            step = Chain(act, s_act)
            f = act.activation

            def roots(n, view):
                act.wait_ge(S["root_wanted"], n)
                step(f(view, view, ACT.Sqrt), S["root_ready"])

            def sumsq():
                for tt in range(TT):
                    step(f(squares[:, tt, :], x[:, tt, :], ACT.Square, accum_out=small[:, tt:tt + 1]), S["ssq_ready"])

            def out_copy(dst, n, func=ACT.Copy, **k):
                b = A.take(act)
                step(f(dst, b[:, 0:n], func, **k), A.free)

            act.wait_ge(S["x_loaded"], 32)
            sumsq()
            roots(1, small[:, 2:4])
            act.wait_ge(B.free, B.upto("colA"))
            step(f(csil[:, :], colA[:, 17:25], ACT.Tanh, scale=0.5), S["csil_tanh"])
            for tt in range(TT):
                b = A.take(act)
                step(f(ckv[:, tt, :], b[:, 0:RANK], ACT.Copy))
                step(f(pT[:, 0, tt, :], b[:, 0:RANK], ACT.Square, accum_out=small[:, 4 + tt:5 + tt]), A.free)
            out_copy(kiT, T)
            b = A.take(act)
            step(f(wi, b[:, 0:16].rearrange("p (t h) -> p t h", t=TT), ACT.Copy, scale=IDX_SCALE), A.free)
            roots(2, small[:, 6:8])
            for m in range(4):
                out_copy(qT[:, m, :], T)
            for m in range(4):
                out_copy(qiT[:, m, :], T)
            for tt in range(TT):
                ns = (tt + 1) * P
                for h in range(HEADS):
                    k = tt * HEADS + h
                    b = A.take(act)
                    if k >= 2:
                        act.wait_ge(S["relu_used"], k - 1)
                    step(f(relu[:, k % 2, 0:ns], b[:, 0:ns], ACT.Relu), A.free)
            for m in range(4):
                out_copy(kvT[:, m, :], T)
            for tt in range(TT):
                out_copy(vnat[:, tt, :], 512)
            for m in range(4):
                out_copy(guT[:, m, :], T, ACT.Gelu_apprx_tanh)
            for j in range(2):
                for tt in range(TT):
                    out_copy(gv[:, tt, j * CW:(j + 1) * CW], CW, ACT.Gelu_apprx_tanh)
            out_copy(wsT, 512)
            roots(3, small[:, 12:14])
            gates = [(tga, m) for m in range(KB)] + [(tgb, m) for m in range(KB)]

            def gate_job():
                if gates:
                    t, m = gates.pop(0)
                    out_copy(t[:, m, :], T, ACT.Tanh, scale=0.5)

            for h in range(HEADS + 1):
                gate_job()
                if h < HEADS:
                    for tt in range(TT):
                        ns = (tt + 1) * P
                        k = 2 * h + tt
                        act.wait_ge(S["sc_ready"], k + 1)
                        if k >= 4:
                            act.wait_ge(A.done, A.upto(f"pT{h - 2}"))
                        step(f(prob[h % 2][tt][:, 0:ns], sc[:, tt, 0:ns], ACT.Exp, bias=rt[:, tt:tt + 1],
                               accum_out=rt[:, 2 + tt:3 + tt]), S["p_ready"])
                gate_job()
                if h >= 1:
                    g = h - 1
                    o = (g % 2) * 64
                    b = A.take(act)
                    step(f(pT[:, g % 2, :, :], b[:, 0:384].rearrange("p (s q) -> p s q", s=3), ACT.Copy), A.free)
                    b = A.take(act)
                    step(f(oaT[o:o + 64, g // 2, :], b[o:o + 64, 0:T], ACT.Copy), A.free)
            act.wait_ge(B.free, B.upto("xo31"))
            sumsq()
            roots(4, small[:, 2:4])
            for tt in range(TT):
                for k in range(2):
                    act.wait_ge(S["exp_wanted"], 2 * tt + k + 1)
                    n = (EG, EPG)[k]
                    src = rt[:, 8:12] if k == 0 else rt[:, 16:24]
                    if k == 0:
                        step(f(rt[:, 12:16], src, ACT.Exp, accum_out=rt[:, 7:8]), S["exp_ready"])
                    else:
                        step(f(rt[:, 24:32], src, ACT.Exp), S["exp_ready"])

            def gate_tanh(e, par):
                act.wait_ge(S["gu_done"], e + 1)
                if isinstance(e, int) and e < 2:
                    pass
                else:
                    act.wait_ge(S["he_ready"], e - 1)
                f(thg[:, par, :], psum[par][:, :], ACT.Tanh, scale=0.5).then_inc(S["tanh_gate"], 1)

            gate_tanh(0, 0)
            gate_tanh(1, 1)
            with act.Fori(1, EXPERTS // 2) as i:
                for j in range(2):
                    gate_tanh(i * 2 + j, j)
            act.wait_ge(S["down_out"], 4 * EXPERTS)
            sumsq()
            roots(5, small[:, 2:4])
            act.wait_ge(S["sp_wanted"], 1)
            step(f(labs, labs, ACT.Exp, scale=-1.0), S["sp_ready"])
            for l in range(LAYERS):
                if l == 0:
                    act.wait_ge(S["rstd_used"], 1)
                else:
                    act.wait_ge(S["layer_done"], l)
                out_copy(modc[:, :], 16)
                for j in range(4):
                    out_copy(gateB[:, j * CW:(j + 1) * CW], CW)
                sumsq()
                roots(6 + 2 * l, small[:, 2:4])
                for m in range(KB):
                    out_copy(rxv[:, m, PAD:PAD + T], T)
                for h in range(KB):
                    b = A.take(act)
                    if h == 0:
                        act.wait_ge(S["mod_ready"], l + 1)
                    step(f(thr[:, h, :], b[:, 0:T], ACT.Tanh, scale=0.5, bias=hb[:, l, h:h + 1]))
                    step(f(thi[:, h, :], b[:, T:2 * T], ACT.Tanh, scale=0.5, bias=hb[:, l, KB + h:KB + h + 1]), A.free)
                for h in range(KB):
                    step(f(aa[:, h, :], thr[:, h, :], ACT.Exp, scale=n4[:, 1, h:h + 1], bias=n4[:, 1, h:h + 1]))
                    step(f(tl[:, h, :], thr[:, h, :], ACT.Tanh, scale=n4[:, 0, h:h + 1], bias=n4[:, 0, h:h + 1]),
                         S["rg_gate"])
                def silu_part(dst, th_dst, name):
                    for m in range(KB):
                        b = A.take(act)
                        step(f(dst[:, m, :], b[:, 0:T], ACT.Copy))
                        step(f(th_dst[:, m, :], b[:, 0:T], ACT.Tanh, scale=0.5), A.free)
                act.wait_ge(S["xn_ready"], 3 + l)
                act.wait_ge(B.free, B.upto(f"hTL{l}7"))
                silu_part(zr, mth, "rz")
                for m in range(KB):
                    out_copy(mxv[:, m, PAD:PAD + T], T)
                act.wait_ge(S["rg_root_wanted"], l + 1)
                step(f(tl[:, :, :], tl[:, :, :], ACT.Sqrt), S["rg_root"])
                for m in range(KB):
                    act.wait_ge(S["mconv_ready"], l * KB + m + 1)
                    step(f(mth[:, m, :], mc[:, m, :], ACT.Tanh, scale=0.5), S["mtanh_ready"])
                for h in range(MLH):
                    b = A.take(act)
                    step(f(mqT[:, 2 * h:2 * h + 2, :], b[:, :].rearrange("p (m t) -> p m t", m=2), ACT.Copy,
                           scale=0.5), A.free)
                for h in range(MLH):
                    b = A.take(act)
                    step(f(mkT[:, 2 * h:2 * h + 2, :], b[:, :].rearrange("p (m t) -> p m t", m=2), ACT.Copy,
                           scale=0.5), A.free)
                for hp in range(2):
                    b = A.take(act)
                    step(f(knat[:, 2 * hp:2 * hp + 2, :], b[:, :].rearrange("p (h c) -> p h c", h=2), ACT.Copy,
                           scale=0.5 * MLD ** -0.5), A.free)
                act.wait_ge(S["rg_done"], l + 1)
                for h in range(MLH):
                    b = A.take(act)
                    step(f(mvT[:, 2 * h:2 * h + 2, :], b[:, :].rearrange("p (m t) -> p m t", m=2), ACT.Copy), A.free)
                for tt in range(TT):
                    for hp in range(2):
                        b = A.take(act)
                        step(f(vaug[:, tt, 2 * hp:2 * hp + 2, 0:MLD], b[:, :].rearrange("p (h c) -> p h c", h=2),
                               ACT.Copy), A.free)
                b = A.take(act)
                step(f(gnat[:, :, :], b[:, 0:16].rearrange("p (t g) -> p t g", t=TT), ACT.Copy), A.free)
                act.wait_ge(S["lf_wanted"], l + 1)
                step(f(rows[:, 2, :], rows[:, 2, :], ACT.Exp, scale=-1.0), S["lf_ready"])
                for j in range(4):
                    for tt in range(TT):
                        out_copy(oth[:, tt, j * CW:(j + 1) * CW], CW, ACT.Tanh, scale=0.5)
                act.wait_ge(S["mc_ready"], l * KB + KB)
                silu_part(zm, mth, "mz")
                act.wait_ge(S["row_wanted"], l + 1)
                step(f(rows[:, 6, 0:P], rows[:, 3, 0:P], ACT.Exp, bias=rsc[:, 0:1]), S["row_ready"])
                step(f(rows[:, 6, P:T], rows[:, 5, P:T], ACT.Exp, bias=rsc[:, 1:2]), S["row_ready"])
                step(f(rows[:, 2, :], rows[:, 2, :], ACT.Exp, scale=-1.0), S["row_ready"])
                act.wait_ge(S["z_used"], 2 * (l + 1))
                for c in range(TT):
                    for h in range(MLH):
                        b = A.take(act)
                        k8 = l * 8 + c * MLH + h
                        if h >= 2:
                            act.wait_ge(B.free, B.upto(f"St{l}{c}{h - 2}"))
                        elif c == 1:
                            act.wait_ge(B.free, B.upto(f"St{l}0{h + 2}"))
                        step(f(ebuf[:, h % 2, :], b[:, 0:P], ACT.Exp), A.free)
                        if c == 1:
                            b = A.take(act)
                            act.wait_ge(B.free, B.upto(f"cols{l}"))
                            if h >= 2:
                                act.wait_ge(S["hh_ready"], k8 - 1)
                            step(f(inter[:, h % 2, :], b[:, 0:VW], ACT.Copy, scale=cols[:, 1, h:h + 1]), A.free)
                    if c == 0:
                        for h in range(MLH):
                            for k in range(2):
                                out_copy(caug[:, h, k, :], VW)
                for c in range(TT):
                    for h in range(MLH):
                        act.wait_ge(S["hh_ready"], l * 8 + c * MLH + h + 1)
                        step(f(mth[:, 0, :], hh[:, c, h * MLD:(h + 1) * MLD], ACT.Square,
                               accum_out=small[:, 16 + c * MLH + h:17 + c * MLH + h]), S["ssq_ready"])
                roots(7 + 2 * l, small[:, 24:32])
            act.wait_ge(S["layer_done"], LAYERS)
            sumsq()
            roots(6 + 2 * LAYERS, small[:, 2:4])

        @block.vector
        def _(v):
            step = Chain(v, s_dve)
            tsc, stt, tten = v.tensor_scalar, v.scalar_tensor_tensor, v.tensor_tensor
            roots_n = {"n": 0, "ssq": 0}

            def rstd(dst, src, scale):
                roots_n["n"] += 1
                step(tsc(dst, src, scale, EPS, ALU.mult, ALU.add), S["root_wanted"])
                v.wait_ge(S["root_ready"], roots_n["n"])
                step(v.reciprocal(dst, dst))

            def norm_x(out_view):
                roots_n["ssq"] += 2
                v.wait_ge(S["ssq_ready"], roots_n["ssq"])
                rstd(small[:, 2:4], small[:, 0:2], 1.0 / D)

            def take_hT(scale, shift=None):
                for kb in range(KB):
                    b = B.take(v)
                    if shift is None:
                        step(tsc(hT[:, kb, :], b[:, 0:T], scale[:, kb:kb + 1], None, ALU.mult), B.free)
                    else:
                        step(tsc(hT[:, kb, :], b[:, 0:T], scale[:, kb:kb + 1], shift[:, kb:kb + 1], ALU.mult, ALU.add),
                             B.free)

            def log1p(dst, e, y, t):
                step(tsc(t, e, 2.0, None, ALU.add))
                step(v.reciprocal(t, t))
                step(tten(y, e, t, ALU.mult))
                step(tten(t, y, y, ALU.mult))
                step(tsc(dst, t, LOG1P[0], None, ALU.mult))
                for c in LOG1P[1:]:
                    step(stt(dst, dst, c, t, ALU.add, ALU.mult))
                step(stt(dst, dst, 1.0, y, ALU.add, ALU.mult))
                step(tsc(dst, dst, 2.0, None, ALU.mult))

            norm_x(None)
            for tt in range(TT):
                ins = tsc(xn[:, tt, :], x[:, tt, :], small[:, 2 + tt:3 + tt], None, ALU.mult)
                step(ins, S["xn_ready"]) if tt == 1 else step(ins)
            b = B.take(v)
            step(v.tensor_copy(colA[:, 0:25], b[:, 0:25]), B.free)
            b = B.take(v)
            step(v.tensor_copy(relrow, b[0:HEADS, :]), B.free)
            for l in range(LAYERS):
                b = B.take(v)
                step(v.tensor_copy(colL[:, l, :], b[:, 0:P]))
                step(v.tensor_copy(colM[:, l, :], b[:, P:P + 16]), B.free)
            take_hT(colA[:, 0:8])
            v.wait_ge(S["csil_tanh"], 1)
            step(stt(csil[:, :], csil[:, :], 1.0, colA[:, 17:25], ALU.add, ALU.mult))
            step(tsc(csil[:, :], csil[:, :], 0.5, None, ALU.mult), S["csil_ready"])
            v.wait_ge(A.free, A.upto("ckv1"))
            rstd(small[:, 6:8], small[:, 4:6], 1.0 / RANK)
            for tt in range(TT):
                ins = tsc(ckv[:, tt, :], ckv[:, tt, :], small[:, 6 + tt:7 + tt], None, ALU.mult)
                step(ins, S["ckv_ready"]) if tt == 1 else step(ins)
            v.wait_ge(A.free, A.upto("wi"))
            for tt in range(TT):
                ns = (tt + 1) * P
                for h in range(HEADS):
                    v.wait_ge(A.free, A.upto(f"idx{tt}{h}"))
                    k = tt * HEADS + h
                    r = relu[:, k % 2, 0:ns]
                    if h == 0:
                        step(tsc(idx[:, tt, 0:ns], r, wi[:, tt, h:h + 1], None, ALU.mult), S["relu_used"])
                    else:
                        step(stt(idx[:, tt, 0:ns], r, wi[:, tt, h:h + 1], idx[:, tt, 0:ns], ALU.mult, ALU.add),
                             S["relu_used"])
            b = B.take(v)
            step(tsc(cT, b[:, 0:T], colA[:, 16:17], None, ALU.mult), B.free)
            for tt in range(TT):
                ns = (tt + 1) * P
                v.wait_ge(S["idx_masked"], tt + 1)
                for r in range(TOPK // 8):
                    step(v.max(m8[:, :], idx[:, tt, 0:ns]))
                    step(v.match_replace(idx[:, tt, 0:ns], m8[:, :], idx[:, tt, 0:ns], TAKEN))
                step(tsc(maskb[:, tt, 0:ns], idx[:, tt, 0:ns], TAKEN, None, ALU.is_equal))
                step(tsc(maskb[:, tt, 0:ns], maskb[:, tt, 0:ns], -1.0, BIG, ALU.add, ALU.mult), S["sel_ready"])
            v.wait_ge(A.free, A.upto("v11"))
            for tt in range(TT):
                step(v.bn_stats(vst[:, 0:6], gv[:, tt, :]))
                step(v.bn_aggr(vst[:, 8 + 2 * tt:10 + 2 * tt], vst[:, 0:6]))
                step(v.tensor_copy(small[:, 12 + tt:13 + tt], vst[:, 9 + 2 * tt:10 + 2 * tt]))
            rstd(small[:, 12:14], small[:, 12:14], 1.0)
            v.wait_ge(S["ln_loaded"], 48)
            for tt in range(TT):
                step(tsc(gv[:, tt, :], gv[:, tt, :], vst[:, 8 + 2 * tt:9 + 2 * tt], small[:, 12 + tt:13 + tt],
                         ALU.subtract, ALU.mult))
                step(tten(gv[:, tt, :], gv[:, tt, :], lng, ALU.mult))
                ins = tten(gv[:, tt, :], gv[:, tt, :], lnb, ALU.add)
                step(ins, S["vln_ready"]) if tt == 1 else step(ins)
            v.wait_ge(S["mask_ready"], 2)
            for h in range(HEADS):
                for tt in range(TT):
                    ns = (tt + 1) * P
                    k = 2 * h + tt
                    b = B.take(v)
                    if k >= 2:
                        v.wait_ge(S["p_ready"], k - 1)
                    step(stt(sc[:, tt, 0:ns], b[:, 0:ns], SCALE, maskb[:, tt, 0:ns], ALU.mult, ALU.add), B.free)
                    step(v.tensor_reduce(rt[:, tt:tt + 1], sc[:, tt, 0:ns], AX.X, ALU.max, negate=True), S["sc_ready"])
                for tt in range(TT):
                    ns = (tt + 1) * P
                    v.wait_ge(S["p_ready"], 2 * h + tt + 1)
                    step(v.reciprocal(rt[:, 4 + tt:5 + tt], rt[:, 2 + tt:3 + tt]))
                    pn = prob[h % 2][tt][:, 0:ns]
                    step(tsc(pn, pn, rt[:, 4 + tt:5 + tt], None, ALU.mult), S["prob_ready"])
            for g in range(GROUPS):
                b = B.take(v)
                step(tten(gmT[:, g, :], b[:, 0:T], guT[:, g, :], ALU.mult), B.free)
            v.wait_ge(A.free, A.upto("g15"))
            for m in range(KB):
                b = B.take(v)
                step(stt(mtmp[:, 0, :], tga[:, m, :], 1.0, b[:, 0:T], ALU.add, ALU.mult), B.free)
                b = B.take(v)
                step(stt(mtmp[:, 1, :], tgb[:, m, :], 1.0, b[:, 0:T], ALU.add, ALU.mult), B.free)
                step(tten(mgT[:, m, :], mtmp[:, 0, :], mtmp[:, 1, :], ALU.add), S["mg_ready"])
            for j in range(4):
                for tt in range(TT):
                    b = B.take(v)
                    xs = x[:, tt, j * CW:(j + 1) * CW]
                    step(stt(xs, b[:, 0:CW], 0.5, xs, ALU.mult, ALU.add), B.free)
            norm_x(None)
            for tt in range(TT):
                ins = tsc(xn[:, tt, :], x[:, tt, :], small[:, 2 + tt:3 + tt], None, ALU.mult)
                step(ins, S["xn_ready"]) if tt == 1 else step(ins)
            take_hT(colA[:, 8:16])
            b = B.take(v)
            NR = EG + EXPERTS
            step(v.tensor_copy(logit[:, :, :], b[:, 0:TT * NR].rearrange("p (t n) -> p t n", t=TT)), B.free)
            v.wait_ge(S["const_ready"], 1)

            def first_max(onehot, vals, n, t1):
                step(v.tensor_reduce(t1, vals, AX.X, ALU.max))
                step(stt(onehot, vals, t1, desc[:, 0:n], ALU.is_equal, ALU.mult))
                step(v.tensor_reduce(t1, onehot, AX.X, ALU.max))
                step(tsc(onehot, desc[:, 0:n], t1, None, ALU.is_equal))

            for tt in range(TT):
                lg = logit[:, tt, 0:EG]
                step(v.tensor_reduce(rt[:, 6:7], lg, AX.X, ALU.max))
                step(tsc(rt[:, 8:12], lg, rt[:, 6:7], None, ALU.subtract), S["exp_wanted"])
                v.wait_ge(S["exp_ready"], 2 * tt + 1)
                step(v.reciprocal(rt[:, 32:33], rt[:, 7:8]))
                first_max(rt[:, 36:40], rt[:, 12:16], EG, rt[:, 33:34])
                for g in range(EG):
                    le = logit[:, tt, EG + g * EPG:EG + (g + 1) * EPG]
                    if g == 0:
                        step(tsc(rt[:, 16:24], le, rt[:, 36:37], None, ALU.mult))
                    else:
                        step(stt(rt[:, 16:24], le, rt[:, 36 + g:37 + g], rt[:, 16:24], ALU.mult, ALU.add))
                step(v.tensor_reduce(rt[:, 6:7], rt[:, 16:24], AX.X, ALU.max))
                step(tsc(rt[:, 16:24], rt[:, 16:24], rt[:, 6:7], None, ALU.subtract), S["exp_wanted"])
                v.wait_ge(S["exp_ready"], 2 * tt + 2)
                first_max(rt[:, 40:48], rt[:, 24:32], EPG, rt[:, 33:34])
                step(stt(rt[:, 24:32], rt[:, 40:48], -2.0, rt[:, 24:32], ALU.mult, ALU.add))
                step(v.tensor_reduce(rt[:, 34:35], rt[:, 24:32], AX.X, ALU.max))
                first_max(rt[:, 48:56], rt[:, 24:32], EPG, rt[:, 33:34])
                step(tsc(rt[:, 35:36], rt[:, 34:35], 1.0, None, ALU.add))
                step(v.reciprocal(rt[:, 35:36], rt[:, 35:36]))
                step(stt(rt[:, 35:36], rt[:, 35:36], 0.5, rt[:, 32:33], ALU.mult, ALU.mult))
                step(stt(rt[:, 48:56], rt[:, 48:56], rt[:, 34:35], rt[:, 40:48], ALU.mult, ALU.add))
                step(tsc(rt[:, 48:56], rt[:, 48:56], rt[:, 35:36], None, ALU.mult))
                for g in range(EG):
                    step(tsc(comb[:, tt, g * EPG:(g + 1) * EPG], rt[:, 48:56], rt[:, 36 + g:37 + g], None, ALU.mult))

            def gu(e, par):
                v.wait_ge(S["tanh_gate"], e + 1)
                v.scalar_tensor_tensor(sg[:, :], thg[:, par, :], 1.0, psum[par][:, :], ALU.add, ALU.mult) \
                    .then_inc(S["silu_ready"], 1)
                v.wait_ge(S["silu_ready"], e + 1)
                v.tensor_tensor(heT[:, par, :, :], psum[2 + par][:, :].rearrange("p (b t) -> p b t", b=2),
                                sg[:, :].rearrange("p (b t) -> p b t", b=2), ALU.mult).then_inc(S["he_ready"], 1)
                v.wait_ge(S["he_ready"], e + 1)

            def down_add(e):
                for tt in range(TT):
                    for hf in range(2):
                        k = 2 * tt + hf
                        v.wait_ge(S["down_done"], e * 4 + (k + 1))
                        if k == 0 and not (isinstance(e, int) and e == 0):
                            v.wait_ge(S["down_out"], e * 4)
                        xs = x[:, tt, hf * 512:(hf + 1) * 512]
                        v.scalar_tensor_tensor(xs, psum[4 + k][:, :], comb[:, tt, bass.ds(e, 1)] if not isinstance(e, int)
                                               else comb[:, tt, e:e + 1], xs, ALU.mult, ALU.add) \
                            .then_inc(S["down_out"], 1)
            gu(0, 0)
            for e in range(2):
                gu(e + 1, (e + 1) % 2)
                down_add(e)
            with v.Fori(1, (EXPERTS - 2) // 2) as i:
                for j in range(2):
                    gu(i * 2 + (j + 1), (j + 1) % 2)
                    down_add(i * 2 + j)
            gu(EXPERTS - 1, 1)
            down_add(EXPERTS - 2)
            down_add(EXPERTS - 1)
            v.wait_ge(S["down_out"], 4 * EXPERTS)
            norm_x(None)
            v.wait_ge(S["gfin_loaded"], 16)
            for tt in range(TT):
                ins = stt(x[:, tt, :], x[:, tt, :], small[:, 2 + tt:3 + tt], gfin[:, :], ALU.mult, ALU.mult)
                if tt == 1:
                    step(ins, S["rstd_used"])
                else:
                    step(ins)
            step(tsc(lneg, colL[:, :, V_LAM:V_LAM + KB], -1.0, None, ALU.mult))
            step(tten(labs, lneg, colL[:, :, V_LAM:V_LAM + KB], ALU.max), S["sp_wanted"])
            v.wait_ge(S["sp_ready"], 1)
            log1p(lsp, labs, ly, lt)
            step(stt(lsp, lneg, 0.0, lsp, ALU.max, ALU.add))
            step(tsc(hb[:, :, :], colL[:, :, V_BA:V_BA + 2 * KB], 0.5, None, ALU.mult), S["hb_ready"])

            for l in range(LAYERS):
                step(v.tensor_copy(cBC[:, :, :], csil[:, :].unsqueeze(2).broadcast_to([P, KB, P])), S["cbc_ready"])
                norm_x(None)
                for tt in range(TT):
                    ins = tsc(xn[:, tt, :], x[:, tt, :], small[:, 2 + tt:3 + tt], None, ALU.mult)
                    step(ins, S["xn_ready"]) if tt == 1 else step(ins)
                v.wait_ge(A.free, A.upto(f"mod{l}"))
                step(tten(modc[:, :], modc[:, :], colL[:, l, V_ADA:V_ADA + 16], ALU.add))
                step(stt(gs[:, :], modc[:, 8:16], 1.0, colL[:, l, V_NORM:V_NORM + KB], ALU.add, ALU.mult))
                step(tsc(n4[:, 0, :], lsp[:, l, :], 4.0, None, ALU.mult))
                step(tsc(n4[:, 1, :], lsp[:, l, :], -4.0, None, ALU.mult), S["mod_ready"])
                take_hT(gs, modc)

                def conv(dst, src, wcol, bcol, m, signal):
                    step(tsc(dst[:, m, :], src[:, m, 0:T], wcol(0, m), bcol(m), ALU.mult, ALU.add))
                    for j in range(1, TAPS):
                        ins = stt(dst[:, m, :], src[:, m, j:j + T], wcol(j, m), dst[:, m, :], ALU.mult, ALU.add)
                        step(ins, signal) if j == TAPS - 1 else step(ins)
                if l == 0:
                    v.wait_ge(S["pads_ready"], 1)
                for m in range(KB):
                    v.wait_ge(A.free, A.upto(f"rx{l}{m}"))
                    conv(rxc, rxv, lambda j, m: colL[:, l, V_RCW + j * KB + m:V_RCW + j * KB + m + 1],
                         lambda m: colL[:, l, V_RCB + m:V_RCB + m + 1], m, S["conv_ready"])
                v.wait_ge(S["rg_gate"], KB * (l + 1))
                step(tten(thr[:, :, :], aa[:, :, :], aa[:, :, :], ALU.mult))
                step(stt(tl[:, :, :], thr[:, :, :], 1.0, tl[:, :, :], ALU.add, ALU.mult), S["rg_root_wanted"])
                step(stt(thi[:, :, :], thi[:, :, :], 1.0, rxc[:, :, :], ALU.add, ALU.mult))
                v.wait_ge(A.free, A.upto(f"rz{l}7"))
                step(stt(zr[:, :, :], mth[:, :, :], 1.0, zr[:, :, :], ALU.add, ALU.mult), S["z_used"])
                for m in range(KB):
                    v.wait_ge(A.free, A.upto(f"mx{l}{m}"))
                    conv(mc, mxv, lambda j, m: colL[:, l, V_MCW + j * KB + m:V_MCW + j * KB + m + 1],
                         lambda m: colM[:, l, m:m + 1], m, S["mconv_ready"])
                for m in range(KB):
                    v.wait_ge(S["mtanh_ready"], l * KB + m + 1)
                    step(stt(mc[:, m, :], mth[:, m, :], 1.0, mc[:, m, :], ALU.add, ALU.mult), S["mc_ready"])
                v.wait_ge(S["rg_root"], l + 1)
                step(stt(thi[:, :, :], tl[:, :, :], 0.5, thi[:, :, :], ALU.mult, ALU.mult))
                for h in range(KB):
                    step(v.tensor_tensor_scan(thr[:, h, :], aa[:, h, :], thi[:, h, :], 0.0, ALU.mult, ALU.add))
                step(stt(thr[:, :, :], thr[:, :, :], 0.5, zr[:, :, :], ALU.mult, ALU.mult), S["rg_done"])
                v.wait_ge(S["gate_b_loaded"], 16 * 3 * LAYERS)
                b = B.take(v)
                step(tsc(rows[:, 0, :], b[0:MLH, 0:T], bif[:, l, 0:1], None, ALU.add))
                step(tsc(rows[:, 1, :], b[0:MLH, T:2 * T], bif[:, l, 1:2], None, ALU.add), B.free)
                step(tsc(rows[:, 2, :], rows[:, 1, :], -1.0, None, ALU.mult))
                step(tten(rows[:, 2, :], rows[:, 2, :], rows[:, 1, :], ALU.max), S["lf_wanted"])
                v.wait_ge(S["lf_ready"], l + 1)
                log1p(rows[:, 4, :], rows[:, 2, :], rows[:, 5, :], rows[:, 6, :])
                step(stt(rows[:, 1, :], rows[:, 1, :], 0.0, rows[:, 4, :], ALU.min, ALU.subtract))
                for c in range(TT):
                    cs = slice(c * P, (c + 1) * P)
                    step(v.tensor_tensor_scan(rows[:, 7, cs], onesr[:, :], rows[:, 1, cs], 0.0, ALU.mult, ALU.add))
                step(tten(rows[:, 3, :], rows[:, 0, :], rows[:, 7, :], ALU.subtract))
                for c in range(TT):
                    cs = slice(c * P, (c + 1) * P)
                    step(v.tensor_tensor_scan(rows[:, 4, cs], rows[:, 3, cs], rows[:, 3, cs],
                                              0.0 if c == 0 else rsc[:, 1:2], ALU.max, ALU.max))
                    if c == 0:
                        step(tten(rsc[:, 1:2], rows[:, 4, P - 1:P], rows[:, 7, P - 1:P], ALU.add))
                        step(tsc(rsc[:, 0:1], rows[:, 4, P - 1:P], -1.0, None, ALU.mult))
                step(tsc(rows[:, 5, :], rows[:, 4, :], -1.0, None, ALU.mult))
                step(tten(rows[:, 2, :], rows[:, 4, :], rows[:, 7, :], ALU.add), S["row_wanted"])
                v.wait_ge(A.free, A.upto(f"mo{l}31"))
                step(tsc(oth_t[:, :], oth_t[:, :], 1.0, None, ALU.add), S["oth_ready"])
                v.wait_ge(A.free, A.upto(f"mz{l}7"))
                step(stt(zm[:, :, :], mth[:, :, :], 1.0, zm[:, :, :], ALU.add, ALU.mult), S["z_used"])
                b = B.take(v)
                step(v.tensor_copy(cols[:, :, :], b[:, 0:16].rearrange("p (n h) -> p n h", n=4)), B.free)
                for h in range(MLH):
                    step(tsc(knat[:, h, :], knat[:, h, :], cols[:, 0, h:h + 1], None, ALU.mult), S["kw_ready"])
                for c in range(TT):
                    for h in range(MLH):
                        b = B.take(v)
                        v.wait_ge(A.free, A.upto(f"E{l}{c}{h}"))
                        step(stt(stb[:, h % 2, :], b[:, 0:P], MLD ** -0.5, ebuf[:, h % 2, :], ALU.mult, ALU.mult),
                             B.free)
                        b = B.take(v)
                        if c == 0:
                            step(v.tensor_copy(hn[:, :], b[:, 0:VW]), B.free)
                        else:
                            v.wait_ge(A.free, A.upto(f"in{l}{h}"))
                            step(tten(hn[:, :], b[:, 0:VW], inter[:, h % 2, :], ALU.add), B.free)
                        step(tsc(rt[:, 0:1], hn[:, MLD:VW], -1.0, None, ALU.mult))
                        step(tten(rt[:, 0:1], rt[:, 0:1], hn[:, MLD:VW], ALU.max))
                        step(tten(rt[:, 0:1], rt[:, 0:1], cols[:, 2 + c, h:h + 1], ALU.max))
                        step(v.reciprocal(rt[:, 1:2], rt[:, 0:1]))
                        step(stt(hh[:, c, h * MLD:(h + 1) * MLD], hn[:, 0:MLD], rt[:, 1:2],
                                 oth[:, c, h * MLD:(h + 1) * MLD], ALU.mult, ALU.mult), S["hh_ready"])
                roots_n["ssq"] += 8
                v.wait_ge(S["ssq_ready"], roots_n["ssq"])
                rstd(small[:, 24:32], small[:, 16:24], 0.25 / MLD)
                step(tsc(small[:, 24:32], small[:, 24:32], 0.25, None, ALU.mult))
                for c in range(TT):
                    for h in range(MLH):
                        hv = hh[:, c, h * MLD:(h + 1) * MLD]
                        n = 24 + c * MLH + h
                        ins = tsc(hv, hv, small[:, n:n + 1], None, ALU.mult)
                        step(ins, S["hq_ready"]) if (c, h) == (1, MLH - 1) else step(ins)
                for m in range(KB):
                    b = B.take(v)
                    step(stt(ymT[:, m, :], b[:, 0:T], colM[:, l, 8 + m:9 + m], zm[:, m, :], ALU.mult, ALU.mult), B.free)
                for j in range(4):
                    for tt in range(TT):
                        b = B.take(v)
                        step(tten(hn[:, 0:CW], b[:, 0:CW], gateB[:, j * CW:(j + 1) * CW], ALU.mult), B.free)
                        xs = x[:, tt, j * CW:(j + 1) * CW]
                        ins = tten(xs, xs, hn[:, 0:CW], ALU.add)
                        step(ins, S["layer_done"]) if (j, tt) == (3, 1) else step(ins)
            norm_x(None)
            v.wait_ge(S["gfin_loaded"], 32)
            for tt in range(TT):
                step(stt(xn[:, tt, :], x[:, tt, :], small[:, 2 + tt:3 + tt], gfin[:, :], ALU.mult, ALU.mult),
                     S["layer_done"])

        @block.gpsimd
        def _(g):
            step = Chain(g, s_pool)
            step(g.memset(ident[:, :], 0.0))
            step(g.affine_select(out=ident[:, :], in_=ident[:, :], compare_op=ALU.not_equal, fill=1.0, base=0,
                                 pattern=[[-1, P]], channel_multiplier=1))
            step(g.memset(anti[:, :], 0.0))
            step(g.affine_select(out=anti[:, :], in_=anti[:, :], compare_op=ALU.not_equal, fill=1.0 / SCALE,
                                 base=1 - P, pattern=[[1, P]], channel_multiplier=1))
            step(g.memset(later[:, :], 0.0))
            step(g.affine_select(out=later[:, :], in_=later[:, :], compare_op=ALU.is_ge, fill=-BIG, base=0,
                                 pattern=[[1, P]], channel_multiplier=-1))
            step(g.memset(ones[:, :], 1.0))
            step(g.memset(onesr[:, :], 1.0))
            step(g.memset(sel4[:, :, :], 0.0))
            step(g.affine_select(out=sel4[:, :, :], in_=sel4[:, :, :], compare_op=ALU.not_equal, fill=1.0, base=0,
                                 pattern=[[-1, MLH], [0, P]], channel_multiplier=1))
            for k in range(EPG):
                step(g.memset(desc[:, k:k + 1], float(EPG - k)), S["const_ready"] if k == EPG - 1 else None)
            def vec(dst, name, src, s):
                g.dma_start(dst, src).then_inc(s, 16)
            s = S["rows_loaded"]
            r8 = lambda ap: ap.rearrange("(k p) -> k p", p=P)
            vec(rowsA[0:8, :], "g1", r8(a["norm1_g"][0]), s)
            vec(rowsA[8:16, :], "g2", r8(a["norm2_g"][0]), s)
            vec(rowsA[16:17, :], "gkv", a["kv_norm_g"], s)
            vec(rowsA[17:25, :], "c", r8(a["c_2"][0]), s)
            vec(rowsA[25:26, :], "pad", a["kv_norm_g"], s)
            g.dma_start(relw, a["rel_bias"]).then_inc(S["rel_loaded"], 16)
            g.dma_start(reltab, a["bucket_of_distance"]).then_inc(S["rel_loaded"], 16)
            s = S["rowsL_loaded"]
            for l in range(LAYERS):
                for row, src in ((V_NORM, r8(a["norm_g_2"][l])), (V_ADA, r8(a["b_ada_2"][l])),
                                 (V_RCW, a["rg_conv_w_2"][l].rearrange("j (k p) -> (j k) p", p=P)),
                                 (V_MCW, a["ml_conv_w_2"][l].rearrange("j (k p) -> (j k) p", p=P)),
                                 (V_RCB, r8(a["rg_conv_b_2"][l])), (V_BA, r8(a["rg_b_a_2"][l])),
                                 (V_BX, r8(a["rg_b_x_2"][l])), (V_LAM, r8(a["rg_lambda_2"][l]))):
                    vec(rowsL[row:row + src.shape[0], l, :], "", src, s)
                vec(rowsM[0:8, l, :], "", r8(a["ml_conv_b_2"][l]), s)
                vec(rowsM[8:16, l, :], "", r8(a["ml_norm_g_2"][l]), s)
            s = S["small_loaded"]
            NR = EG + EXPERTS
            g.dma_start(wi_w[:, :, :], cols_of(w_in, C_WI, 8)).then_inc(s, 16)
            g.dma_start(rt_w[:, :, 0:EG], cols_of(a["router_group_w"][0], 0, EG)).then_inc(s, 16)
            g.dma_start(rt_w[:, :, EG:NR], cols_of(a["router_expert_w"][0], 0, EXPERTS)).then_inc(s, 16)
            g.dma_start(rt_b[0:1, 0:EG], a["router_group_b"]).then_inc(s, 16)
            g.dma_start(rt_b[0:1, EG:NR], a["router_expert_b"]).then_inc(s, 16)
            g.dma_start(wuk, a["w_uk"][0].rearrange("r h d -> r (h d)")).then_inc(S["attn_loaded"], 16)
            g.dma_start(wuv, a["w_uv"][0].rearrange("r h d -> r (h d)")).then_inc(S["attn_loaded"], 16)
            g.dma_start(wsn, a["w_spatial"][0].rearrange("g i j -> i g j")).then_inc(S["relrow_ready"], 16)
            g.dma_start(lng, bcast(a["ln_v_g"][0], 512)) \
                .then_inc(S["ln_loaded"], 16)
            g.dma_start(lnb, bcast(a["ln_v_b"][0], 512)).then_inc(S["ln_loaded"], 16)
            g.dma_start(bsp[0:1, :], a["b_spatial"].rearrange("a g i -> a (g i)")).then_inc(S["ln_loaded"], 16)
            g.wait_ge(B.free, B.upto("relrow"))
            g.dma_start(relscr_ap, relrow).then_inc(S["relrow_stored"], 16)
            g.wait_ge(S["relrow_stored"], 16)
            g.dma_start(biasT, diag).then_inc(S["bias_loaded"], 16)
            g.wait_ge(S["relrow_ready"], 16)
            step(g.affine_select(out=wsn, in_=wsn, compare_op=ALU.is_ge, fill=0.0, base=0,
                                 pattern=[[0, GROUPS], [-1, P]], channel_multiplier=1), S["ws_masked"])
            for tt in range(TT):
                ns = (tt + 1) * P
                g.wait_ge(S["relu_used"], (tt + 1) * HEADS)
                step(g.affine_select(out=idx[:, tt, 0:ns], in_=idx[:, tt, 0:ns], compare_op=ALU.is_ge, fill=MASKED,
                                     base=tt * P, pattern=[[-1, ns]], channel_multiplier=1), S["idx_masked"])
            for tt in range(TT):
                ns = (tt + 1) * P
                g.wait_ge(S["sel_ready"], tt + 1)
                step(g.affine_select(out=maskb[:, tt, 0:ns], in_=maskb[:, tt, 0:ns], compare_op=ALU.is_ge, fill=-BIG,
                                     base=tt * P, pattern=[[-1, ns]], channel_multiplier=1), S["mask_ready"])
            for l in range(LAYERS):
                g.dma_start(wif[:, l, :, :], a["ml_w_if_2"][l].rearrange("(k p) g -> p k g", p=P)) \
                    .then_inc(S["gate_b_loaded"], 16)
                for k in range(2):
                    g.dma_start(bif[:, l, k:k + 1], a["ml_b_if_2"][l, k * MLH:(k + 1) * MLH].rearrange("(h o) -> h o", o=1)) \
                        .then_inc(S["gate_b_loaded"], 16)
            g.wait_ge(S["vln_ready"], 1)
            g.dma_start(gfin[:, :], bcast(a["final_norm_g"], D)).then_inc(S["gfin_loaded"], 16)
            g.wait_ge(S["rstd_used"], 1)
            step(g.memset(rxp[:, :], 0.0))
            step(g.memset(mxp[:, :], 0.0))
            step(g.memset(vaug_t[:, :], 1.0), S["pads_ready"])
            for l in range(LAYERS):
                if l:
                    g.wait_ge(S["layer_done"], l)
                g.dma_start(adab[0:1, :], a["b_ada_2"][l:l + 1, 2 * D:3 * D]).then_inc(S["adab_loaded"], 16)
            g.wait_ge(S["layer_done"], LAYERS)
            g.dma_start(gfin[:, :], bcast(a["final_g_2"], D)).then_inc(S["gfin_loaded"], 16)


def bucket_of_distance():
    n = np.maximum(T - 1 - np.arange(512), 0)
    exact = BUCKETS // 2
    nf = np.maximum(n, 1).astype(np.float32)
    large = exact + (np.log(nf / np.float32(exact)) / np.float32(np.log(128 / exact))
                     * np.float32(BUCKETS - exact)).astype(np.int32)
    bucket = np.where(n < exact, n, np.minimum(large, BUCKETS - 1))
    return (np.arange(BUCKETS)[:, None] == bucket[None, :]).astype(np.float32)


def kernel(**inputs):
    import concourse.bacc as bacc
    from concourse.bass_utils import run_bass_kernel_spmd

    nc = bacc.Bacc("TRN2", target_bir_lowering=False, num_devices=1)
    arrays, args = {}, {}
    for name, value in list(inputs.items()) + [("bucket_of_distance", bucket_of_distance())]:
        value = np.ascontiguousarray(value)
        arrays[f"in_{name}"] = value
        args[name] = nc.dram_tensor(f"in_{name}", value.shape, mybir.dt.from_np(value.dtype), kind="ExternalInput").ap()
    out = nc.dram_tensor("out", (1, T, D), F32, kind="ExternalOutput").ap()
    build(nc, args, out)
    result = run_bass_kernel_spmd(nc, [arrays], core_ids=[0])
    return result.results[0]["out"]
```

```python
from contextlib import ExitStack

import numpy as np
import concourse.bass as bass
from concourse import mybir

F32 = mybir.dt.float32
ALU = mybir.AluOpType
ACT = mybir.ActivationFunctionType
AX = mybir.AxisListType

P = 128
T = 256
TT = T // P
D = 1024
KB = D // P
HEADS, HD = 8, 64
RANK = 128
TOPK = min(256, T // 4)
BUCKETS = 32
GROUPS, GDIM = 4, 128
EG, EPG = 4, 8
EXPERTS = EG * EPG
FF = 256
EPS = 1e-6
LAYERS = 2
MLH, MLD = 4, 256
TAPS = 4
PAD = TAPS - 1
XW = T + 4
VW = MLD + 1
CW = 256
RING = 6
SLOTS = 64
PAIRS = EXPERTS // 2
BIG = 1e30
MASKED, TAKEN = -1e38, -3e38
SCALE = HD ** -0.5
IDX_SCALE = (8 ** -0.5) * (64 ** -0.5)
C_Q, C_CKV, C_QI, C_KI, C_WI, C_U, C_V, C_GA, C_GB = 0, 512, 640, 1152, 1216, 1224, 1736, 2248, 3272
V_NORM, V_ADA, V_RCW, V_MCW, V_RCB, V_BA, V_BX, V_LAM = 0, 8, 32, 64, 96, 104, 112, 120
LOG1P = [1.0 / k for k in (17, 15, 13, 11, 9, 7, 5, 3)]


class Banks:

    def __init__(self, banks, done, free):
        self.banks, self.done, self.free = banks, done, free
        self.put, self.got, self.names = 0, 0, {}

    def acquire(self, pe, name=None):
        n = self.put
        self.put += 1
        self.names[name] = n + 1
        if n >= len(self.banks):
            pe.wait_ge(self.free, n + 1 - len(self.banks))
        return self.banks[n % len(self.banks)]

    def take(self, eng):
        n = self.got
        self.got += 1
        eng.wait_ge(self.done, n + 1)
        return self.banks[n % len(self.banks)]

    def upto(self, name):
        return self.names[name]


class Chain:

    def __init__(self, eng, sem):
        self.eng, self.sem, self.count = eng, sem, {}

    def __call__(self, ins, sem=None):
        sem = sem or self.sem
        n = self.count.get(sem.name, 0) + 1
        self.count[sem.name] = n
        ins.then_inc(sem, 1)
        self.eng.wait_ge(sem, n)


def build(nc, a, out):
    with ExitStack() as ctx:
        def sb(name, shape):
            return ctx.enter_context(nc.sbuf_tensor(name, shape, F32))

        def sem(name):
            return ctx.enter_context(nc.semaphore(name))

        psum = [ctx.enter_context(nc.psum_tensor(f"bank{i}", [P, 512], F32)) for i in range(8)]

        ring = [sb(f"ring{i}", [P, KB * CW]) for i in range(RING)]
        x = sb("x", [P, TT, D])
        hT = sb("hT", [P, KB, T])
        tmp = sb("tmp", [P, 2048])
        rxp = sb("rxp", [P, KB * XW])
        mxp = sb("mxp", [P, KB * XW])
        s0, s1, s2, s3, s4 = (sb(f"s{i}", [P, MLH * 2 * VW]) for i in range(5))
        z0, z1, s5, s6, s7 = (sb(n, [P, 2048]) for n in ("z0", "z1", "s5", "s6", "s7"))
        vaug_t = sb("vaug", [P, TT * MLH * VW])
        w4 = sb("w4", [P, 1024])
        gateB = sb("gateB", [P, D])
        oth_t = sb("oth", [P, 2048])
        ident = sb("ident", [P, P])
        anti = sb("anti", [P, P])
        later = sb("later", [P, P])
        ones = sb("ones", [1, P])
        onesr = sb("onesr", [MLH, P])
        sel4 = sb("sel4", [MLH, MLH, P])
        rowsA = sb("rowsA", [32, P])
        colA = sb("colA", [P, 32])
        rowsL = sb("rowsL", [P, LAYERS, P])
        rowsM = sb("rowsM", [16, LAYERS, P])
        colL = sb("colL", [P, LAYERS, P])
        colM = sb("colM", [P, LAYERS, 16])
        small = sb("small", [P, 64])
        rt_b = sb("rt_b", [1, EG + EXPERTS])
        wif = sb("wif", [P, LAYERS, 24, 8])
        bif = sb("bif", [MLH, LAYERS, 2])
        csil = sb("csil", [P, KB])
        modc = sb("modc", [P, 16])
        gs = sb("gs", [P, KB])
        n4 = sb("n4", [P, 2, KB])
        lam = sb("lam", [P, 5, LAYERS, KB])
        hb = sb("hb", [P, LAYERS, 2 * KB])
        gnat = sb("gnat", [P, TT, 8])
        rsc = sb("rsc", [MLH, 4])
        cols = sb("cols", [P, 4, MLH])
        logit = sb("logit", [P, TT, EG + EXPERTS])
        comb = sb("comb", [P, TT, EXPERTS])
        rt = sb("rt", [P, 128])
        desc = sb("desc", [P, EPG])
        m8 = sb("m8", [P, 8])
        most = ctx.enter_context(nc.sbuf_tensor("most", [P, 1], mybir.dt.int32))

        lneg, labs, lsp, ly, lt = (lam[:, i, :, :] for i in range(5))
        squares = s7[:, :].rearrange("p (t d) -> p t d", t=TT)

        xn = tmp[:, :].rearrange("p (t d) -> p t d", t=TT)
        qT = s0[:, 0:1024].rearrange("p (b t) -> p b t", b=4)
        qiT = s0[:, 1024:2048].rearrange("p (b t) -> p b t", b=4)
        kvT = s1[:, 0:1024].rearrange("p (b t) -> p b t", b=4)
        vnat = s1[:, 1024:2048].rearrange("p (s c) -> p s c", s=TT)
        biasT = s2[:, 0:2048].rearrange("p (h j) -> p h j", h=HEADS)
        idx = s3[:, 0:512].rearrange("p (t s) -> p t s", t=TT)
        maskb = s3[:, 512:1024].rearrange("p (t s) -> p t s", t=TT)
        relu = s3[:, 1024:1536].rearrange("p (b s) -> p b s", b=2)
        sc = s3[:, 1536:2048].rearrange("p (t s) -> p t s", t=TT)
        prob = [[tmp[:, 384 * i:384 * i + P], tmp[:, 384 * i + P:384 * i + 3 * P]] for i in range(2)]
        pT = s4[:, 0:768].rearrange("p (b s q) -> p b s q", b=2, s=3)
        kiT = s4[:, 768:1024]
        cT = s4[:, 1024:1280]
        ckv = s4[:, 1280:1536].rearrange("p (t r) -> p t r", t=TT)
        wi = s4[:, 1536:1552].rearrange("p (t h) -> p t h", t=TT)
        vst = s4[:, 1552:1568]
        bkt = s4[0:BUCKETS, 1568:2056]
        tga = z0[:, :].rearrange("p (b t) -> p b t", b=KB)
        tgb = z1[:, :].rearrange("p (b t) -> p b t", b=KB)
        guT = s5[:, 0:1024].rearrange("p (b t) -> p b t", b=GROUPS)
        gv = s5[:, 1024:2048].rearrange("p (t c) -> p t c", t=TT)
        gmT = s6[:, 0:1024].rearrange("p (b t) -> p b t", b=GROUPS)
        oaT = s6[:, 1024:2048].rearrange("p (b t) -> p b t", b=4)
        mgT = s7[:, :].rearrange("p (b t) -> p b t", b=KB)
        mtmp = vaug_t[:, 0:512].rearrange("p (b t) -> p b t", b=2)
        reltab = vaug_t[0:BUCKETS, 512:1024]
        relw = vaug_t[0:BUCKETS, 1024:1032]
        relrow = vaug_t[0:HEADS, 1032:1544]
        wuk = w4[:, 0:512]
        wuv = w4[:, 512:1024]
        lng = gateB[:, 0:512]
        lnb = gateB[:, 512:1024]
        wsn = oth_t[:, 0:512].rearrange("p (g j) -> p g j", g=GROUPS)
        wsT = oth_t[:, 512:1024].rearrange("p (g j) -> p g j", g=GROUPS)
        bsp = rxp[0:1, 0:512]
        wi_w = mxp[:, 0:64].rearrange("p (k n) -> p k n", k=KB)
        rt_w = mxp[:, 64:64 + KB * (EG + EXPERTS)].rearrange("p (k n) -> p k n", k=KB)
        heT = s5[:, 0:1024].rearrange("p (e b t) -> p e b t", e=2, b=2)
        thg = s5[:, 1024:2048].rearrange("p (e n) -> p e n", e=2)
        sg = s6[:, 0:512]
        xg = xn
        hgT = z0[:, 0:KB * P].rearrange("p (b s) -> p b s", b=KB)
        he = s5[:, 0:FF]
        heTs = s5[:, FF:2 * FF].rearrange("p (b s) -> p b s", b=2)
        thgs = s5[:, 2 * FF:3 * FF]
        ye = z1[:, 0:D]
        combT = s7[:, 0:512].rearrange("p (q t) -> p q t", q=2)
        pick = mxp[:, 512:1024].rearrange("p (q t s) -> p q t s", q=2, t=TT)
        pickw = mxp[:, 1024:1536].rearrange("p (q t s) -> p q t s", q=2, t=TT)
        slotno = mxp[:, 1536:1536 + SLOTS]
        upto = rxp[:, 512:512 + P]
        allone = rxp[:, 640:640 + P]
        key = rxp[:, 768:768 + TT * EXPERTS].rearrange("p (t e) -> p t e", t=TT)
        member = rxp[:, 832:832 + TT * EXPERTS].rearrange("p (t e) -> p t e", t=TT)
        norm2 = oth_t[:, 1024:2048]
        gfin = gateB
        rxv = rxp[:, :].rearrange("p (b t) -> p b t", b=KB)
        mxv = mxp[:, :].rearrange("p (b t) -> p b t", b=KB)

        def v8(s):
            return s[:, 0:2048].rearrange("p (b t) -> p b t", b=KB)
        rxc, thr, thi, aa, tl = v8(s0), v8(s1), v8(s2), v8(s3), v8(s4)
        zr, zm = v8(z0), v8(z1)
        mc, mqT, mkT = v8(s5), v8(s6), v8(s7)
        mth = v8(tmp)
        mvT = v8(s3)
        rows = s2[0:MLH, 0:8 * T].rearrange("p (r t) -> p r t", r=8)
        adab = z1[0:1, 0:D]
        cBC = v8(z0)[:, :, 0:P]
        ebuf = tmp[:, 256:512].rearrange("p (b t) -> p b t", b=2)
        stb = tmp[:, 512:768].rearrange("p (b t) -> p b t", b=2)
        hn = tmp[:, 768:768 + VW]
        inter = tmp[:, 1032:1032 + 2 * VW].rearrange("p (b c) -> p b c", b=2)
        vaug = vaug_t[:, :].rearrange("p (t h c) -> p t h c", t=TT, h=MLH)
        knat = w4[:, :].rearrange("p (h c) -> p h c", h=MLH)
        caug = s0[:, :].rearrange("p (h k c) -> p h k c", h=MLH, k=2)
        oth = oth_t[:, :].rearrange("p (t c) -> p t c", t=TT)
        hh = s3[:, 0:2048].rearrange("p (t c) -> p t c", t=TT)
        ymT = v8(s4)

        relscr = nc.dram_tensor("rel_scratch", (HEADS, 512), F32)
        relscr_ap = relscr.ap() if hasattr(relscr, "ap") else relscr

        diag = bass.AP(relscr_ap.tensor, 0, [[1, P], [512, HEADS], [1, T]])

        def bcast(ap, n):
            return bass.AP(ap.tensor, ap.offset, [[0, P], [1, n]])

        A = Banks(psum[0:4], sem("a_done"), sem("a_free"))
        B = Banks(psum[4:8], sem("b_done"), sem("b_free"))
        slot_full = [sem(f"slot_full{i}") for i in range(RING)]
        chunk_used = sem("chunk_used")
        s_act, s_dve, s_pool = sem("act_step"), sem("dve_step"), sem("pool_step")
        S = {n: sem(n) for n in (
            "x_loaded", "rows_loaded", "small_loaded", "attn_loaded", "rel_loaded", "const_ready", "rowsL_loaded",
            "ssq_ready", "root_wanted", "root_ready", "xn_ready", "relrow_ready", "relrow_stored", "bias_loaded",
            "relu_used", "idx_ready", "idx_masked", "sel_ready", "mask_ready", "sc_ready", "p_ready",
            "prob_ready", "cT_wanted", "ws_masked", "vln_ready", "mg_ready", "cbc_ready", "csil_ready", "gate_b_loaded",
            "exp_wanted", "exp_ready", "comb_ready", "tanh_gate", "silu_ready", "he_ready", "gu_done",
            "gate_done", "down_done", "down_out", "gfin_loaded", "x_stored", "mod_ready", "conv_ready", "rg_gate", "rg_root_wanted",
            "rg_root", "mconv_ready", "mtanh_ready", "mc_ready", "pads_ready", "lf_wanted", "lf_ready",
            "row_wanted", "row_ready", "kw_ready", "hh_ready", "hq_ready", "y_ready",
            "adab_loaded", "layer_done", "sp_wanted", "sp_ready", "csil_wanted", "csil_tanh", "hT_ready", "ln_loaded",
            "norm2_loaded", "routed", "most_ready", "slots_ready", "gather_done", "gather_ready", "combT_done",
            "combT_ready", "ye_ready", "mixed", "heT_done", "heT_ready", "down_half",
            "z_used", "rg_done", "oth_ready", "ckv_ready", "rstd_used", "hb_ready")}

        def cols_of(w, c, n=CW):
            return w[:, c:c + n].rearrange("(k p) c -> p k c", p=P)

        w_in = a["w_in"][0]
        chunks = []
        def add(*parts):
            chunks.append(parts)
        full = lambda t: t[:, :].rearrange("p (k c) -> p k c", k=KB)
        def colpart(lo, n):
            return lambda t: full(t)[:, :, lo:lo + n]
        add((colpart(0, 128), cols_of(w_in, C_CKV, 128)), (colpart(128, 64), cols_of(w_in, C_KI, 64)),
            (colpart(192, 64), cols_of(w_in, C_KI, 64)))
        for c in (C_Q, C_QI, C_U, C_V):
            for j in range(2):
                add((full, cols_of(w_in, c + j * CW)))
        for c in (C_GA, C_GB):
            for j in range(4):
                add((full, cols_of(w_in, c + j * CW)))
        for j in range(4):
            add((lambda t: full(t)[:, 0:4, :], cols_of(a["w_proj_a"][0], j * CW)),
                (lambda t: full(t)[:, 4:8, :], cols_of(a["w_proj_b"][0], j * CW)))
        for j in range(4):
            add((full, cols_of(a["w_out"][0], j * CW)))
        first_expert_chunk = len(chunks)
        assert first_expert_chunk == 25
        NB1 = first_expert_chunk
        tail = []
        def addt(*parts):
            tail.append(parts)
        for l in range(LAYERS):
            for j in range(12):
                addt((full, cols_of(a["w_ada_2"][l], j * CW)))
            wi2 = a["w_in_2"][l]
            for j in range(4):
                addt((full, cols_of(wi2, j * CW)))
            addt((colpart(0, 128), a["rg_w_a_2"][l].rearrange("h d e -> d h e")),
                 (colpart(128, 128), a["rg_w_x_2"][l].rearrange("h d e -> d h e")))
            for c in (D, 2 * D):
                for j in range(4):
                    addt((full, cols_of(wi2, c + j * CW)))
            for n in ("ml_w_q_2", "ml_w_k_2", "ml_w_v_2"):
                addt((full, a[n][l].rearrange("h (k p) e -> p (h k) e", p=P)))
            for c in (3 * D, 4 * D):
                for j in range(4):
                    addt((full, cols_of(wi2, c + j * CW)))
            for j in range(4):
                for kh in range(2):
                    addt((full, cols_of(a["w_out_2"][l][kh * D:(kh + 1) * D, :], j * CW)))
        E0 = NB1
        L0 = NB1 + 3 * EXPERTS

        block = ctx.enter_context(nc.Block())

        nparts = [len(c) for c in chunks] + [1] * (3 * EXPERTS) + [len(c) for c in tail]
        fill_value, filled = [], [0] * RING
        for n, k in enumerate(nparts):
            filled[n % RING] += 16 * k
            fill_value.append(filled[n % RING])

        chunk_free = []

        @block.tensor
        def _(pe):
            state = {"n": 0, "free": 0}

            def chunk(k=None):
                n = state["n"]
                state["n"] += 1
                pe.wait_ge(slot_full[n % RING], fill_value[n])
                return ring[n % RING]

            def tr(dst, src, k=P):
                return pe.transpose(dst, src, ident[0:k, 0:k])

            def transpose_x(ready, tag):
                pe.wait_ge(S["xn_ready"], ready)
                for kb in range(KB):
                    b = B.acquire(pe, f"hT{tag}{kb}")
                    for tt in range(TT):
                        m = tr(b[:, tt * P:(tt + 1) * P], xn[:, tt, kb * P:(kb + 1) * P])
                    m.then_inc(B.done, 1)

            def projT(w, m, rhs, pool, name=None, nk=KB, k0=0):
                b = pool.acquire(pe, name)
                for kb in range(nk):
                    mm = pe.matmul(b[:, 0:T], w[:, (k0 + kb) * CW + m * P:(k0 + kb) * CW + (m + 1) * P], rhs[:, kb, :],
                                   start=(kb == 0), stop=(kb == nk - 1))
                mm.then_inc(pool.done, 1)
                return mm

            def used(pool=A, mm=None):
                if mm is None:
                    chunk_free.append((pool.done, pool.put))
                else:
                    state["free"] += 1
                    mm.then_inc(chunk_used, 1)
                    chunk_free.append((chunk_used, state["free"]))

            pe.wait_ge(S["const_ready"], 1)
            pe.wait_ge(S["rows_loaded"], 16 * 5)
            b = B.acquire(pe, "colA")
            tr(b[:, 0:25], rowsA[0:25, :], 25).then_inc(B.done, 1)
            pe.wait_ge(S["rel_loaded"], 32)
            b = B.acquire(pe, "relrow")
            pe.matmul(b[0:HEADS, :], relw, reltab, start=True, stop=True).then_inc(B.done, 1)
            pe.wait_ge(S["rowsL_loaded"], 16 * 20)
            for l in range(LAYERS):
                b = B.acquire(pe, f"colL{l}")
                tr(b[:, 0:P], rowsL[:, l, :])
                tr(b[:, P:P + 16], rowsM[:, l, :], 16).then_inc(B.done, 1)

            transpose_x(1, "A")
            pe.wait_ge(B.free, B.upto("hTA7"))

            w = chunk()
            wv = full(w)
            for tt in range(TT):
                b = A.acquire(pe, f"ckv{tt}")
                for kb in range(KB):
                    mm = pe.matmul(b[:, 0:RANK], hT[:, kb, tt * P:(tt + 1) * P], wv[:, kb, 0:RANK],
                                   start=(kb == 0), stop=(kb == KB - 1))
                mm.then_inc(A.done, 1)
            projT(w, 1, hT, A, "kiT")
            used()
            pe.wait_ge(S["small_loaded"], 16 * 5)
            b = A.acquire(pe, "wi")
            for tt in range(TT):
                for kb in range(KB):
                    mm = pe.matmul(b[:, tt * 8:tt * 8 + 8], hT[:, kb, tt * P:(tt + 1) * P], wi_w[:, kb, :],
                                   start=(kb == 0), stop=(kb == KB - 1))
            mm.then_inc(A.done, 1)
            for name in ("q", "qi"):
                for j in range(2):
                    w = chunk()
                    for m in range(2):
                        projT(w, m, hT, A, f"{name}{2 * j + m}")
                    used()
            pe.wait_ge(A.free, A.upto("qi3"))
            for tt in range(TT):
                ns = (tt + 1) * P
                for h in range(HEADS):
                    o = (h % 2) * 64
                    b = A.acquire(pe, f"idx{tt}{h}")
                    pe.matmul(b[:, 0:ns], qiT[o:o + 64, h // 2, tt * P:(tt + 1) * P], kiT[o:o + 64, 0:ns],
                              start=True, stop=True).then_inc(A.done, 1)
            pe.wait_ge(S["ckv_ready"], 1)
            b = B.acquire(pe, "cT")
            for tt in range(TT):
                mm = tr(b[:, tt * P:(tt + 1) * P], ckv[:, tt, :])
            mm.then_inc(B.done, 1)
            pe.wait_ge(B.free, B.upto("cT"))
            pe.wait_ge(S["attn_loaded"], 32)
            for m in range(4):
                b = A.acquire(pe, f"K{m}")
                pe.matmul(b[:, 0:T], wuk[:, m * P:(m + 1) * P], cT, start=True, stop=True).then_inc(A.done, 1)
            for tt in range(TT):
                b = A.acquire(pe, f"V{tt}")
                pe.matmul(b[:, :], cT[:, tt * P:(tt + 1) * P], wuv, start=True, stop=True).then_inc(A.done, 1)
            for j in range(2):
                w = chunk()
                for m in range(2):
                    projT(w, m, hT, A, f"u{2 * j + m}")
                used()
            for j in range(2):
                w = full(chunk())
                for tt in range(TT):
                    b = A.acquire(pe, f"v{j}{tt}")
                    for kb in range(KB):
                        mm = pe.matmul(b[:, 0:CW], hT[:, kb, tt * P:(tt + 1) * P], w[:, kb, :],
                                       start=(kb == 0), stop=(kb == KB - 1))
                    mm.then_inc(A.done, 1)
                used()
            pe.wait_ge(S["ws_masked"], 1)
            b = A.acquire(pe, "wsT")
            for g in range(GROUPS):
                mm = tr(b[:, g * P:(g + 1) * P], wsn[:, g, :])
            mm.then_inc(A.done, 1)

            gate_jobs = [(j, m) for j in range(8) for m in range(2)]
            gst = {}

            def gate_job():
                if not gate_jobs:
                    return
                j, m = gate_jobs.pop(0)
                if m == 0:
                    gst["w"] = chunk()
                projT(gst["w"], m, hT, A, f"g{2 * j + m}")
                if m == 1:
                    used()

            for h in range(HEADS + 1):
                gate_job()
                if h < HEADS:
                    o = (h % 2) * 64
                    for tt in range(TT):
                        ns = (tt + 1) * P
                        b = B.acquire(pe, f"S{h}{tt}")
                        if (h, tt) == (0, 0):
                            pe.wait_ge(S["bias_loaded"], 16)
                        pe.matmul(b[:, 0:ns], anti[:, :], biasT[:, h, T - ns:T], start=True, stop=False)
                        pe.matmul(b[:, 0:ns], qT[o:o + 64, h // 2, tt * P:(tt + 1) * P], kvT[o:o + 64, h // 2, 0:ns],
                                  start=False, stop=True).then_inc(B.done, 1)
                gate_job()
                if h >= 1:
                    g = h - 1
                    o = (g % 2) * 64
                    pe.wait_ge(S["prob_ready"], 2 * g + 2)
                    b = A.acquire(pe, f"pT{g}")
                    pn = prob[g % 2]
                    tr(b[:, 0:P], pn[0][:, 0:P])
                    tr(b[:, P:2 * P], pn[1][:, 0:P])
                    tr(b[:, 2 * P:3 * P], pn[1][:, P:2 * P]).then_inc(A.done, 1)
                    pe.wait_ge(A.free, A.upto(f"pT{g}"))
                    b = A.acquire(pe, f"o{g}")
                    pe.matmul(b[o:o + 64, 0:P], vnat[:, 0, g * HD:(g + 1) * HD], pT[:, g % 2, 0, :],
                              start=True, stop=True)
                    for st in range(2):
                        mm = pe.matmul(b[o:o + 64, P:2 * P], vnat[:, st, g * HD:(g + 1) * HD], pT[:, g % 2, 1 + st, :],
                                       start=(st == 0), stop=(st == 1))
                    mm.then_inc(A.done, 1)
            assert not gate_jobs
            pe.wait_ge(S["vln_ready"], 1)
            pe.wait_ge(S["ln_loaded"], 48)
            pe.wait_ge(A.free, A.upto("wsT"))
            for g in range(GROUPS):
                b = B.acquire(pe, f"gm{g}")
                for c in range(TT):
                    pe.matmul(b[:, c * P:(c + 1) * P], ones[0:1, :], bsp[0:1, g * P:(g + 1) * P], start=True, stop=False)
                    mm = pe.matmul(b[:, c * P:(c + 1) * P], gv[:, c, g * P:(g + 1) * P], wsT[:, g, :],
                                   start=False, stop=True)
                mm.then_inc(B.done, 1)
            pe.wait_ge(B.free, B.upto("gm3"))
            pe.wait_ge(A.free, A.upto("o7"))
            for j in range(4):
                w = chunk()
                for m in range(2):
                    projT(w, m, oaT, B, f"ya{2 * j + m}", 4, 0)
                    projT(w, m, gmT, B, f"yb{2 * j + m}", 4, 4)
                used(B)
            pe.wait_ge(S["mg_ready"], KB)
            for j in range(4):
                w = full(chunk())
                for tt in range(TT):
                    b = B.acquire(pe, f"xo{j}{tt}")
                    for kb in range(KB):
                        mm = pe.matmul(b[:, 0:CW], mgT[:, kb, tt * P:(tt + 1) * P], w[:, kb, :],
                                       start=(kb == 0), stop=(kb == KB - 1))
                    mm.then_inc(B.done, 1)
                used(B)

            transpose_x(2, "B")
            pe.wait_ge(B.free, B.upto("hTB7"))
            b = B.acquire(pe, "router")
            NR = EG + EXPERTS
            for tt in range(TT):
                for kb in range(KB):
                    pe.matmul(b[:, tt * NR:(tt + 1) * NR], hT[:, kb, tt * P:(tt + 1) * P], rt_w[:, kb, :],
                              start=(kb == 0), stop=False)
                mm = pe.matmul(b[:, tt * NR:(tt + 1) * NR], ones[0:1, :], rt_b[0:1, :], start=False, stop=True)
            mm.then_inc(B.done, 1)
            pe.wait_ge(S["routed"], TT)
            b = B.acquire(pe, "rank")
            pe.matmul(b[:, 0:EXPERTS], upto, member[:, 0, :], start=True, stop=True)
            pe.matmul(b[:, EXPERTS:2 * EXPERTS], upto, member[:, 1, :], start=True, stop=False)
            pe.matmul(b[:, EXPERTS:2 * EXPERTS], allone, member[:, 0, :], start=False, stop=True)
            for tt in range(TT):
                pe.matmul(b[:, 2 * EXPERTS:3 * EXPERTS], allone, member[:, tt, :], start=(tt == 0), stop=(tt == 1))
            pe.matmul(b[:, 3 * EXPERTS:3 * EXPERTS + SLOTS], allone, upto[:, 0:SLOTS], start=True, stop=True) \
                .then_inc(B.done, 1)
            pe.wait_ge(A.free, A.put)
            pe.wait_ge(S["most_ready"], 1)
            fullest = pe.value_load(most[0:1, 0:1], min_val=0, max_val=T)

            assert RING == 6

            def of_pair(p, k):
                n0 = E0 + k
                return n0 % RING, p * 16 + fill_value[n0]

            def loaded(w):
                pe.wait_ge(slot_full[w[0]], w[1])
                return ring[w[0]]

            def gather(p, q, first=False):
                pe.wait_ge(S["slots_ready"], p * 8 + 8)
                for hf in range(2):
                    for kb in range(4):
                        for tt in range(TT):
                            c = (4 * hf + kb) * P
                            mm = pe.matmul(psum[hf][:, kb * P:(kb + 1) * P], xg[:, tt, c:c + P], pick[:, q, tt, :],
                                           start=(tt == 0), stop=(tt == TT - 1))
                    mm.then_inc(S["gather_done"], 1)
                if not first:
                    pe.wait_ge(S["combT_ready"], p)
                for tt in range(TT):
                    mm = tr(psum[2][:, tt * P:(tt + 1) * P], pickw[:, q, tt, :])
                mm.then_inc(S["combT_done"], 1)

            def gate_up_own(p):
                pe.wait_ge(S["gather_ready"], p * 2 + 2)
                for c, done in ((0, S["gate_done"]), (1, S["gu_done"])):
                    wt = [full(loaded(of_pair(p, 2 * c + par))) for par in range(2)]
                    for kb in range(KB):
                        for par in range(2):
                            half = slice(par * SLOTS, (par + 1) * SLOTS)
                            mm = pe.matmul(psum[3][half, c * FF:(c + 1) * FF], hgT[:, kb, half], wt[par][:, kb, :],
                                           start=(kb == 0), stop=(kb == KB - 1))
                            if kb == KB - 1:
                                mm.then_inc(done, 1)

            def down_own(p):
                pe.wait_ge(S["heT_ready"], p + 1)
                wt = [loaded(of_pair(p, 4 + par))[:, :].rearrange("p (k c) -> p k c", k=2) for par in range(2)]
                for hf in range(2):
                    for k in range(2):
                        for par in range(2):
                            half = slice(par * SLOTS, (par + 1) * SLOTS)
                            mm = pe.matmul(psum[5 + hf][half, :], heTs[:, k, half],
                                           wt[par][:, k, hf * 512:(hf + 1) * 512], start=(k == 0), stop=(k == 1))
                            if (hf, k) == (1, 1):
                                mm.then_inc(S["down_done"], 4)
                            elif (k, par) == (1, 1):
                                mm.then_inc(S["down_half"], 1)

            def turn(p):
                pe.wait_ge(S["he_ready"], p + 1)
                for k in range(2):
                    mm = tr(psum[3][:, k * P:(k + 1) * P], he[:, k * P:(k + 1) * P])
                mm.then_inc(S["heT_done"], 1)

            def mix(p, q):
                pe.wait_ge(S["ye_ready"], p * 2 + 2)
                pe.wait_ge(S["combT_ready"], p + 1)
                for r in range(4):
                    if not isinstance(p, int) or 4 * p + r >= 2:
                        pe.wait_ge(S["down_out"], p * 8 + (2 * r - 2))
                    pe.matmul(psum[(7, 4)[r % 2]][:, :], combT[:, q, (r // 2) * P:(r // 2 + 1) * P],
                              ye[:, (r % 2) * 512:(r % 2 + 1) * 512], start=True, stop=True) \
                        .then_inc(S["mixed"], 1)

            def pair(p, q):
                gate_up_own(p)
                if not isinstance(p, int) or p >= 1:
                    mix(p - 1, 1 - q)
                turn(p)
                if not isinstance(p, int) or p + 1 < PAIRS:
                    gather(p + 1, 1 - q)
                down_own(p)

            def pair_all(p):
                for k, done in ((0, S["gate_done"]), (1, S["gu_done"])):
                    for par in range(2):
                        if not isinstance(p, int) or p >= 1:
                            pe.wait_ge(S["he_ready"], p * 2 + (par - 1))
                        wt = loaded(of_pair(p, 2 * k + par))
                        for m in range(2):
                            for kb in range(KB):
                                mm = pe.matmul(psum[2 * k + par][:, m * T:(m + 1) * T],
                                               wt[:, kb * CW + m * P:kb * CW + (m + 1) * P],
                                               hT[:, kb, :], start=(kb == 0), stop=(kb == KB - 1))
                        mm.then_inc(done, 1)
                for par in range(2):
                    pe.wait_ge(S["he_ready"], p * 2 + (par + 1))
                    if par == 1 or not isinstance(p, int) or p >= 1:
                        pe.wait_ge(S["down_out"], p * 8 + 4 * par)
                    wt = loaded(of_pair(p, 4 + par))[:, :].rearrange("p (k c) -> p k c", k=2)
                    for tt in range(TT):
                        for hf in range(2):
                            for k in range(2):
                                mm = pe.matmul(psum[4 + 2 * tt + hf][:, :], heT[:, par, k, tt * P:(tt + 1) * P],
                                               wt[:, k, hf * 512:(hf + 1) * 512], start=(k == 0), stop=(k == 1))
                            mm.then_inc(S["down_done"], 1)

            with pe.If(fullest < SLOTS + 1):
                gather(0, 0, first=True)
                for p in range(2):
                    pair(p, p % 2)
                with pe.Fori(1, (PAIRS - 2) // 2) as i:
                    for j in range(2):
                        pair(i * 2 + j, j)
                for p in range(PAIRS - 2, PAIRS):
                    pair(p, p % 2)
                mix(PAIRS - 1, 1)
            with pe.Else():
                pair_all(0)
                with pe.Fori(1, PAIRS) as i:
                    pair_all(i)
            state["n"] = L0
            for p in range(PAIRS):
                for done, n in ((S["gate_done"], 1), (S["gu_done"], 1), (S["down_done"], 4)):
                    chunk_free.extend([(done, n * (2 * p + 1)), (done, n * (2 * p + 2))])
            assert len(chunk_free) == L0
            pe.wait_ge(S["down_out"], 4 * EXPERTS)

            for l in range(LAYERS):
                pe.wait_ge(S["csil_ready"], 1)
                b = A.acquire(pe, f"mod{l}")
                for j in range(8):
                    w = chunk()
                    for m in range(2):
                        c = 2 * j + m
                        for kb in range(KB):
                            mm = pe.matmul(b[:, c:c + 1], w[:, kb * CW + m * P:kb * CW + (m + 1) * P],
                                           csil[:, kb:kb + 1], start=(kb == 0), stop=(kb == KB - 1))
                    if j < 7:
                        used(mm=mm)
                mm.then_inc(A.done, 1)
                used()
                pe.wait_ge(S["cbc_ready"], l + 1)
                pe.wait_ge(S["adab_loaded"], 16 * (l + 1))
                for j in range(4):
                    w = full(chunk())
                    b = A.acquire(pe, f"gate{l}{j}")
                    for kb in range(KB):
                        pe.matmul(b[:, 0:CW], cBC[:, kb, :], w[:, kb, :], start=(kb == 0), stop=False)
                    pe.matmul(b[:, 0:CW], ones[0:1, :], adab[0:1, j * CW:(j + 1) * CW], start=False,
                              stop=True).then_inc(A.done, 1)
                    used()
                transpose_x(3 + l, f"L{l}")
                pe.wait_ge(B.free, B.upto(f"hTL{l}7"))
                for j in range(4):
                    w = chunk()
                    for m in range(2):
                        projT(w, m, hT, A, f"rx{l}{2 * j + m}")
                    used()
                w = full(chunk())
                for h in range(KB):
                    pe.wait_ge(S["conv_ready"], l * KB + h + 1)
                    b = A.acquire(pe, f"ri{l}{h}")
                    pe.matmul(b[:, 0:T], w[:, h, 0:P], rxc[:, h, :], start=True, stop=True)
                    pe.matmul(b[:, T:2 * T], w[:, h, P:2 * P], rxc[:, h, :], start=True, stop=True).then_inc(A.done, 1)
                used()
                for name in ("rz", "mx"):
                    for j in range(4):
                        w = chunk()
                        for m in range(2):
                            projT(w, m, hT, A, f"{name}{l}{2 * j + m}")
                        used()
                wq = full(chunk())
                pe.wait_ge(S["mc_ready"], l * KB + KB)

                def headT(w, src, name):
                    for h in range(MLH):
                        b = A.acquire(pe, f"{name}{l}{h}")
                        for m in range(2):
                            for k in range(2):
                                mm = pe.matmul(b[:, m * T:(m + 1) * T], w[:, 2 * h + k, m * P:(m + 1) * P],
                                               src(2 * h + k), start=(k == 0), stop=(k == 1))
                        mm.then_inc(A.done, 1)
                headT(wq, lambda k: mc[:, k, :], "mq")
                used()
                wk = full(chunk())
                headT(wk, lambda k: mc[:, k, :], "mk")
                for hp in range(2):
                    b = A.acquire(pe, f"kn{l}{hp}")
                    for h in range(2):
                        for k in range(2):
                            mm = pe.matmul(b[:, h * MLD:(h + 1) * MLD], mc[:, 2 * (2 * hp + h) + k, 0:P],
                                           wk[:, 2 * (2 * hp + h) + k, :], start=(k == 0), stop=(k == 1))
                    mm.then_inc(A.done, 1)
                used()
                wv2 = full(chunk())
                headT(wv2, lambda k: mxv[:, k, PAD:PAD + T], "mv")
                for tt in range(TT):
                    for hp in range(2):
                        b = A.acquire(pe, f"vn{l}{tt}{hp}")
                        for h in range(2):
                            for k in range(2):
                                kk = 2 * (2 * hp + h) + k
                                mm = pe.matmul(b[:, h * MLD:(h + 1) * MLD],
                                               mxv[:, kk, PAD + tt * P:PAD + (tt + 1) * P],
                                               wv2[:, kk, :], start=(k == 0), stop=(k == 1))
                        mm.then_inc(A.done, 1)
                used()
                pe.wait_ge(A.free, A.upto(f"mv{l}3"))
                pe.wait_ge(S["gate_b_loaded"], 16 * 3 * LAYERS)
                b = A.acquire(pe, f"gt{l}")
                for tt in range(TT):
                    for k in range(24):
                        src = (mqT, mkT, mvT)[k // 8]
                        mm = pe.matmul(b[:, tt * 8:tt * 8 + 8], src[:, k % 8, tt * P:(tt + 1) * P], wif[:, l, k, :],
                                       start=(k == 0), stop=(k == 23))
                mm.then_inc(A.done, 1)
                pe.wait_ge(A.free, A.upto(f"gt{l}"))
                b = B.acquire(pe, f"gr{l}")
                for g in range(2):
                    for tt in range(TT):
                        mm = tr(b[0:MLH, g * T + tt * P:g * T + (tt + 1) * P], gnat[:, tt, g * 4:g * 4 + 4])
                mm.then_inc(B.done, 1)
                for j in range(4):
                    w = full(chunk())
                    for tt in range(TT):
                        b = A.acquire(pe, f"mo{l}{j}{tt}")
                        for kb in range(KB):
                            mm = pe.matmul(b[:, 0:CW], hT[:, kb, tt * P:(tt + 1) * P], w[:, kb, :],
                                           start=(kb == 0), stop=(kb == KB - 1))
                        mm.then_inc(A.done, 1)
                    used()
                for j in range(4):
                    w = chunk()
                    for m in range(2):
                        projT(w, m, hT, A, f"mz{l}{2 * j + m}")
                    used()
                pe.wait_ge(S["row_ready"], 3 * (l + 1))
                b = B.acquire(pe, f"cols{l}")
                for n, (r, o) in enumerate(((6, 0), (6, P), (2, 0), (2, P))):
                    mm = tr(b[:, n * MLH:(n + 1) * MLH], rows[:, r, o:o + P], MLH)
                mm.then_inc(B.done, 1)
                for c in range(TT):
                    for h in range(MLH):
                        b = A.acquire(pe, f"E{l}{c}{h}")
                        pe.matmul(b[:, 0:P], rows[:, 3, c * P:(c + 1) * P], sel4[:, h, :], start=True, stop=False)
                        pe.matmul(b[:, 0:P], sel4[:, h, :], rows[:, 5, c * P:(c + 1) * P], start=False, stop=False)
                        pe.matmul(b[:, 0:P], ident[:, :], later[:, :], start=False, stop=True).then_inc(A.done, 1)
                        b = B.acquire(pe, f"St{l}{c}{h}")
                        for k in range(2):
                            mm = pe.matmul(b[:, 0:P], mkT[:, 2 * h + k, c * P:(c + 1) * P],
                                           mqT[:, 2 * h + k, c * P:(c + 1) * P], start=(k == 0), stop=(k == 1))
                        mm.then_inc(B.done, 1)
                        if c == 1:
                            b = A.acquire(pe, f"in{l}{h}")
                            for k in range(2):
                                mm = pe.matmul(b[:, 0:VW], mqT[:, 2 * h + k, P:2 * P], caug[:, h, k, :],
                                               start=(k == 0), stop=(k == 1))
                            mm.then_inc(A.done, 1)
                        pe.wait_ge(B.free, B.upto(f"St{l}{c}{h}"))
                        b = B.acquire(pe, f"nm{l}{c}{h}")
                        pe.matmul(b[:, 0:VW], stb[:, h % 2, :], vaug[:, c, h, :], start=True, stop=True) \
                            .then_inc(B.done, 1)
                    if c == 0:
                        pe.wait_ge(S["kw_ready"], MLH * (l + 1))
                        pe.wait_ge(S["rg_done"], l + 1)
                        for h in range(MLH):
                            for k in range(2):
                                b = A.acquire(pe, f"C{l}{h}{k}")
                                pe.matmul(b[:, 0:VW], knat[:, h, k * P:(k + 1) * P], vaug[:, 0, h, :],
                                          start=True, stop=True).then_inc(A.done, 1)
                        pe.wait_ge(A.free, A.upto(f"C{l}31"))
                pe.wait_ge(S["hq_ready"], l + 1)
                for m in range(KB):
                    b = B.acquire(pe, f"ym{l}{m}")
                    for tt in range(TT):
                        mm = tr(b[:, tt * P:(tt + 1) * P], hh[:, tt, m * P:(m + 1) * P])
                    mm.then_inc(B.done, 1)
                pe.wait_ge(B.free, B.upto(f"ym{l}7"))
                for j in range(4):
                    bb = [B.acquire(pe, f"xo{l}{j}{tt}") for tt in range(TT)]
                    for kh, yT in ((0, thr), (1, ymT)):
                        w = full(chunk())
                        for tt in range(TT):
                            for kb in range(KB):
                                mm = pe.matmul(bb[tt][:, 0:CW], yT[:, kb, tt * P:(tt + 1) * P], w[:, kb, :],
                                               start=(kh == 0 and kb == 0), stop=(kh == 1 and kb == KB - 1))
                            if kh == 1:
                                mm.then_inc(B.done, 1)
                        if kh == 1:
                            used(B)
                        else:
                            used(mm=mm)
            assert state["n"] == len(nparts), state

        @block.sync
        def _(sp):
            sp.dma_start(x[:, 0, :], a["x"][0, 0:P, :]).then_inc(S["x_loaded"], 16)
            sp.dma_start(x[:, 1, :], a["x"][0, P:T, :]).then_inc(S["x_loaded"], 16)

            def load(n, parts):
                if n >= RING:
                    sp.wait_ge(*chunk_free[n - RING])
                for dst, src in parts:
                    sp.dma_start(dst(ring[n % RING]), src).then_inc(slot_full[n % RING], 16)

            for n, parts in enumerate(chunks):
                load(n, parts)

            def expert_part(e, kind):
                k = 2 if kind == "w_down" else KB
                return (lambda t: t[:, :].rearrange("p (k c) -> p k c", k=k),
                        a[kind][0, e].rearrange("(k p) c -> p k c", p=P))

            kinds = (("w_gate", S["gate_done"], 1), ("w_up", S["gu_done"], 1), ("w_down", S["down_done"], 4))
            for k, (kind, _, _) in enumerate(kinds):
                for par in range(2):
                    load(E0 + 2 * k + par, [expert_part(par, kind)])
            with sp.Fori(1, PAIRS) as i:
                for k, (kind, used_sem, per_expert) in enumerate(kinds):
                    for par in range(2):
                        n0 = E0 + 2 * k + par
                        sp.wait_ge(used_sem, i * (2 * per_expert) + (par - 1) * per_expert)
                        dst, src = expert_part(i * 2 + par, kind)
                        sp.dma_start(dst(ring[n0 % RING]), src).then_inc(slot_full[n0 % RING], 16)

            for n, parts in enumerate(tail):
                load(L0 + n, parts)
            for tt in range(TT):
                sp.wait_ge(S["layer_done"], LAYERS + tt + 1)
                sp.dma_start(out[0, tt * P:(tt + 1) * P, :], xn[:, tt, :]).then_inc(S["x_stored"], 16)
            sp.wait_ge(S["x_stored"], 32)

        @block.scalar
        def _(act):
            step = Chain(act, s_act)
            f = act.activation

            def roots(n, view):
                act.wait_ge(S["root_wanted"], n)
                step(f(view, view, ACT.Sqrt), S["root_ready"])

            def sumsq():
                for tt in range(TT):
                    step(f(squares[:, tt, :], x[:, tt, :], ACT.Square, accum_out=small[:, tt:tt + 1]), S["ssq_ready"])

            def out_copy(dst, n, func=ACT.Copy, **k):
                b = A.take(act)
                step(f(dst, b[:, 0:n], func, **k), A.free)

            act.wait_ge(S["x_loaded"], 32)
            sumsq()
            roots(1, small[:, 2:4])
            act.wait_ge(B.free, B.upto("colA"))
            step(f(csil[:, :], colA[:, 17:25], ACT.Tanh, scale=0.5), S["csil_tanh"])
            for tt in range(TT):
                b = A.take(act)
                step(f(ckv[:, tt, :], b[:, 0:RANK], ACT.Copy))
                step(f(pT[:, 0, tt, :], b[:, 0:RANK], ACT.Square, accum_out=small[:, 4 + tt:5 + tt]), A.free)
            out_copy(kiT, T)
            b = A.take(act)
            step(f(wi, b[:, 0:16].rearrange("p (t h) -> p t h", t=TT), ACT.Copy, scale=IDX_SCALE), A.free)
            roots(2, small[:, 6:8])
            for m in range(4):
                out_copy(qT[:, m, :], T)
            for m in range(4):
                out_copy(qiT[:, m, :], T)
            for tt in range(TT):
                ns = (tt + 1) * P
                for h in range(HEADS):
                    k = tt * HEADS + h
                    b = A.take(act)
                    if k >= 2:
                        act.wait_ge(S["relu_used"], k - 1)
                    step(f(relu[:, k % 2, 0:ns], b[:, 0:ns], ACT.Relu), A.free)
            for m in range(4):
                out_copy(kvT[:, m, :], T)
            for tt in range(TT):
                out_copy(vnat[:, tt, :], 512)
            for m in range(4):
                out_copy(guT[:, m, :], T, ACT.Gelu_apprx_tanh)
            for j in range(2):
                for tt in range(TT):
                    out_copy(gv[:, tt, j * CW:(j + 1) * CW], CW, ACT.Gelu_apprx_tanh)
            out_copy(wsT, 512)
            roots(3, small[:, 12:14])
            gates = [(tga, m) for m in range(KB)] + [(tgb, m) for m in range(KB)]

            def gate_job():
                if gates:
                    t, m = gates.pop(0)
                    out_copy(t[:, m, :], T, ACT.Tanh, scale=0.5)

            for h in range(HEADS + 1):
                gate_job()
                if h < HEADS:
                    for tt in range(TT):
                        ns = (tt + 1) * P
                        k = 2 * h + tt
                        act.wait_ge(S["sc_ready"], k + 1)
                        if k >= 4:
                            act.wait_ge(A.done, A.upto(f"pT{h - 2}"))
                        step(f(prob[h % 2][tt][:, 0:ns], sc[:, tt, 0:ns], ACT.Exp, bias=rt[:, tt:tt + 1],
                               accum_out=rt[:, 2 + tt:3 + tt]), S["p_ready"])
                gate_job()
                if h >= 1:
                    g = h - 1
                    o = (g % 2) * 64
                    b = A.take(act)
                    step(f(pT[:, g % 2, :, :], b[:, 0:384].rearrange("p (s q) -> p s q", s=3), ACT.Copy), A.free)
                    b = A.take(act)
                    step(f(oaT[o:o + 64, g // 2, :], b[o:o + 64, 0:T], ACT.Copy), A.free)
            act.wait_ge(B.free, B.upto("xo31"))
            sumsq()
            roots(4, small[:, 2:4])
            for tt in range(TT):
                for k in range(2):
                    act.wait_ge(S["exp_wanted"], 2 * tt + k + 1)
                    n = (EG, EPG)[k]
                    src = rt[:, 8:12] if k == 0 else rt[:, 16:24]
                    if k == 0:
                        step(f(rt[:, 12:16], src, ACT.Exp, accum_out=rt[:, 7:8]), S["exp_ready"])
                    else:
                        step(f(rt[:, 24:32], src, ACT.Exp), S["exp_ready"])
            act.wait_ge(S["most_ready"], 1)
            fullest = act.value_load(most[0:1, 0:1], min_val=0, max_val=T)

            def gathered(p, q):
                for hf in range(2):
                    act.wait_ge(S["gather_done"], p * 2 + (hf + 1))
                    f(hgT[:, 4 * hf:4 * hf + 4, :], psum[hf][:, :].rearrange("p (b s) -> p b s", b=4), ACT.Copy) \
                        .then_inc(S["gather_ready"], 1)
                act.wait_ge(S["combT_done"], p + 1)
                f(combT[:, q, :], psum[2][:, 0:T], ACT.Copy).then_inc(S["combT_ready"], 1)

            def pair(p, q):
                act.wait_ge(S["gu_done"], p * 2 + 2)
                f(thgs, psum[3][:, 0:FF], ACT.Tanh, scale=0.5).then_inc(S["tanh_gate"], 1)
                act.wait_ge(S["heT_done"], p + 1)
                f(heTs, psum[3][:, 0:2 * P].rearrange("p (b s) -> p b s", b=2), ACT.Copy).then_inc(S["heT_ready"], 1)
                if not isinstance(p, int) or p + 1 < PAIRS:
                    gathered(p + 1, 1 - q)
                for hf in range(2):
                    if hf == 0:
                        act.wait_ge(S["down_half"], p + 1)
                    else:
                        act.wait_ge(S["down_done"], p * 8 + 8)
                    f(ye[:, hf * 512:(hf + 1) * 512], psum[5 + hf][:, :], ACT.Copy).then_inc(S["ye_ready"], 1)

            def gate_tanh(e, par):
                act.wait_ge(S["gu_done"], e + 1)
                if isinstance(e, int) and e < 2:
                    pass
                else:
                    act.wait_ge(S["he_ready"], e - 1)
                f(thg[:, par, :], psum[par][:, :], ACT.Tanh, scale=0.5).then_inc(S["tanh_gate"], 1)

            with act.If(fullest < SLOTS + 1):
                gathered(0, 0)
                for p in range(2):
                    pair(p, p % 2)
                with act.Fori(1, (PAIRS - 2) // 2) as i:
                    for j in range(2):
                        pair(i * 2 + j, j)
                for p in range(PAIRS - 2, PAIRS):
                    pair(p, p % 2)
            with act.Else():
                gate_tanh(0, 0)
                gate_tanh(1, 1)
                with act.Fori(1, EXPERTS // 2) as i:
                    for j in range(2):
                        gate_tanh(i * 2 + j, j)
            act.wait_ge(S["down_out"], 4 * EXPERTS)
            sumsq()
            roots(5, small[:, 2:4])
            act.wait_ge(S["sp_wanted"], 1)
            step(f(labs, labs, ACT.Exp, scale=-1.0), S["sp_ready"])
            for l in range(LAYERS):
                if l == 0:
                    act.wait_ge(S["rstd_used"], 1)
                else:
                    act.wait_ge(S["layer_done"], l)
                out_copy(modc[:, :], 16)
                for j in range(4):
                    out_copy(gateB[:, j * CW:(j + 1) * CW], CW)
                sumsq()
                roots(6 + 2 * l, small[:, 2:4])
                for m in range(KB):
                    out_copy(rxv[:, m, PAD:PAD + T], T)
                for h in range(KB):
                    b = A.take(act)
                    if h == 0:
                        act.wait_ge(S["mod_ready"], l + 1)
                    step(f(thr[:, h, :], b[:, 0:T], ACT.Tanh, scale=0.5, bias=hb[:, l, h:h + 1]))
                    step(f(thi[:, h, :], b[:, T:2 * T], ACT.Tanh, scale=0.5, bias=hb[:, l, KB + h:KB + h + 1]), A.free)
                for h in range(KB):
                    step(f(aa[:, h, :], thr[:, h, :], ACT.Exp, scale=n4[:, 1, h:h + 1], bias=n4[:, 1, h:h + 1]))
                    step(f(tl[:, h, :], thr[:, h, :], ACT.Tanh, scale=n4[:, 0, h:h + 1], bias=n4[:, 0, h:h + 1]),
                         S["rg_gate"])
                def silu_part(dst, th_dst, name):
                    for m in range(KB):
                        b = A.take(act)
                        step(f(dst[:, m, :], b[:, 0:T], ACT.Copy))
                        step(f(th_dst[:, m, :], b[:, 0:T], ACT.Tanh, scale=0.5), A.free)
                act.wait_ge(S["xn_ready"], 3 + l)
                act.wait_ge(B.free, B.upto(f"hTL{l}7"))
                silu_part(zr, mth, "rz")
                for m in range(KB):
                    out_copy(mxv[:, m, PAD:PAD + T], T)
                act.wait_ge(S["rg_root_wanted"], l + 1)
                step(f(tl[:, :, :], tl[:, :, :], ACT.Sqrt), S["rg_root"])
                for m in range(KB):
                    act.wait_ge(S["mconv_ready"], l * KB + m + 1)
                    step(f(mth[:, m, :], mc[:, m, :], ACT.Tanh, scale=0.5), S["mtanh_ready"])
                for h in range(MLH):
                    b = A.take(act)
                    step(f(mqT[:, 2 * h:2 * h + 2, :], b[:, :].rearrange("p (m t) -> p m t", m=2), ACT.Copy,
                           scale=0.5), A.free)
                for h in range(MLH):
                    b = A.take(act)
                    step(f(mkT[:, 2 * h:2 * h + 2, :], b[:, :].rearrange("p (m t) -> p m t", m=2), ACT.Copy,
                           scale=0.5), A.free)
                for hp in range(2):
                    b = A.take(act)
                    step(f(knat[:, 2 * hp:2 * hp + 2, :], b[:, :].rearrange("p (h c) -> p h c", h=2), ACT.Copy,
                           scale=0.5 * MLD ** -0.5), A.free)
                act.wait_ge(S["rg_done"], l + 1)
                for h in range(MLH):
                    b = A.take(act)
                    step(f(mvT[:, 2 * h:2 * h + 2, :], b[:, :].rearrange("p (m t) -> p m t", m=2), ACT.Copy), A.free)
                for tt in range(TT):
                    for hp in range(2):
                        b = A.take(act)
                        step(f(vaug[:, tt, 2 * hp:2 * hp + 2, 0:MLD], b[:, :].rearrange("p (h c) -> p h c", h=2),
                               ACT.Copy), A.free)
                b = A.take(act)
                step(f(gnat[:, :, :], b[:, 0:16].rearrange("p (t g) -> p t g", t=TT), ACT.Copy), A.free)
                act.wait_ge(S["lf_wanted"], l + 1)
                step(f(rows[:, 2, :], rows[:, 2, :], ACT.Exp, scale=-1.0), S["lf_ready"])
                for j in range(4):
                    for tt in range(TT):
                        out_copy(oth[:, tt, j * CW:(j + 1) * CW], CW, ACT.Tanh, scale=0.5)
                act.wait_ge(S["mc_ready"], l * KB + KB)
                silu_part(zm, mth, "mz")
                act.wait_ge(S["row_wanted"], l + 1)
                step(f(rows[:, 6, 0:P], rows[:, 3, 0:P], ACT.Exp, bias=rsc[:, 0:1]), S["row_ready"])
                step(f(rows[:, 6, P:T], rows[:, 5, P:T], ACT.Exp, bias=rsc[:, 1:2]), S["row_ready"])
                step(f(rows[:, 2, :], rows[:, 2, :], ACT.Exp, scale=-1.0), S["row_ready"])
                act.wait_ge(S["z_used"], 2 * (l + 1))
                for c in range(TT):
                    for h in range(MLH):
                        b = A.take(act)
                        k8 = l * 8 + c * MLH + h
                        if h >= 2:
                            act.wait_ge(B.free, B.upto(f"St{l}{c}{h - 2}"))
                        elif c == 1:
                            act.wait_ge(B.free, B.upto(f"St{l}0{h + 2}"))
                        step(f(ebuf[:, h % 2, :], b[:, 0:P], ACT.Exp), A.free)
                        if c == 1:
                            b = A.take(act)
                            act.wait_ge(B.free, B.upto(f"cols{l}"))
                            if h >= 2:
                                act.wait_ge(S["hh_ready"], k8 - 1)
                            step(f(inter[:, h % 2, :], b[:, 0:VW], ACT.Copy, scale=cols[:, 1, h:h + 1]), A.free)
                    if c == 0:
                        for h in range(MLH):
                            for k in range(2):
                                out_copy(caug[:, h, k, :], VW)
                for c in range(TT):
                    for h in range(MLH):
                        act.wait_ge(S["hh_ready"], l * 8 + c * MLH + h + 1)
                        step(f(mth[:, 0, :], hh[:, c, h * MLD:(h + 1) * MLD], ACT.Square,
                               accum_out=small[:, 16 + c * MLH + h:17 + c * MLH + h]), S["ssq_ready"])
                roots(7 + 2 * l, small[:, 24:32])
            act.wait_ge(S["layer_done"], LAYERS)
            sumsq()
            roots(6 + 2 * LAYERS, small[:, 2:4])

        @block.vector
        def _(v):
            step = Chain(v, s_dve)
            tsc, stt, tten = v.tensor_scalar, v.scalar_tensor_tensor, v.tensor_tensor
            roots_n = {"n": 0, "ssq": 0}

            def rstd(dst, src, scale):
                roots_n["n"] += 1
                step(tsc(dst, src, scale, EPS, ALU.mult, ALU.add), S["root_wanted"])
                v.wait_ge(S["root_ready"], roots_n["n"])
                step(v.reciprocal(dst, dst))

            def norm_x():
                roots_n["ssq"] += 2
                v.wait_ge(S["ssq_ready"], roots_n["ssq"])
                rstd(small[:, 2:4], small[:, 0:2], 1.0 / D)

            def take_hT(scale, shift=None):
                for kb in range(KB):
                    b = B.take(v)
                    if shift is None:
                        step(tsc(hT[:, kb, :], b[:, 0:T], scale[:, kb:kb + 1], None, ALU.mult), B.free)
                    else:
                        step(tsc(hT[:, kb, :], b[:, 0:T], scale[:, kb:kb + 1], shift[:, kb:kb + 1], ALU.mult, ALU.add),
                             B.free)

            def log1p(dst, e, y, t):
                step(tsc(t, e, 2.0, None, ALU.add))
                step(v.reciprocal(t, t))
                step(tten(y, e, t, ALU.mult))
                step(tten(t, y, y, ALU.mult))
                step(tsc(dst, t, LOG1P[0], None, ALU.mult))
                for c in LOG1P[1:]:
                    step(stt(dst, dst, c, t, ALU.add, ALU.mult))
                step(stt(dst, dst, 1.0, y, ALU.add, ALU.mult))
                step(tsc(dst, dst, 2.0, None, ALU.mult))

            norm_x()
            for tt in range(TT):
                ins = tsc(xn[:, tt, :], x[:, tt, :], small[:, 2 + tt:3 + tt], None, ALU.mult)
                step(ins, S["xn_ready"]) if tt == 1 else step(ins)
            b = B.take(v)
            step(v.tensor_copy(colA[:, 0:25], b[:, 0:25]), B.free)
            b = B.take(v)
            step(v.tensor_copy(relrow, b[0:HEADS, :]), B.free)
            for l in range(LAYERS):
                b = B.take(v)
                step(v.tensor_copy(colL[:, l, :], b[:, 0:P]))
                step(v.tensor_copy(colM[:, l, :], b[:, P:P + 16]), B.free)
            take_hT(colA[:, 0:8])
            v.wait_ge(S["csil_tanh"], 1)
            step(stt(csil[:, :], csil[:, :], 1.0, colA[:, 17:25], ALU.add, ALU.mult))
            step(tsc(csil[:, :], csil[:, :], 0.5, None, ALU.mult), S["csil_ready"])
            v.wait_ge(A.free, A.upto("ckv1"))
            rstd(small[:, 6:8], small[:, 4:6], 1.0 / RANK)
            for tt in range(TT):
                ins = tsc(ckv[:, tt, :], ckv[:, tt, :], small[:, 6 + tt:7 + tt], None, ALU.mult)
                step(ins, S["ckv_ready"]) if tt == 1 else step(ins)
            v.wait_ge(A.free, A.upto("wi"))
            for tt in range(TT):
                ns = (tt + 1) * P
                for h in range(HEADS):
                    v.wait_ge(A.free, A.upto(f"idx{tt}{h}"))
                    k = tt * HEADS + h
                    r = relu[:, k % 2, 0:ns]
                    if h == 0:
                        step(tsc(idx[:, tt, 0:ns], r, wi[:, tt, h:h + 1], None, ALU.mult), S["relu_used"])
                    else:
                        step(stt(idx[:, tt, 0:ns], r, wi[:, tt, h:h + 1], idx[:, tt, 0:ns], ALU.mult, ALU.add),
                             S["relu_used"])
            b = B.take(v)
            step(tsc(cT, b[:, 0:T], colA[:, 16:17], None, ALU.mult), B.free)
            for tt in range(TT):
                ns = (tt + 1) * P
                v.wait_ge(S["idx_masked"], tt + 1)
                for r in range(TOPK // 8):
                    step(v.max(m8[:, :], idx[:, tt, 0:ns]))
                    step(v.match_replace(idx[:, tt, 0:ns], m8[:, :], idx[:, tt, 0:ns], TAKEN))
                step(tsc(maskb[:, tt, 0:ns], idx[:, tt, 0:ns], TAKEN, None, ALU.is_equal))
                step(tsc(maskb[:, tt, 0:ns], maskb[:, tt, 0:ns], -1.0, BIG, ALU.add, ALU.mult), S["sel_ready"])
            v.wait_ge(A.free, A.upto("v11"))
            for tt in range(TT):
                step(v.bn_stats(vst[:, 0:6], gv[:, tt, :]))
                step(v.bn_aggr(vst[:, 8 + 2 * tt:10 + 2 * tt], vst[:, 0:6]))
                step(v.tensor_copy(small[:, 12 + tt:13 + tt], vst[:, 9 + 2 * tt:10 + 2 * tt]))
            rstd(small[:, 12:14], small[:, 12:14], 1.0)
            v.wait_ge(S["ln_loaded"], 48)
            for tt in range(TT):
                step(tsc(gv[:, tt, :], gv[:, tt, :], vst[:, 8 + 2 * tt:9 + 2 * tt], small[:, 12 + tt:13 + tt],
                         ALU.subtract, ALU.mult))
                step(tten(gv[:, tt, :], gv[:, tt, :], lng, ALU.mult))
                ins = tten(gv[:, tt, :], gv[:, tt, :], lnb, ALU.add)
                step(ins, S["vln_ready"]) if tt == 1 else step(ins)
            v.wait_ge(S["mask_ready"], 2)
            for h in range(HEADS):
                for tt in range(TT):
                    ns = (tt + 1) * P
                    k = 2 * h + tt
                    b = B.take(v)
                    if k >= 2:
                        v.wait_ge(S["p_ready"], k - 1)
                    step(stt(sc[:, tt, 0:ns], b[:, 0:ns], SCALE, maskb[:, tt, 0:ns], ALU.mult, ALU.add), B.free)
                    step(v.tensor_reduce(rt[:, tt:tt + 1], sc[:, tt, 0:ns], AX.X, ALU.max, negate=True), S["sc_ready"])
                for tt in range(TT):
                    ns = (tt + 1) * P
                    v.wait_ge(S["p_ready"], 2 * h + tt + 1)
                    step(v.reciprocal(rt[:, 4 + tt:5 + tt], rt[:, 2 + tt:3 + tt]))
                    pn = prob[h % 2][tt][:, 0:ns]
                    step(tsc(pn, pn, rt[:, 4 + tt:5 + tt], None, ALU.mult), S["prob_ready"])
            for g in range(GROUPS):
                b = B.take(v)
                step(tten(gmT[:, g, :], b[:, 0:T], guT[:, g, :], ALU.mult), B.free)
            v.wait_ge(A.free, A.upto("g15"))
            for m in range(KB):
                b = B.take(v)
                step(stt(mtmp[:, 0, :], tga[:, m, :], 1.0, b[:, 0:T], ALU.add, ALU.mult), B.free)
                b = B.take(v)
                step(stt(mtmp[:, 1, :], tgb[:, m, :], 1.0, b[:, 0:T], ALU.add, ALU.mult), B.free)
                step(tten(mgT[:, m, :], mtmp[:, 0, :], mtmp[:, 1, :], ALU.add), S["mg_ready"])
            for j in range(4):
                for tt in range(TT):
                    b = B.take(v)
                    xs = x[:, tt, j * CW:(j + 1) * CW]
                    step(stt(xs, b[:, 0:CW], 0.5, xs, ALU.mult, ALU.add), B.free)
            norm_x()
            v.wait_ge(S["norm2_loaded"], 16)
            for tt in range(TT):
                ins = stt(xg[:, tt, :], x[:, tt, :], small[:, 2 + tt:3 + tt], norm2, ALU.mult, ALU.mult)
                step(ins, S["xn_ready"]) if tt == 1 else step(ins)
            for kb in range(KB):
                b = B.take(v)
                step(v.tensor_copy(hT[:, kb, :], b[:, 0:T]), B.free)
            b = B.take(v)
            NR = EG + EXPERTS
            step(v.tensor_copy(logit[:, :, :], b[:, 0:TT * NR].rearrange("p (t n) -> p t n", t=TT)), B.free)
            v.wait_ge(S["const_ready"], 1)

            def first_max(onehot, vals, n, t1):
                step(v.tensor_reduce(t1, vals, AX.X, ALU.max))
                step(stt(onehot, vals, t1, desc[:, 0:n], ALU.is_equal, ALU.mult))
                step(v.tensor_reduce(t1, onehot, AX.X, ALU.max))
                step(tsc(onehot, desc[:, 0:n], t1, None, ALU.is_equal))

            for tt in range(TT):
                lg = logit[:, tt, 0:EG]
                step(v.tensor_reduce(rt[:, 6:7], lg, AX.X, ALU.max))
                step(tsc(rt[:, 8:12], lg, rt[:, 6:7], None, ALU.subtract), S["exp_wanted"])
                v.wait_ge(S["exp_ready"], 2 * tt + 1)
                step(v.reciprocal(rt[:, 32:33], rt[:, 7:8]))
                first_max(rt[:, 36:40], rt[:, 12:16], EG, rt[:, 33:34])
                for g in range(EG):
                    le = logit[:, tt, EG + g * EPG:EG + (g + 1) * EPG]
                    if g == 0:
                        step(tsc(rt[:, 16:24], le, rt[:, 36:37], None, ALU.mult))
                    else:
                        step(stt(rt[:, 16:24], le, rt[:, 36 + g:37 + g], rt[:, 16:24], ALU.mult, ALU.add))
                step(v.tensor_reduce(rt[:, 6:7], rt[:, 16:24], AX.X, ALU.max))
                step(tsc(rt[:, 16:24], rt[:, 16:24], rt[:, 6:7], None, ALU.subtract), S["exp_wanted"])
                v.wait_ge(S["exp_ready"], 2 * tt + 2)
                first_max(rt[:, 40:48], rt[:, 24:32], EPG, rt[:, 33:34])
                step(stt(rt[:, 24:32], rt[:, 40:48], -2.0, rt[:, 24:32], ALU.mult, ALU.add))
                step(v.tensor_reduce(rt[:, 34:35], rt[:, 24:32], AX.X, ALU.max))
                first_max(rt[:, 48:56], rt[:, 24:32], EPG, rt[:, 33:34])
                step(tsc(rt[:, 35:36], rt[:, 34:35], 1.0, None, ALU.add))
                step(v.reciprocal(rt[:, 35:36], rt[:, 35:36]))
                step(stt(rt[:, 35:36], rt[:, 35:36], 0.5, rt[:, 32:33], ALU.mult, ALU.mult))
                step(stt(rt[:, 48:56], rt[:, 48:56], rt[:, 34:35], rt[:, 40:48], ALU.mult, ALU.add))
                step(tsc(rt[:, 48:56], rt[:, 48:56], rt[:, 35:36], None, ALU.mult))
                for g in range(EG):
                    step(tsc(comb[:, tt, g * EPG:(g + 1) * EPG], rt[:, 48:56], rt[:, 36 + g:37 + g], None, ALU.mult))
                step(tsc(member[:, tt, :], comb[:, tt, :], 0.0, None, ALU.is_gt), S["routed"])
            b = B.take(v)
            step(tten(key[:, :, :], b[:, 0:2 * EXPERTS].rearrange("p (t e) -> p t e", t=TT), member[:, :, :],
                      ALU.mult))
            step(v.tensor_copy(slotno, b[:, 3 * EXPERTS:3 * EXPERTS + SLOTS]))
            step(v.tensor_reduce(rt[:, 0:1], b[:, 2 * EXPERTS:3 * EXPERTS], AX.X, ALU.max), B.free)
            step(v.tensor_copy(most[:, :], rt[:, 0:1]), S["most_ready"])
            fullest = v.value_load(most[0:1, 0:1], min_val=0, max_val=T)

            def slots(p, q):
                if not isinstance(p, int) or p >= 2:
                    v.wait_ge(S["combT_done"], p - 1)
                for tt in range(TT):
                    for j in range(2):
                        e = p * 2 + j
                        es = slice(e, e + 1) if isinstance(e, int) else bass.ds(e, 1)
                        js = slice(j * SLOTS, (j + 1) * SLOTS)
                        tsc(pick[:, q, tt, js], slotno, key[:, tt, es], None, ALU.is_equal) \
                            .then_inc(S["slots_ready"], 1)
                        tsc(pickw[:, q, tt, js], slotno, key[:, tt, es], comb[:, tt, es], ALU.is_equal, ALU.mult) \
                            .then_inc(S["slots_ready"], 1)

            def act_own(p):
                v.wait_ge(S["tanh_gate"], p + 1)
                stt(sg[:, 0:FF], thgs, 1.0, psum[3][:, 0:FF], ALU.add, ALU.mult).then_inc(S["silu_ready"], 1)
                v.wait_ge(S["silu_ready"], p + 1)
                tten(he, psum[3][:, FF:2 * FF], sg[:, 0:FF], ALU.mult).then_inc(S["he_ready"], 1)
                v.wait_ge(S["he_ready"], p + 1)

            def mix_add(p):
                for r in range(4):
                    v.wait_ge(S["mixed"], p * 4 + (r + 1))
                    if r == 0 and not (isinstance(p, int) and p == 0):
                        v.wait_ge(S["down_out"], p * 8)
                    xs = x[:, r // 2, (r % 2) * 512:(r % 2 + 1) * 512]
                    tten(xs, psum[(7, 4)[r % 2]][:, :], xs, ALU.add).then_inc(S["down_out"], 2)

            def pair(p, q):
                act_own(p)
                if not isinstance(p, int) or p >= 1:
                    mix_add(p - 1)
                if not isinstance(p, int) or p + 2 < PAIRS:
                    slots(p + 2, q)

            def gu(e, par):
                v.wait_ge(S["tanh_gate"], e + 1)
                v.scalar_tensor_tensor(sg[:, :], thg[:, par, :], 1.0, psum[par][:, :], ALU.add, ALU.mult) \
                    .then_inc(S["silu_ready"], 1)
                v.wait_ge(S["silu_ready"], e + 1)
                v.tensor_tensor(heT[:, par, :, :], psum[2 + par][:, :].rearrange("p (b t) -> p b t", b=2),
                                sg[:, :].rearrange("p (b t) -> p b t", b=2), ALU.mult).then_inc(S["he_ready"], 1)
                v.wait_ge(S["he_ready"], e + 1)

            def down_add(e):
                for tt in range(TT):
                    for hf in range(2):
                        k = 2 * tt + hf
                        v.wait_ge(S["down_done"], e * 4 + (k + 1))
                        if k == 0 and not (isinstance(e, int) and e == 0):
                            v.wait_ge(S["down_out"], e * 4)
                        xs = x[:, tt, hf * 512:(hf + 1) * 512]
                        v.scalar_tensor_tensor(xs, psum[4 + k][:, :], comb[:, tt, bass.ds(e, 1)] if not isinstance(e, int)
                                               else comb[:, tt, e:e + 1], xs, ALU.mult, ALU.add) \
                            .then_inc(S["down_out"], 1)
            with v.If(fullest < SLOTS + 1):
                slots(0, 0)
                slots(1, 1)
                for p in range(2):
                    pair(p, p % 2)
                with v.Fori(1, (PAIRS - 2) // 2) as i:
                    for j in range(2):
                        pair(i * 2 + j, j)
                for p in range(PAIRS - 2, PAIRS):
                    pair(p, p % 2)
                mix_add(PAIRS - 1)
            with v.Else():
                def pair_all(p):
                    for par in range(2):
                        gu(p * 2 + par, par)
                    for par in range(2):
                        down_add(p * 2 + par)

                pair_all(0)
                with v.Fori(1, PAIRS) as i:
                    pair_all(i)
            v.wait_ge(S["down_out"], 4 * EXPERTS)
            norm_x()
            v.wait_ge(S["gfin_loaded"], 16)
            for tt in range(TT):
                ins = stt(x[:, tt, :], x[:, tt, :], small[:, 2 + tt:3 + tt], gfin[:, :], ALU.mult, ALU.mult)
                if tt == 1:
                    step(ins, S["rstd_used"])
                else:
                    step(ins)
            step(tsc(lneg, colL[:, :, V_LAM:V_LAM + KB], -1.0, None, ALU.mult))
            step(tten(labs, lneg, colL[:, :, V_LAM:V_LAM + KB], ALU.max), S["sp_wanted"])
            v.wait_ge(S["sp_ready"], 1)
            log1p(lsp, labs, ly, lt)
            step(stt(lsp, lneg, 0.0, lsp, ALU.max, ALU.add))
            step(tsc(hb[:, :, :], colL[:, :, V_BA:V_BA + 2 * KB], 0.5, None, ALU.mult), S["hb_ready"])

            for l in range(LAYERS):
                step(v.tensor_copy(cBC[:, :, :], csil[:, :].unsqueeze(2).broadcast_to([P, KB, P])), S["cbc_ready"])
                norm_x()
                for tt in range(TT):
                    ins = tsc(xn[:, tt, :], x[:, tt, :], small[:, 2 + tt:3 + tt], None, ALU.mult)
                    step(ins, S["xn_ready"]) if tt == 1 else step(ins)
                v.wait_ge(A.free, A.upto(f"mod{l}"))
                step(tten(modc[:, :], modc[:, :], colL[:, l, V_ADA:V_ADA + 16], ALU.add))
                step(stt(gs[:, :], modc[:, 8:16], 1.0, colL[:, l, V_NORM:V_NORM + KB], ALU.add, ALU.mult))
                step(tsc(n4[:, 0, :], lsp[:, l, :], 4.0, None, ALU.mult))
                step(tsc(n4[:, 1, :], lsp[:, l, :], -4.0, None, ALU.mult), S["mod_ready"])
                take_hT(gs, modc)

                def conv(dst, src, wcol, bcol, m, signal):
                    step(tsc(dst[:, m, :], src[:, m, 0:T], wcol(0, m), bcol(m), ALU.mult, ALU.add))
                    for j in range(1, TAPS):
                        ins = stt(dst[:, m, :], src[:, m, j:j + T], wcol(j, m), dst[:, m, :], ALU.mult, ALU.add)
                        step(ins, signal) if j == TAPS - 1 else step(ins)
                if l == 0:
                    v.wait_ge(S["pads_ready"], 1)
                for m in range(KB):
                    v.wait_ge(A.free, A.upto(f"rx{l}{m}"))
                    conv(rxc, rxv, lambda j, m: colL[:, l, V_RCW + j * KB + m:V_RCW + j * KB + m + 1],
                         lambda m: colL[:, l, V_RCB + m:V_RCB + m + 1], m, S["conv_ready"])
                v.wait_ge(S["rg_gate"], KB * (l + 1))
                step(tten(thr[:, :, :], aa[:, :, :], aa[:, :, :], ALU.mult))
                step(stt(tl[:, :, :], thr[:, :, :], 1.0, tl[:, :, :], ALU.add, ALU.mult), S["rg_root_wanted"])
                step(stt(thi[:, :, :], thi[:, :, :], 1.0, rxc[:, :, :], ALU.add, ALU.mult))
                v.wait_ge(A.free, A.upto(f"rz{l}7"))
                step(stt(zr[:, :, :], mth[:, :, :], 1.0, zr[:, :, :], ALU.add, ALU.mult), S["z_used"])
                for m in range(KB):
                    v.wait_ge(A.free, A.upto(f"mx{l}{m}"))
                    conv(mc, mxv, lambda j, m: colL[:, l, V_MCW + j * KB + m:V_MCW + j * KB + m + 1],
                         lambda m: colM[:, l, m:m + 1], m, S["mconv_ready"])
                for m in range(KB):
                    v.wait_ge(S["mtanh_ready"], l * KB + m + 1)
                    step(stt(mc[:, m, :], mth[:, m, :], 1.0, mc[:, m, :], ALU.add, ALU.mult), S["mc_ready"])
                v.wait_ge(S["rg_root"], l + 1)
                step(stt(thi[:, :, :], tl[:, :, :], 0.5, thi[:, :, :], ALU.mult, ALU.mult))
                for h in range(KB):
                    step(v.tensor_tensor_scan(thr[:, h, :], aa[:, h, :], thi[:, h, :], 0.0, ALU.mult, ALU.add))
                step(stt(thr[:, :, :], thr[:, :, :], 0.5, zr[:, :, :], ALU.mult, ALU.mult), S["rg_done"])
                v.wait_ge(S["gate_b_loaded"], 16 * 3 * LAYERS)
                b = B.take(v)
                step(tsc(rows[:, 0, :], b[0:MLH, 0:T], bif[:, l, 0:1], None, ALU.add))
                step(tsc(rows[:, 1, :], b[0:MLH, T:2 * T], bif[:, l, 1:2], None, ALU.add), B.free)
                step(tsc(rows[:, 2, :], rows[:, 1, :], -1.0, None, ALU.mult))
                step(tten(rows[:, 2, :], rows[:, 2, :], rows[:, 1, :], ALU.max), S["lf_wanted"])
                v.wait_ge(S["lf_ready"], l + 1)
                log1p(rows[:, 4, :], rows[:, 2, :], rows[:, 5, :], rows[:, 6, :])
                step(stt(rows[:, 1, :], rows[:, 1, :], 0.0, rows[:, 4, :], ALU.min, ALU.subtract))
                for c in range(TT):
                    cs = slice(c * P, (c + 1) * P)
                    step(v.tensor_tensor_scan(rows[:, 7, cs], onesr[:, :], rows[:, 1, cs], 0.0, ALU.mult, ALU.add))
                step(tten(rows[:, 3, :], rows[:, 0, :], rows[:, 7, :], ALU.subtract))
                for c in range(TT):
                    cs = slice(c * P, (c + 1) * P)
                    step(v.tensor_tensor_scan(rows[:, 4, cs], rows[:, 3, cs], rows[:, 3, cs],
                                              0.0 if c == 0 else rsc[:, 1:2], ALU.max, ALU.max))
                    if c == 0:
                        step(tten(rsc[:, 1:2], rows[:, 4, P - 1:P], rows[:, 7, P - 1:P], ALU.add))
                        step(tsc(rsc[:, 0:1], rows[:, 4, P - 1:P], -1.0, None, ALU.mult))
                step(tsc(rows[:, 5, :], rows[:, 4, :], -1.0, None, ALU.mult))
                step(tten(rows[:, 2, :], rows[:, 4, :], rows[:, 7, :], ALU.add), S["row_wanted"])
                v.wait_ge(A.free, A.upto(f"mo{l}31"))
                step(tsc(oth_t[:, :], oth_t[:, :], 1.0, None, ALU.add), S["oth_ready"])
                v.wait_ge(A.free, A.upto(f"mz{l}7"))
                step(stt(zm[:, :, :], mth[:, :, :], 1.0, zm[:, :, :], ALU.add, ALU.mult), S["z_used"])
                b = B.take(v)
                step(v.tensor_copy(cols[:, :, :], b[:, 0:16].rearrange("p (n h) -> p n h", n=4)), B.free)
                for h in range(MLH):
                    step(tsc(knat[:, h, :], knat[:, h, :], cols[:, 0, h:h + 1], None, ALU.mult), S["kw_ready"])
                for c in range(TT):
                    for h in range(MLH):
                        b = B.take(v)
                        v.wait_ge(A.free, A.upto(f"E{l}{c}{h}"))
                        step(stt(stb[:, h % 2, :], b[:, 0:P], MLD ** -0.5, ebuf[:, h % 2, :], ALU.mult, ALU.mult),
                             B.free)
                        b = B.take(v)
                        if c == 0:
                            step(v.tensor_copy(hn[:, :], b[:, 0:VW]), B.free)
                        else:
                            v.wait_ge(A.free, A.upto(f"in{l}{h}"))
                            step(tten(hn[:, :], b[:, 0:VW], inter[:, h % 2, :], ALU.add), B.free)
                        step(tsc(rt[:, 0:1], hn[:, MLD:VW], -1.0, None, ALU.mult))
                        step(tten(rt[:, 0:1], rt[:, 0:1], hn[:, MLD:VW], ALU.max))
                        step(tten(rt[:, 0:1], rt[:, 0:1], cols[:, 2 + c, h:h + 1], ALU.max))
                        step(v.reciprocal(rt[:, 1:2], rt[:, 0:1]))
                        step(stt(hh[:, c, h * MLD:(h + 1) * MLD], hn[:, 0:MLD], rt[:, 1:2],
                                 oth[:, c, h * MLD:(h + 1) * MLD], ALU.mult, ALU.mult), S["hh_ready"])
                roots_n["ssq"] += 8
                v.wait_ge(S["ssq_ready"], roots_n["ssq"])
                rstd(small[:, 24:32], small[:, 16:24], 0.25 / MLD)
                step(tsc(small[:, 24:32], small[:, 24:32], 0.25, None, ALU.mult))
                for c in range(TT):
                    for h in range(MLH):
                        hv = hh[:, c, h * MLD:(h + 1) * MLD]
                        n = 24 + c * MLH + h
                        ins = tsc(hv, hv, small[:, n:n + 1], None, ALU.mult)
                        step(ins, S["hq_ready"]) if (c, h) == (1, MLH - 1) else step(ins)
                for m in range(KB):
                    b = B.take(v)
                    step(stt(ymT[:, m, :], b[:, 0:T], colM[:, l, 8 + m:9 + m], zm[:, m, :], ALU.mult, ALU.mult), B.free)
                for j in range(4):
                    for tt in range(TT):
                        b = B.take(v)
                        step(tten(hn[:, 0:CW], b[:, 0:CW], gateB[:, j * CW:(j + 1) * CW], ALU.mult), B.free)
                        xs = x[:, tt, j * CW:(j + 1) * CW]
                        ins = tten(xs, xs, hn[:, 0:CW], ALU.add)
                        step(ins, S["layer_done"]) if (j, tt) == (3, 1) else step(ins)
            norm_x()
            v.wait_ge(S["gfin_loaded"], 32)
            for tt in range(TT):
                step(stt(xn[:, tt, :], x[:, tt, :], small[:, 2 + tt:3 + tt], gfin[:, :], ALU.mult, ALU.mult),
                     S["layer_done"])

        @block.gpsimd
        def _(g):
            step = Chain(g, s_pool)
            step(g.memset(ident[:, :], 0.0))
            step(g.affine_select(out=ident[:, :], in_=ident[:, :], compare_op=ALU.not_equal, fill=1.0, base=0,
                                 pattern=[[-1, P]], channel_multiplier=1))
            step(g.memset(anti[:, :], 0.0))
            step(g.affine_select(out=anti[:, :], in_=anti[:, :], compare_op=ALU.not_equal, fill=1.0 / SCALE,
                                 base=1 - P, pattern=[[1, P]], channel_multiplier=1))
            step(g.memset(later[:, :], 0.0))
            step(g.affine_select(out=later[:, :], in_=later[:, :], compare_op=ALU.is_ge, fill=-BIG, base=0,
                                 pattern=[[1, P]], channel_multiplier=-1))
            step(g.memset(ones[:, :], 1.0))
            step(g.memset(allone, 1.0))
            step(g.memset(upto, 1.0))
            step(g.affine_select(out=upto, in_=upto, compare_op=ALU.is_ge, fill=0.0, base=0, pattern=[[1, P]],
                                 channel_multiplier=-1))
            step(g.memset(onesr[:, :], 1.0))
            step(g.memset(sel4[:, :, :], 0.0))
            step(g.affine_select(out=sel4[:, :, :], in_=sel4[:, :, :], compare_op=ALU.not_equal, fill=1.0, base=0,
                                 pattern=[[-1, MLH], [0, P]], channel_multiplier=1))
            for k in range(EPG):
                step(g.memset(desc[:, k:k + 1], float(EPG - k)), S["const_ready"] if k == EPG - 1 else None)
            def vec(dst, name, src, s):
                g.dma_start(dst, src).then_inc(s, 16)
            s = S["rows_loaded"]
            r8 = lambda ap: ap.rearrange("(k p) -> k p", p=P)
            vec(rowsA[0:8, :], "g1", r8(a["norm1_g"][0]), s)
            vec(rowsA[8:16, :], "g2", r8(a["norm2_g"][0]), s)
            vec(rowsA[16:17, :], "gkv", a["kv_norm_g"], s)
            vec(rowsA[17:25, :], "c", r8(a["c_2"][0]), s)
            vec(rowsA[25:26, :], "pad", a["kv_norm_g"], s)
            g.dma_start(relw, a["rel_bias"]).then_inc(S["rel_loaded"], 16)
            g.dma_start(reltab, a["bucket_of_distance"]).then_inc(S["rel_loaded"], 16)
            s = S["rowsL_loaded"]
            for l in range(LAYERS):
                for row, src in ((V_NORM, r8(a["norm_g_2"][l])), (V_ADA, r8(a["b_ada_2"][l])),
                                 (V_RCW, a["rg_conv_w_2"][l].rearrange("j (k p) -> (j k) p", p=P)),
                                 (V_MCW, a["ml_conv_w_2"][l].rearrange("j (k p) -> (j k) p", p=P)),
                                 (V_RCB, r8(a["rg_conv_b_2"][l])), (V_BA, r8(a["rg_b_a_2"][l])),
                                 (V_BX, r8(a["rg_b_x_2"][l])), (V_LAM, r8(a["rg_lambda_2"][l]))):
                    vec(rowsL[row:row + src.shape[0], l, :], "", src, s)
                vec(rowsM[0:8, l, :], "", r8(a["ml_conv_b_2"][l]), s)
                vec(rowsM[8:16, l, :], "", r8(a["ml_norm_g_2"][l]), s)
            g.dma_start(norm2, bcast(a["norm2_g"][0], D)).then_inc(S["norm2_loaded"], 16)
            s = S["small_loaded"]
            NR = EG + EXPERTS
            g.dma_start(wi_w[:, :, :], cols_of(w_in, C_WI, 8)).then_inc(s, 16)
            g.dma_start(rt_w[:, :, 0:EG], cols_of(a["router_group_w"][0], 0, EG)).then_inc(s, 16)
            g.dma_start(rt_w[:, :, EG:NR], cols_of(a["router_expert_w"][0], 0, EXPERTS)).then_inc(s, 16)
            g.dma_start(rt_b[0:1, 0:EG], a["router_group_b"]).then_inc(s, 16)
            g.dma_start(rt_b[0:1, EG:NR], a["router_expert_b"]).then_inc(s, 16)
            g.dma_start(wuk, a["w_uk"][0].rearrange("r h d -> r (h d)")).then_inc(S["attn_loaded"], 16)
            g.dma_start(wuv, a["w_uv"][0].rearrange("r h d -> r (h d)")).then_inc(S["attn_loaded"], 16)
            g.dma_start(wsn, a["w_spatial"][0].rearrange("g i j -> i g j")).then_inc(S["relrow_ready"], 16)
            g.dma_start(lng, bcast(a["ln_v_g"][0], 512)) \
                .then_inc(S["ln_loaded"], 16)
            g.dma_start(lnb, bcast(a["ln_v_b"][0], 512)).then_inc(S["ln_loaded"], 16)
            g.dma_start(bsp[0:1, :], a["b_spatial"].rearrange("a g i -> a (g i)")).then_inc(S["ln_loaded"], 16)
            g.wait_ge(B.free, B.upto("relrow"))
            g.dma_start(relscr_ap, relrow).then_inc(S["relrow_stored"], 16)
            g.wait_ge(S["relrow_stored"], 16)
            g.dma_start(biasT, diag).then_inc(S["bias_loaded"], 16)
            g.wait_ge(S["relrow_ready"], 16)
            step(g.affine_select(out=wsn, in_=wsn, compare_op=ALU.is_ge, fill=0.0, base=0,
                                 pattern=[[0, GROUPS], [-1, P]], channel_multiplier=1), S["ws_masked"])
            for tt in range(TT):
                ns = (tt + 1) * P
                g.wait_ge(S["relu_used"], (tt + 1) * HEADS)
                step(g.affine_select(out=idx[:, tt, 0:ns], in_=idx[:, tt, 0:ns], compare_op=ALU.is_ge, fill=MASKED,
                                     base=tt * P, pattern=[[-1, ns]], channel_multiplier=1), S["idx_masked"])
            for tt in range(TT):
                ns = (tt + 1) * P
                g.wait_ge(S["sel_ready"], tt + 1)
                step(g.affine_select(out=maskb[:, tt, 0:ns], in_=maskb[:, tt, 0:ns], compare_op=ALU.is_ge, fill=-BIG,
                                     base=tt * P, pattern=[[-1, ns]], channel_multiplier=1), S["mask_ready"])
            for l in range(LAYERS):
                g.dma_start(wif[:, l, :, :], a["ml_w_if_2"][l].rearrange("(k p) g -> p k g", p=P)) \
                    .then_inc(S["gate_b_loaded"], 16)
                for k in range(2):
                    g.dma_start(bif[:, l, k:k + 1], a["ml_b_if_2"][l, k * MLH:(k + 1) * MLH].rearrange("(h o) -> h o", o=1)) \
                        .then_inc(S["gate_b_loaded"], 16)
            g.wait_ge(S["vln_ready"], 1)
            g.dma_start(gfin[:, :], bcast(a["final_norm_g"], D)).then_inc(S["gfin_loaded"], 16)
            g.wait_ge(S["rstd_used"], 1)
            step(g.memset(rxp[:, :], 0.0))
            step(g.memset(mxp[:, :], 0.0))
            step(g.memset(vaug_t[:, :], 1.0), S["pads_ready"])
            for l in range(LAYERS):
                if l:
                    g.wait_ge(S["layer_done"], l)
                g.dma_start(adab[0:1, :], a["b_ada_2"][l:l + 1, 2 * D:3 * D]).then_inc(S["adab_loaded"], 16)
            g.wait_ge(S["layer_done"], LAYERS)
            g.dma_start(gfin[:, :], bcast(a["final_g_2"], D)).then_inc(S["gfin_loaded"], 16)


def bucket_of_distance():
    n = np.maximum(T - 1 - np.arange(512), 0)
    exact = BUCKETS // 2
    nf = np.maximum(n, 1).astype(np.float32)
    large = exact + (np.log(nf / np.float32(exact)) / np.float32(np.log(128 / exact))
                     * np.float32(BUCKETS - exact)).astype(np.int32)
    bucket = np.where(n < exact, n, np.minimum(large, BUCKETS - 1))
    return (np.arange(BUCKETS)[:, None] == bucket[None, :]).astype(np.float32)


def kernel(**inputs):
    import concourse.bacc as bacc
    from concourse.bass_utils import run_bass_kernel_spmd

    nc = bacc.Bacc("TRN2", target_bir_lowering=False, num_devices=1)
    arrays, args = {}, {}
    for name, value in list(inputs.items()) + [("bucket_of_distance", bucket_of_distance())]:
        value = np.ascontiguousarray(value)
        arrays[f"in_{name}"] = value
        args[name] = nc.dram_tensor(f"in_{name}", value.shape, mybir.dt.from_np(value.dtype), kind="ExternalInput").ap()
    out = nc.dram_tensor("out", (1, T, D), F32, kind="ExternalOutput").ap()
    build(nc, args, out)
    result = run_bass_kernel_spmd(nc, [arrays], core_ids=[0])
    return result.results[0]["out"]
```

```python
from contextlib import ExitStack

import numpy as np
import concourse.bass as bass
from concourse import mybir

F32 = mybir.dt.float32
ALU = mybir.AluOpType
ACT = mybir.ActivationFunctionType
AX = mybir.AxisListType

P = 128
T = 256
TT = T // P
D = 1024
KB = D // P
HEADS, HD = 8, 64
RANK = 128
TOPK = min(256, T // 4)
BUCKETS = 32
GROUPS, GDIM = 4, 128
EG, EPG = 4, 8
EXPERTS = EG * EPG
FF = 256
EPS = 1e-6
LAYERS = 2
MLH, MLD = 4, 256
TAPS = 4
PAD = TAPS - 1
XW = T + 4
VW = MLD + 1
CW = 256
RING = 6
SLOTS = 64
PAIRS = EXPERTS // 2
BIG = 1e30
MASKED, TAKEN = -1e38, -3e38
SCALE = HD ** -0.5
IDX_SCALE = (8 ** -0.5) * (64 ** -0.5)
C_Q, C_CKV, C_QI, C_KI, C_WI, C_U, C_V, C_GA, C_GB = 0, 512, 640, 1152, 1216, 1224, 1736, 2248, 3272
V_NORM, V_ADA, V_RCW, V_MCW, V_RCB, V_BA, V_BX, V_LAM = 0, 8, 32, 64, 96, 104, 112, 120
OUT_ORDER = ((0, 0), (0, 1), (1, 0), (1, 1), (0, 2), (1, 2), (0, 3), (1, 3))
MIX_BANKS = (7, 4, 0, 1)
ADA_CHUNKS = LAYERS * 3 * D // CW
ADA_LAG = 2
ADA_POOL = 17
LOG1P = [1.0 / k for k in (17, 15, 13, 11, 9, 7, 5, 3)]


class Banks:

    def __init__(self, banks, done, free):
        self.banks, self.done, self.free = banks, done, free
        self.put, self.got, self.names = 0, 0, {}

    def acquire(self, pe, name=None):
        n = self.put
        self.put += 1
        self.names[name] = n + 1
        if n >= len(self.banks):
            pe.wait_ge(self.free, n + 1 - len(self.banks))
        return self.banks[n % len(self.banks)]

    def take(self, eng):
        n = self.got
        self.got += 1
        eng.wait_ge(self.done, n + 1)
        return self.banks[n % len(self.banks)]

    def upto(self, name):
        return self.names[name]

    def bank(self, n):
        return self.banks[(n - 1) % len(self.banks)]


class Chain:

    def __init__(self, eng, sem):
        self.eng, self.sem, self.count = eng, sem, {}

    def skip(self, sem, n):
        self.count[sem.name] = self.count.get(sem.name, 0) + n

    def __call__(self, ins, sem=None):
        sem = sem or self.sem
        n = self.count.get(sem.name, 0) + 1
        self.count[sem.name] = n
        ins.then_inc(sem, 1)
        self.eng.wait_ge(sem, n)


def build(nc, a, out):
    with ExitStack() as ctx:
        def sb(name, shape):
            return ctx.enter_context(nc.sbuf_tensor(name, shape, F32))

        def sem(name):
            return ctx.enter_context(nc.semaphore(name))

        psum = [ctx.enter_context(nc.psum_tensor(f"bank{i}", [P, 512], F32)) for i in range(8)]

        ring = [sb(f"ring{i}", [P, KB * CW]) for i in range(RING)]
        x = sb("x", [P, TT, D])
        hT = sb("hT", [P, KB, T])
        tmp = sb("tmp", [P, 2048])
        rxp = sb("rxp", [P, KB * XW])
        mxp = sb("mxp", [P, KB * XW])
        s0, s1, s2, s3, s4 = (sb(f"s{i}", [P, MLH * 2 * VW]) for i in range(5))
        z0, z1, s5, s6, s7 = (sb(n, [P, 2048]) for n in ("z0", "z1", "s5", "s6", "s7"))
        vaug_t = sb("vaug", [P, TT * MLH * VW])
        w4 = sb("w4", [P, 1024])
        gateB = sb("gateB", [P, D])
        oth_t = sb("oth", [P, 2048])
        ident = sb("ident", [P, P])
        anti = sb("anti", [P, P])
        later = sb("later", [P, P])
        ones = sb("ones", [1, P])
        onesr = sb("onesr", [MLH, P])
        sel4 = sb("sel4", [MLH, MLH, P])
        rowsA = sb("rowsA", [32, P])
        colA = sb("colA", [P, 32])
        rowsL = sb("rowsL", [P, LAYERS, P])
        rowsM = sb("rowsM", [16, LAYERS, P])
        colL = sb("colL", [P, LAYERS, P])
        colM = sb("colM", [P, LAYERS, 16])
        small = sb("small", [P, 64])
        rt_b = sb("rt_b", [1, EG + EXPERTS])
        wif = sb("wif", [P, LAYERS, 24, 8])
        bif = sb("bif", [MLH, LAYERS, 2])
        csil = sb("csil", [P, KB])
        adac = sb("adac", [P, LAYERS, 3 * KB])
        allone = sb("allone", [P, P])
        gs = sb("gs", [P, KB])
        n4 = sb("n4", [P, 2, KB])
        lam = sb("lam", [P, 5, LAYERS, KB])
        hb = sb("hb", [P, LAYERS, 2 * KB])
        rsc = sb("rsc", [MLH, 4])
        cols = sb("cols", [P, 4, MLH])
        logit = sb("logit", [P, TT, EG + EXPERTS])
        comb = sb("comb", [P, TT, EXPERTS])
        rt = sb("rt", [P, 128])
        desc = sb("desc", [P, EPG])
        m8 = sb("m8", [P, 8])
        most = ctx.enter_context(nc.sbuf_tensor("most", [P, 1], mybir.dt.int32))

        lneg, labs, lsp, ly, lt = (lam[:, i, :, :] for i in range(5))
        squares = s6[:, :].rearrange("p (t d) -> p t d", t=TT)

        xn = tmp[:, :].rearrange("p (t d) -> p t d", t=TT)
        qT = s0[:, 0:1024].rearrange("p (b t) -> p b t", b=4)
        qiT = s0[:, 1024:2048].rearrange("p (b t) -> p b t", b=4)
        kvT = s1[:, 0:1024].rearrange("p (b t) -> p b t", b=4)
        vnat = s1[:, 1024:2048].rearrange("p (s c) -> p s c", s=TT)
        biasT = s2[:, 0:2048].rearrange("p (h j) -> p h j", h=HEADS)
        idx = s3[:, 0:512].rearrange("p (t s) -> p t s", t=TT)
        maskb = s3[:, 512:1024].rearrange("p (t s) -> p t s", t=TT)
        relu = s3[:, 1024:1536].rearrange("p (b s) -> p b s", b=2)
        sc = s3[:, 1536:2048].rearrange("p (t s) -> p t s", t=TT)
        prob = [[tmp[:, 384 * i:384 * i + P], tmp[:, 384 * i + P:384 * i + 3 * P]] for i in range(2)]
        pT = s4[:, 0:768].rearrange("p (b s q) -> p b s q", b=2, s=3)
        kiT = s4[:, 768:1024]
        cT = s4[:, 1024:1280]
        ckv = s4[:, 1280:1536].rearrange("p (t r) -> p t r", t=TT)
        wi = s4[:, 1536:1552].rearrange("p (t h) -> p t h", t=TT)
        vst = s4[:, 1552:1568]
        tga = z0[:, :].rearrange("p (b t) -> p b t", b=KB)
        tgb = z1[:, :].rearrange("p (b t) -> p b t", b=KB)
        guT = s5[:, 0:1024].rearrange("p (b t) -> p b t", b=GROUPS)
        gv = s5[:, 1024:2048].rearrange("p (t c) -> p t c", t=TT)
        gmT = s6[:, 0:1024].rearrange("p (b t) -> p b t", b=GROUPS)
        oaT = s6[:, 1024:2048].rearrange("p (b t) -> p b t", b=4)
        mgT = s7[:, :].rearrange("p (b t) -> p b t", b=KB)
        mtmp = vaug_t[:, 0:512].rearrange("p (b t) -> p b t", b=2)
        reltab = vaug_t[0:BUCKETS, 512:1024]
        relw = vaug_t[0:BUCKETS, 1024:1032]
        relrow = vaug_t[0:HEADS, 1032:1544]
        wuk = w4[:, 0:512]
        wuv = w4[:, 512:1024]
        lng = gateB[:, 0:512]
        lnb = gateB[:, 512:1024]
        wsn = oth_t[:, 0:512].rearrange("p (g j) -> p g j", g=GROUPS)
        wsT = oth_t[:, 512:1024].rearrange("p (g j) -> p g j", g=GROUPS)
        bsp = rxp[0:1, 0:512]
        wi_w = mxp[:, 0:64].rearrange("p (k n) -> p k n", k=KB)
        rt_w = mxp[:, 64:64 + KB * (EG + EXPERTS)].rearrange("p (k n) -> p k n", k=KB)
        heT = s5[:, 0:1024].rearrange("p (e b t) -> p e b t", e=2, b=2)
        thg = s5[:, 1024:2048].rearrange("p (e n) -> p e n", e=2)
        sg = s6[:, 0:512]
        xg = xn
        hgT = z0[:, 0:KB * P].rearrange("p (b s) -> p b s", b=KB)
        he = s5[:, 0:FF]
        heTs = s5[:, FF:2 * FF].rearrange("p (b s) -> p b s", b=2)
        thgs = s5[:, 2 * FF:3 * FF]
        ye = z1[:, 0:D]
        combT = s7[:, 0:512].rearrange("p (q t) -> p q t", q=2)
        pick = mxp[:, 512:1024].rearrange("p (q t s) -> p q t s", q=2, t=TT)
        pickw = mxp[:, 1024:1536].rearrange("p (q t s) -> p q t s", q=2, t=TT)
        slotno = mxp[:, 1536:1536 + SLOTS]
        upto = rxp[:, 512:512 + P]
        adasum = rxp[:, 896:896 + 3 * CW].rearrange("p (q c) -> p q c", q=3)
        key = rxp[:, 768:768 + TT * EXPERTS].rearrange("p (t e) -> p t e", t=TT)
        member = rxp[:, 832:832 + TT * EXPERTS].rearrange("p (t e) -> p t e", t=TT)
        norm2 = oth_t[:, 1024:2048]
        gfin = gateB
        rxv = rxp[:, :].rearrange("p (b t) -> p b t", b=KB)
        mxv = mxp[:, :].rearrange("p (b t) -> p b t", b=KB)

        def v8(s):
            return s[:, 0:2048].rearrange("p (b t) -> p b t", b=KB)
        rxc, thr, thi, aa, tl = v8(s0), v8(s1), v8(s2), v8(s3), v8(s4)
        zr, zm = v8(z0), v8(z1)
        mc, mqT, mkT = v8(s5), v8(s6), v8(s7)
        mth = v8(tmp)
        mvT = v8(s3)
        rows = s2[0:MLH, 0:8 * T].rearrange("p (r t) -> p r t", r=8)
        gdiag = z0[:, 0:KB * P].rearrange("p (k n) -> p k n", k=KB)
        gated = tmp[:, 256:768].rearrange("p (t c) -> p t c", t=TT)
        zth = (tmp[:, 0:T], tmp[:, 1546:1546 + T])
        ebuf = tmp[:, 256:512].rearrange("p (b t) -> p b t", b=2)
        stb = tmp[:, 512:768].rearrange("p (b t) -> p b t", b=2)
        hn = tmp[:, 768:768 + VW]
        inter = tmp[:, 1032:1032 + 2 * VW].rearrange("p (b c) -> p b c", b=2)
        vaug = vaug_t[:, :].rearrange("p (t h c) -> p t h c", t=TT, h=MLH)
        knat = w4[:, :].rearrange("p (h c) -> p h c", h=MLH)
        caug = s0[:, :].rearrange("p (h k c) -> p h k c", h=MLH, k=2)
        oth = oth_t[:, :].rearrange("p (t c) -> p t c", t=TT)
        hh = s3[:, 0:2048].rearrange("p (t c) -> p t c", t=TT)
        ymT = v8(s4)

        relscr = nc.dram_tensor("rel_scratch", (HEADS, 512), F32)
        relscr_ap = relscr.ap() if hasattr(relscr, "ap") else relscr

        diag = bass.AP(relscr_ap.tensor, 0, [[1, P], [512, HEADS], [1, T]])

        def bcast(ap, n):
            return bass.AP(ap.tensor, ap.offset, [[0, P], [1, n]])

        def r8(ap):
            return ap.rearrange("(k p) -> k p", p=P)

        A = Banks(psum[0:4], sem("a_done"), sem("a_free"))
        B = Banks(psum[4:8], sem("b_done"), sem("b_free"))
        slot_full = [sem(f"slot_full{i}") for i in range(RING)]
        chunk_used = sem("chunk_used")
        s_act, s_dve, s_pool = sem("act_step"), sem("dve_step"), sem("pool_step")
        S = {n: sem(n) for n in (
            "x_loaded", "rows_loaded", "small_loaded", "attn_loaded", "rel_loaded", "const_ready", "rowsL_loaded",
            "ssq_ready", "root_wanted", "root_ready", "xn_ready", "relrow_stored", "bias_loaded",
            "relu_used", "idx_masked", "sel_ready", "mask_ready", "sc_ready", "p_ready",
            "prob_ready", "ws_masked", "vln_ready", "mg_ready", "cbc_ready", "csil_ready", "gate_b_loaded",
            "exp_wanted", "exp_ready", "tanh_gate", "silu_ready", "he_ready", "gu_done",
            "gate_done", "down_done", "down_out", "gfin_loaded", "x_stored", "mod_ready", "conv_ready", "rg_gate", "rg_root_wanted",
            "rg_root", "mconv_ready", "mtanh_ready", "mc_ready", "pads_ready", "lf_wanted", "lf_ready",
            "row_wanted", "row_ready", "kw_ready", "hh_ready", "hq_ready",
            "layer_done", "tile0_done", "sp_wanted", "sp_ready", "csil_tanh", "ln_loaded",
            "norm2_loaded", "routed", "most_ready", "slots_ready", "gather_done", "gather_ready", "combT_done",
            "combT_ready", "ye_ready", "mixed", "heT_done", "heT_ready", "down_half",
            "rg_done", "ckv_ready", "xg_ready", "ada_summed", "ada_summed_v", "zm_ready", "ident_ready", "ws_loaded")}

        def cols_of(w, c, n=CW):
            return w[:, c:c + n].rearrange("(k p) c -> p k c", p=P)

        w_in = a["w_in"][0]
        chunks = []
        def add(*parts):
            chunks.append(parts)
        full = lambda t: t[:, :].rearrange("p (k c) -> p k c", k=KB)
        def colpart(lo, n):
            return lambda t: full(t)[:, :, lo:lo + n]
        add((colpart(0, 128), cols_of(w_in, C_CKV, 128)), (colpart(128, 64), cols_of(w_in, C_KI, 64)),
            (colpart(192, 64), cols_of(w_in, C_KI, 64)))
        ada_chunks = []
        ada_left = [(l, j) for l in range(LAYERS) for j in range(3 * D // CW)]

        def add_ada(n=1):
            for _ in range(n):
                l, j = ada_left.pop(0)
                ada_chunks.append(len(chunks))
                add((full, cols_of(a["w_ada_2"][l], j * CW)))

        for c in (C_Q, C_QI, C_U, C_V):
            for j in range(2):
                add((full, cols_of(w_in, c + j * CW)))
                add_ada()
        for c in (C_GA, C_GB):
            for j in range(4):
                add((full, cols_of(w_in, c + j * CW)))
                add_ada()
        for j in range(4):
            add((lambda t: full(t)[:, 0:4, :], cols_of(a["w_proj_a"][0], j * CW)),
                (lambda t: full(t)[:, 4:8, :], cols_of(a["w_proj_b"][0], j * CW)))
            add_ada()
        for j in range(4):
            add((full, cols_of(a["w_out"][0], j * CW)))
            if j < 3:
                add_ada(2 if j == 2 else 1)
        assert not ada_left
        first_expert_chunk = len(chunks)
        NB1 = first_expert_chunk
        tail = []
        def addt(*parts):
            tail.append(parts)
        for l in range(LAYERS):
            wi2 = a["w_in_2"][l]
            for j in range(4):
                addt((full, cols_of(wi2, j * CW)))
            addt((colpart(0, 128), a["rg_w_a_2"][l].rearrange("h d e -> d h e")),
                 (colpart(128, 128), a["rg_w_x_2"][l].rearrange("h d e -> d h e")))
            for c in (D, 2 * D):
                for j in range(4):
                    addt((full, cols_of(wi2, c + j * CW)))
            for j in range(2):
                addt((full, cols_of(wi2, 3 * D + j * CW)))
            for n in ("ml_w_q_2", "ml_w_k_2", "ml_w_v_2"):
                addt((full, a[n][l].rearrange("h (k p) e -> p (h k) e", p=P)))
            for j in range(2, 4):
                addt((full, cols_of(wi2, 3 * D + j * CW)))
            for j in range(4):
                addt((full, cols_of(wi2, 4 * D + j * CW)))
            for kh, j in OUT_ORDER:
                addt((full, cols_of(a["w_out_2"][l][kh * D:(kh + 1) * D, :], j * CW)))
        E0 = NB1
        L0 = NB1 + 3 * EXPERTS

        block = ctx.enter_context(nc.Block())

        nparts = [len(c) for c in chunks] + [1] * (3 * EXPERTS) + [len(c) for c in tail]
        fill_value, filled = [], [0] * RING
        for n, k in enumerate(nparts):
            filled[n % RING] += 16 * k
            fill_value.append(filled[n % RING])

        def ada_done(n):
            return (S["ada_summed"], n + 1) if n < ADA_POOL else (S["ada_summed_v"], n + 1 - ADA_POOL)

        chunk_free = []

        @block.tensor
        def _(pe):
            state = {"n": 0, "free": 0, "ada": 0}

            def chunk(k=None):
                n = state["n"]
                state["n"] += 1
                pe.wait_ge(slot_full[n % RING], fill_value[n])
                return ring[n % RING]

            def tr(dst, src, k=P):
                return pe.transpose(dst, src, ident[0:k, 0:k])

            def transpose_x(ready, tag):
                pe.wait_ge(S["xn_ready"], ready)
                for kb in range(KB):
                    b = B.acquire(pe, f"hT{tag}{kb}")
                    for tt in range(TT):
                        m = tr(b[:, tt * P:(tt + 1) * P], xn[:, tt, kb * P:(kb + 1) * P])
                    m.then_inc(B.done, 1)

            def projT(w, m, rhs, pool, name=None, nk=KB, k0=0, tag=None):
                b = pool.acquire(pe, name)
                for kb in range(nk):
                    if tag:
                        pe.wait_ge(B.free, B.upto(f"hT{tag}{kb}"))
                    mm = pe.matmul(b[:, 0:T], w[:, (k0 + kb) * CW + m * P:(k0 + kb) * CW + (m + 1) * P], rhs[:, kb, :],
                                   start=(kb == 0), stop=(kb == nk - 1))
                mm.then_inc(pool.done, 1)
                return mm

            def used(pool=A, mm=None):
                if mm is None:
                    chunk_free.append((pool.done, pool.put))
                else:
                    state["free"] += 1
                    mm.then_inc(chunk_used, 1)
                    chunk_free.append((chunk_used, state["free"]))

            def ada_job():
                n = state["ada"]
                state["ada"] += 1
                if n < ADA_CHUNKS:
                    state["n"] += 1
                    chunk_free.append(ada_done(n))
                if n >= ADA_LAG:
                    n -= ADA_LAG
                    pe.wait_ge(*ada_done(n))
                    b = A.acquire(pe, f"ada{n}")
                    for m in range(2):
                        mm = pe.matmul(b[:, m:m + 1], adasum[:, n % 3, m * P:(m + 1) * P], allone[:, 0:1],
                                       start=True, stop=True)
                    mm.then_inc(A.done, 1)

            pe.wait_ge(S["ident_ready"], 1)
            pe.wait_ge(S["rows_loaded"], 16 * 4)
            b = B.acquire(pe, "colA")
            tr(b[:, 0:25], rowsA[0:25, :], 25).then_inc(B.done, 1)
            transpose_x(1, "A")
            w = chunk()
            wv = full(w)
            for tt in range(TT):
                b = A.acquire(pe, f"ckv{tt}")
                for kb in range(KB):
                    if tt == 0:
                        pe.wait_ge(B.free, B.upto(f"hTA{kb}"))
                    mm = pe.matmul(b[:, 0:RANK], hT[:, kb, tt * P:(tt + 1) * P], wv[:, kb, 0:RANK],
                                   start=(kb == 0), stop=(kb == KB - 1))
                mm.then_inc(A.done, 1)
            projT(w, 1, hT, A, "kiT")
            used()
            pe.wait_ge(S["small_loaded"], 16 * 5)
            b = A.acquire(pe, "wi")
            for tt in range(TT):
                for kb in range(KB):
                    mm = pe.matmul(b[:, tt * 8:tt * 8 + 8], hT[:, kb, tt * P:(tt + 1) * P], wi_w[:, kb, :],
                                   start=(kb == 0), stop=(kb == KB - 1))
            mm.then_inc(A.done, 1)
            pe.wait_ge(S["rowsL_loaded"], 16 * 20)
            for l in range(LAYERS):
                b = B.acquire(pe, f"colL{l}")
                tr(b[:, 0:P], rowsL[:, l, :])
                tr(b[:, P:P + 16], rowsM[:, l, :], 16).then_inc(B.done, 1)
            pe.wait_ge(S["rel_loaded"], 32)
            b = B.acquire(pe, "relrow")
            pe.matmul(b[0:HEADS, :], relw, reltab, start=True, stop=True).then_inc(B.done, 1)
            pe.wait_ge(S["const_ready"], 1)
            for name in ("q", "qi"):
                for j in range(2):
                    w = chunk()
                    for m in range(2):
                        projT(w, m, hT, A, f"{name}{2 * j + m}")
                    used()
                    ada_job()
            pe.wait_ge(A.free, A.upto("qi3"))
            for tt in range(TT):
                ns = (tt + 1) * P
                for h in range(HEADS):
                    o = (h % 2) * 64
                    b = A.acquire(pe, f"idx{tt}{h}")
                    pe.matmul(b[:, 0:ns], qiT[o:o + 64, h // 2, tt * P:(tt + 1) * P], kiT[o:o + 64, 0:ns],
                              start=True, stop=True).then_inc(A.done, 1)
            pe.wait_ge(S["ckv_ready"], 1)
            b = B.acquire(pe, "cT")
            for tt in range(TT):
                mm = tr(b[:, tt * P:(tt + 1) * P], ckv[:, tt, :])
            mm.then_inc(B.done, 1)
            pe.wait_ge(B.free, B.upto("cT"))
            pe.wait_ge(S["attn_loaded"], 32)
            for m in range(4):
                b = A.acquire(pe, f"K{m}")
                pe.matmul(b[:, 0:T], wuk[:, m * P:(m + 1) * P], cT, start=True, stop=True).then_inc(A.done, 1)
            for tt in range(TT):
                b = A.acquire(pe, f"V{tt}")
                pe.matmul(b[:, :], cT[:, tt * P:(tt + 1) * P], wuv, start=True, stop=True).then_inc(A.done, 1)
            for j in range(2):
                w = chunk()
                for m in range(2):
                    projT(w, m, hT, A, f"u{2 * j + m}")
                used()
                ada_job()
            for j in range(2):
                w = full(chunk())
                for tt in range(TT):
                    b = A.acquire(pe, f"v{j}{tt}")
                    for kb in range(KB):
                        mm = pe.matmul(b[:, 0:CW], hT[:, kb, tt * P:(tt + 1) * P], w[:, kb, :],
                                       start=(kb == 0), stop=(kb == KB - 1))
                    mm.then_inc(A.done, 1)
                used()
                ada_job()
            pe.wait_ge(S["ws_masked"], 1)
            b = A.acquire(pe, "wsT")
            for g in range(GROUPS):
                mm = tr(b[:, g * P:(g + 1) * P], wsn[:, g, :])
            mm.then_inc(A.done, 1)

            gate_jobs = [(j, m) for j in range(8) for m in range(2)]
            gst = {}

            def gate_job():
                if not gate_jobs:
                    return
                j, m = gate_jobs.pop(0)
                if m == 0:
                    gst["w"] = chunk()
                projT(gst["w"], m, hT, A, f"g{2 * j + m}")
                if m == 1:
                    used()
                    ada_job()

            for h in range(HEADS + 1):
                gate_job()
                if h < HEADS:
                    o = (h % 2) * 64
                    for tt in range(TT):
                        ns = (tt + 1) * P
                        b = B.acquire(pe, f"S{h}{tt}")
                        if (h, tt) == (0, 0):
                            pe.wait_ge(S["bias_loaded"], 16)
                        pe.matmul(b[:, 0:ns], anti[:, :], biasT[:, h, T - ns:T], start=True, stop=False)
                        pe.matmul(b[:, 0:ns], qT[o:o + 64, h // 2, tt * P:(tt + 1) * P], kvT[o:o + 64, h // 2, 0:ns],
                                  start=False, stop=True).then_inc(B.done, 1)
                gate_job()
                if h >= 1:
                    g = h - 1
                    o = (g % 2) * 64
                    pe.wait_ge(S["prob_ready"], 2 * g + 2)
                    b = A.acquire(pe, f"pT{g}")
                    pn = prob[g % 2]
                    tr(b[:, 0:P], pn[0][:, 0:P])
                    tr(b[:, P:2 * P], pn[1][:, 0:P])
                    tr(b[:, 2 * P:3 * P], pn[1][:, P:2 * P]).then_inc(A.done, 1)
                    pe.wait_ge(A.free, A.upto(f"pT{g}"))
                    b = A.acquire(pe, f"o{g}")
                    pe.matmul(b[o:o + 64, 0:P], vnat[:, 0, g * HD:(g + 1) * HD], pT[:, g % 2, 0, :],
                              start=True, stop=True)
                    for st in range(2):
                        mm = pe.matmul(b[o:o + 64, P:2 * P], vnat[:, st, g * HD:(g + 1) * HD], pT[:, g % 2, 1 + st, :],
                                       start=(st == 0), stop=(st == 1))
                    mm.then_inc(A.done, 1)
            assert not gate_jobs
            pe.wait_ge(S["vln_ready"], 1)
            pe.wait_ge(S["ln_loaded"], 48)
            pe.wait_ge(A.free, A.upto("wsT"))
            for g in range(GROUPS):
                b = B.acquire(pe, f"gm{g}")
                for c in range(TT):
                    pe.matmul(b[:, c * P:(c + 1) * P], ones[0:1, :], bsp[0:1, g * P:(g + 1) * P], start=True, stop=False)
                    mm = pe.matmul(b[:, c * P:(c + 1) * P], gv[:, c, g * P:(g + 1) * P], wsT[:, g, :],
                                   start=False, stop=True)
                mm.then_inc(B.done, 1)
            pe.wait_ge(B.free, B.upto("gm3"))
            pe.wait_ge(A.free, A.upto("o7"))
            for j in range(4):
                w = chunk()
                for m in range(2):
                    projT(w, m, oaT, B, f"ya{2 * j + m}", 4, 0)
                    projT(w, m, gmT, B, f"yb{2 * j + m}", 4, 4)
                used(B)
                ada_job()
            pe.wait_ge(S["mg_ready"], KB)
            for j in range(4):
                w = full(chunk())
                for tt in range(TT):
                    b = B.acquire(pe, f"xo{j}{tt}")
                    for kb in range(KB):
                        mm = pe.matmul(b[:, 0:CW], mgT[:, kb, tt * P:(tt + 1) * P], w[:, kb, :],
                                       start=(kb == 0), stop=(kb == KB - 1))
                    mm.then_inc(B.done, 1)
                used(B)
                for _ in range((1, 1, 2, 0)[j]):
                    ada_job()

            transpose_x(2, "B")
            b = B.acquire(pe, "router")
            NR = EG + EXPERTS
            for tt in range(TT):
                for kb in range(KB):
                    if tt == 0:
                        pe.wait_ge(B.free, B.upto(f"hTB{kb}"))
                    pe.matmul(b[:, tt * NR:(tt + 1) * NR], hT[:, kb, tt * P:(tt + 1) * P], rt_w[:, kb, :],
                              start=(kb == 0), stop=False)
                mm = pe.matmul(b[:, tt * NR:(tt + 1) * NR], ones[0:1, :], rt_b[0:1, :], start=False, stop=True)
            mm.then_inc(B.done, 1)
            for _ in range(ADA_LAG):
                ada_job()
            pe.wait_ge(S["routed"], 1)
            b = B.acquire(pe, "rank")
            pe.matmul(b[:, 0:EXPERTS], upto, member[:, 0, :], start=True, stop=True)
            pe.matmul(b[:, EXPERTS:2 * EXPERTS], upto, member[:, 1, :], start=True, stop=False)
            pe.matmul(b[:, EXPERTS:2 * EXPERTS], allone[:, :], member[:, 0, :], start=False, stop=True)
            for tt in range(TT):
                pe.matmul(b[:, 2 * EXPERTS:3 * EXPERTS], allone[:, :], member[:, tt, :], start=(tt == 0), stop=(tt == 1))
            pe.matmul(b[:, 3 * EXPERTS:3 * EXPERTS + SLOTS], allone[:, :], upto[:, 0:SLOTS], start=True, stop=True) \
                .then_inc(B.done, 1)
            pe.wait_ge(A.free, A.put)
            pe.wait_ge(S["most_ready"], 1)
            fullest = pe.value_load(most[0:1, 0:1], min_val=0, max_val=T)

            assert RING == 6

            def of_pair(p, k):
                n0 = E0 + k
                return n0 % RING, p * 16 + fill_value[n0]

            def loaded(w):
                pe.wait_ge(slot_full[w[0]], w[1])
                return ring[w[0]]

            def gather(p, q, first=False):
                pe.wait_ge(S["slots_ready"], p * 8 + 8)
                for hf in range(2):
                    if not isinstance(p, int) or p >= 2:
                        pe.wait_ge(S["down_out"], p * 8 + (2 * hf - 10))
                    for kb in range(4):
                        for tt in range(TT):
                            c = (4 * hf + kb) * P
                            mm = pe.matmul(psum[hf][:, kb * P:(kb + 1) * P], xg[:, tt, c:c + P], pick[:, q, tt, :],
                                           start=(tt == 0), stop=(tt == TT - 1))
                    mm.then_inc(S["gather_done"], 1)
                if not first:
                    pe.wait_ge(S["combT_ready"], p)
                for tt in range(TT):
                    mm = tr(psum[2][:, tt * P:(tt + 1) * P], pickw[:, q, tt, :])
                mm.then_inc(S["combT_done"], 1)

            def gate_up_own(p):
                pe.wait_ge(S["gather_ready"], p * 2 + 2)
                for c, done in ((0, S["gate_done"]), (1, S["gu_done"])):
                    wt = [full(loaded(of_pair(p, 2 * c + par))) for par in range(2)]
                    for kb in range(KB):
                        for par in range(2):
                            half = slice(par * SLOTS, (par + 1) * SLOTS)
                            mm = pe.matmul(psum[3][half, c * FF:(c + 1) * FF], hgT[:, kb, half], wt[par][:, kb, :],
                                           start=(kb == 0), stop=(kb == KB - 1))
                            if kb == KB - 1:
                                mm.then_inc(done, 1)

            def down_own(p):
                pe.wait_ge(S["heT_ready"], p + 1)
                wt = [loaded(of_pair(p, 4 + par))[:, :].rearrange("p (k c) -> p k c", k=2) for par in range(2)]
                for hf in range(2):
                    for k in range(2):
                        for par in range(2):
                            half = slice(par * SLOTS, (par + 1) * SLOTS)
                            mm = pe.matmul(psum[5 + hf][half, :], heTs[:, k, half],
                                           wt[par][:, k, hf * 512:(hf + 1) * 512], start=(k == 0), stop=(k == 1))
                            if (hf, k) == (1, 1):
                                mm.then_inc(S["down_done"], 4)
                            elif (k, par) == (1, 1):
                                mm.then_inc(S["down_half"], 1)

            def turn(p):
                pe.wait_ge(S["he_ready"], p + 1)
                for k in range(2):
                    mm = tr(psum[3][:, k * P:(k + 1) * P], he[:, k * P:(k + 1) * P])
                mm.then_inc(S["heT_done"], 1)

            def mix(p, q):
                pe.wait_ge(S["ye_ready"], p * 2 + 2)
                pe.wait_ge(S["combT_ready"], p + 1)
                for r in range(4):
                    if not isinstance(p, int) or p >= 1:
                        pe.wait_ge(S["down_out"], p * 8 + (2 * r - 6))
                    pe.matmul(psum[MIX_BANKS[r]][:, :], combT[:, q, (r // 2) * P:(r // 2 + 1) * P],
                              ye[:, (r % 2) * 512:(r % 2 + 1) * 512], start=True, stop=True) \
                        .then_inc(S["mixed"], 1)

            def pair(p, q):
                gate_up_own(p)
                if not isinstance(p, int) or p >= 1:
                    mix(p - 1, 1 - q)
                turn(p)
                if not isinstance(p, int) or p + 1 < PAIRS:
                    gather(p + 1, 1 - q)
                down_own(p)

            def pair_all(p):
                for k, done in ((0, S["gate_done"]), (1, S["gu_done"])):
                    for par in range(2):
                        if not isinstance(p, int) or p >= 1:
                            pe.wait_ge(S["he_ready"], p * 2 + (par - 1))
                        wt = loaded(of_pair(p, 2 * k + par))
                        for m in range(2):
                            for kb in range(KB):
                                mm = pe.matmul(psum[2 * k + par][:, m * T:(m + 1) * T],
                                               wt[:, kb * CW + m * P:kb * CW + (m + 1) * P],
                                               hT[:, kb, :], start=(kb == 0), stop=(kb == KB - 1))
                        mm.then_inc(done, 1)
                for par in range(2):
                    pe.wait_ge(S["he_ready"], p * 2 + (par + 1))
                    if par == 1 or not isinstance(p, int) or p >= 1:
                        pe.wait_ge(S["down_out"], p * 8 + 4 * par)
                    wt = loaded(of_pair(p, 4 + par))[:, :].rearrange("p (k c) -> p k c", k=2)
                    for tt in range(TT):
                        for hf in range(2):
                            for k in range(2):
                                mm = pe.matmul(psum[4 + 2 * tt + hf][:, :], heT[:, par, k, tt * P:(tt + 1) * P],
                                               wt[:, k, hf * 512:(hf + 1) * 512], start=(k == 0), stop=(k == 1))
                            mm.then_inc(S["down_done"], 1)

            with pe.If(fullest < SLOTS + 1):
                gather(0, 0, first=True)
                for p in range(2):
                    pair(p, p % 2)
                with pe.Fori(1, (PAIRS - 2) // 2) as i:
                    for j in range(2):
                        pair(i * 2 + j, j)
                for p in range(PAIRS - 2, PAIRS):
                    pair(p, p % 2)
                mix(PAIRS - 1, 1)
            with pe.Else():
                pair_all(0)
                with pe.Fori(1, PAIRS) as i:
                    pair_all(i)
            state["n"] = L0
            for p in range(PAIRS):
                for done, n in ((S["gate_done"], 1), (S["gu_done"], 1), (S["down_done"], 4)):
                    chunk_free.extend([(done, n * (2 * p + 1)), (done, n * (2 * p + 2))])
            assert len(chunk_free) == L0
            pe.wait_ge(S["down_out"], 4 * EXPERTS)

            for l in range(LAYERS):
                pe.wait_ge(S["cbc_ready"], l + 1)
                for hf in range(2):
                    b = A.acquire(pe, f"gate{l}{hf}")
                    pe.matmul(b[:, :], allone[:, :], gdiag[:, 4 * hf:4 * hf + 4, :], start=True, stop=True) \
                        .then_inc(A.done, 1)
                transpose_x(3 + l, f"L{l}")
                for j in range(4):
                    w = chunk()
                    for m in range(2):
                        projT(w, m, hT, A, f"rx{l}{2 * j + m}", tag=f"L{l}" if j == m == 0 else None)
                    used()
                w = full(chunk())
                for h in range(KB):
                    pe.wait_ge(S["conv_ready"], l * KB + h + 1)
                    b = A.acquire(pe, f"ri{l}{h}")
                    pe.matmul(b[:, 0:T], w[:, h, 0:P], rxc[:, h, :], start=True, stop=True)
                    pe.matmul(b[:, T:2 * T], w[:, h, P:2 * P], rxc[:, h, :], start=True, stop=True).then_inc(A.done, 1)
                used()
                for name in ("rz", "mx"):
                    for j in range(4):
                        w = chunk()
                        for m in range(2):
                            projT(w, m, hT, A, f"{name}{l}{2 * j + m}")
                        used()
                def out_gate(j):
                    w = full(chunk())
                    for tt in range(TT):
                        b = A.acquire(pe, f"mo{l}{j}{tt}")
                        for kb in range(KB):
                            mm = pe.matmul(b[:, 0:CW], hT[:, kb, tt * P:(tt + 1) * P], w[:, kb, :],
                                           start=(kb == 0), stop=(kb == KB - 1))
                        mm.then_inc(A.done, 1)
                    used()
                out_gate(0)
                out_gate(1)
                wq = full(chunk())
                pe.wait_ge(S["mc_ready"], l * KB + KB)

                def headT(w, src, name):
                    for h in range(MLH):
                        b = A.acquire(pe, f"{name}{l}{h}")
                        for m in range(2):
                            for k in range(2):
                                mm = pe.matmul(b[:, m * T:(m + 1) * T], w[:, 2 * h + k, m * P:(m + 1) * P],
                                               src(2 * h + k), start=(k == 0), stop=(k == 1))
                        mm.then_inc(A.done, 1)
                headT(wq, lambda k: mc[:, k, :], "mq")
                used()
                wk = full(chunk())
                headT(wk, lambda k: mc[:, k, :], "mk")
                used()
                wv2 = full(chunk())
                for tt in range(TT):
                    for hp in range(2):
                        b = A.acquire(pe, f"vn{l}{tt}{hp}")
                        for h in range(2):
                            for k in range(2):
                                kk = 2 * (2 * hp + h) + k
                                mm = pe.matmul(b[:, h * MLD:(h + 1) * MLD],
                                               mxv[:, kk, PAD + tt * P:PAD + (tt + 1) * P],
                                               wv2[:, kk, :], start=(k == 0), stop=(k == 1))
                        mm.then_inc(A.done, 1)
                used()
                pe.wait_ge(A.free, A.upto(f"mk{l}3"))
                for hp in range(2):
                    b = A.acquire(pe, f"kn{l}{hp}")
                    for n in range(4):
                        mm = tr(b[:, n * P:(n + 1) * P], mkT[:, 4 * hp + n, 0:P])
                    mm.then_inc(A.done, 1)
                pe.wait_ge(A.free, A.upto(f"vn{l}11"))
                for h in range(MLH):
                    b = A.acquire(pe, f"mv{l}{h}")
                    for m in range(2):
                        for tt in range(TT):
                            mm = tr(b[:, m * T + tt * P:m * T + (tt + 1) * P], vaug[:, tt, h, m * P:(m + 1) * P])
                    mm.then_inc(A.done, 1)
                pe.wait_ge(A.free, A.upto(f"mv{l}3"))
                pe.wait_ge(S["gate_b_loaded"], 16 * 3 * LAYERS)
                b = B.acquire(pe, f"gr{l}")
                for k in range(0, 24, 2):
                    for odd in range(2):
                        src = (mqT, mkT, mvT)[k // 8]
                        for g in range(2):
                            q = 32 * (2 * odd + g)
                            mm = pe.matmul(b[q:q + MLH, 0:T], wif[:, l, k + odd, g * MLH:(g + 1) * MLH],
                                           src[:, k % 8 + odd, :], start=(k == 0), stop=(k == 22))
                mm.then_inc(B.done, 1)
                out_gate(2)
                out_gate(3)
                z_left = list(range(KB))
                zst = {}

                def z_job():
                    m = z_left.pop(0)
                    if m % 2 == 0:
                        zst["w"] = chunk()
                    projT(zst["w"], m % 2, hT, A, f"mz{l}{m}")
                    if m % 2:
                        used()

                z_job()
                z_job()
                pe.wait_ge(S["row_ready"], 3 * (l + 1))
                b = B.acquire(pe, f"cols{l}")
                for n, (r, o) in enumerate(((6, 0), (6, P), (2, 0), (2, P))):
                    mm = tr(b[:, n * MLH:(n + 1) * MLH], rows[:, r, o:o + P], MLH)
                mm.then_inc(B.done, 1)
                for c in range(TT):
                    for h in range(MLH):
                        b = A.acquire(pe, f"E{l}{c}{h}")
                        pe.matmul(b[:, 0:P], rows[:, 3, c * P:(c + 1) * P], sel4[:, h, :], start=True, stop=False)
                        pe.matmul(b[:, 0:P], sel4[:, h, :], rows[:, 5, c * P:(c + 1) * P], start=False, stop=False)
                        pe.matmul(b[:, 0:P], ident[:, :], later[:, :], start=False, stop=True).then_inc(A.done, 1)
                        b = B.acquire(pe, f"St{l}{c}{h}")
                        for k in range(2):
                            mm = pe.matmul(b[:, 0:P], mkT[:, 2 * h + k, c * P:(c + 1) * P],
                                           mqT[:, 2 * h + k, c * P:(c + 1) * P], start=(k == 0), stop=(k == 1))
                        mm.then_inc(B.done, 1)
                        if c == 1:
                            b = A.acquire(pe, f"in{l}{h}")
                            for k in range(2):
                                mm = pe.matmul(b[:, 0:VW], mqT[:, 2 * h + k, P:2 * P], caug[:, h, k, :],
                                               start=(k == 0), stop=(k == 1))
                            mm.then_inc(A.done, 1)
                        if z_left:
                            z_job()
                        pe.wait_ge(B.free, B.upto(f"St{l}{c}{h}"))
                        b = B.acquire(pe, f"nm{l}{c}{h}")
                        pe.matmul(b[:, 0:VW], stb[:, h % 2, :], vaug[:, c, h, :], start=True, stop=True) \
                            .then_inc(B.done, 1)
                    if c == 0:
                        pe.wait_ge(S["kw_ready"], MLH * (l + 1))
                        pe.wait_ge(S["rg_done"], l + 1)
                        for h in range(MLH):
                            for k in range(2):
                                b = A.acquire(pe, f"C{l}{h}{k}")
                                pe.matmul(b[:, 0:VW], knat[:, h, k * P:(k + 1) * P], vaug[:, 0, h, :],
                                          start=True, stop=True).then_inc(A.done, 1)
                        pe.wait_ge(A.free, A.upto(f"C{l}31"))
                assert not z_left
                xo = {}
                for n, (kh, j) in enumerate(OUT_ORDER):
                    if n == 2:
                        pe.wait_ge(S["hq_ready"], l + 1)
                        for m in range(KB):
                            b = B.acquire(pe, f"ym{l}{m}")
                            for tt in range(TT):
                                mm = tr(b[:, tt * P:(tt + 1) * P], hh[:, tt, m * P:(m + 1) * P])
                            mm.then_inc(B.done, 1)
                        pe.wait_ge(B.free, B.upto(f"ym{l}7"))
                    w = full(chunk())
                    yT = ymT if kh else thr
                    for tt in range(TT):
                        if kh == 0:
                            xo[j, tt] = A.acquire(pe, f"xo{l}{j}{tt}")
                        for kb in range(KB):
                            mm = pe.matmul(xo[j, tt][:, 0:CW], yT[:, kb, tt * P:(tt + 1) * P], w[:, kb, :],
                                           start=(kh == 0 and kb == 0), stop=(kh == 1 and kb == KB - 1))
                        if kh == 1:
                            mm.then_inc(A.done, 1)
                    if kh == 0:
                        used(mm=mm)
                    else:
                        chunk_free.append((A.done, A.upto(f"xo{l}{j}1")))
            assert state["n"] == len(nparts), state

        @block.sync
        def _(sp):
            sp.dma_start(x[:, 0, :], a["x"][0, 0:P, :]).then_inc(S["x_loaded"], 16)
            sp.dma_start(x[:, 1, :], a["x"][0, P:T, :]).then_inc(S["x_loaded"], 16)

            def load_layer_rows():
                for l in range(LAYERS):
                    for row, src in ((V_NORM, r8(a["norm_g_2"][l])), (V_ADA, r8(a["b_ada_2"][l])),
                                     (V_RCW, a["rg_conv_w_2"][l].rearrange("j (k p) -> (j k) p", p=P)),
                                     (V_MCW, a["ml_conv_w_2"][l].rearrange("j (k p) -> (j k) p", p=P)),
                                     (V_RCB, r8(a["rg_conv_b_2"][l])), (V_BA, r8(a["rg_b_a_2"][l])),
                                     (V_BX, r8(a["rg_b_x_2"][l])), (V_LAM, r8(a["rg_lambda_2"][l]))):
                        sp.dma_start(rowsL[row:row + src.shape[0], l, :], src).then_inc(S["rowsL_loaded"], 16)
                    sp.dma_start(rowsM[0:8, l, :], r8(a["ml_conv_b_2"][l])).then_inc(S["rowsL_loaded"], 16)
                    sp.dma_start(rowsM[8:16, l, :], r8(a["ml_norm_g_2"][l])).then_inc(S["rowsL_loaded"], 16)

            def load(n, parts):
                if n >= RING:
                    sp.wait_ge(*chunk_free[n - RING])
                for dst, src in parts:
                    sp.dma_start(dst(ring[n % RING]), src).then_inc(slot_full[n % RING], 16)

            for n, parts in enumerate(chunks):
                load(n, parts)
                if n == 1:
                    load_layer_rows()

            def expert_part(e, kind):
                k = 2 if kind == "w_down" else KB
                return (lambda t: t[:, :].rearrange("p (k c) -> p k c", k=k),
                        a[kind][0, e].rearrange("(k p) c -> p k c", p=P))

            kinds = (("w_gate", S["gate_done"], 1), ("w_up", S["gu_done"], 1), ("w_down", S["down_done"], 4))
            for k, (kind, _, _) in enumerate(kinds):
                for par in range(2):
                    load(E0 + 2 * k + par, [expert_part(par, kind)])
            with sp.Fori(1, PAIRS) as i:
                for k, (kind, used_sem, per_expert) in enumerate(kinds):
                    for par in range(2):
                        n0 = E0 + 2 * k + par
                        sp.wait_ge(used_sem, i * (2 * per_expert) + (par - 1) * per_expert)
                        dst, src = expert_part(i * 2 + par, kind)
                        sp.dma_start(dst(ring[n0 % RING]), src).then_inc(slot_full[n0 % RING], 16)

            for n, parts in enumerate(tail):
                load(L0 + n, parts)
            for tt in range(TT):
                sp.wait_ge(S["layer_done"], LAYERS + tt + 1)
                sp.dma_start(out[0, tt * P:(tt + 1) * P, :], xn[:, tt, :]).then_inc(S["x_stored"], 16)
            sp.wait_ge(S["x_stored"], 32)

        @block.scalar
        def _(act):
            step = Chain(act, s_act)
            f = act.activation

            def roots(n, view):
                act.wait_ge(S["root_wanted"], n)
                step(f(view, view, ACT.Sqrt), S["root_ready"])

            def sumsq(ready=((), ())):
                for tt in range(TT):
                    if ready[tt]:
                        act.wait_ge(*ready[tt])
                    step(f(squares[:, tt, :], x[:, tt, :], ACT.Square, accum_out=small[:, tt:tt + 1]), S["ssq_ready"])

            def load_root_table():
                act.wait_ge(S["const_ready"], 1)
                step(f(small[:, 40:41], desc[:, 0:1], ACT.Sqrt))

            def out_copy(dst, n, func=ACT.Copy, **k):
                b = A.take(act)
                step(f(dst, b[:, 0:n], func, **k), A.free)

            ada = {"n": 0}

            def ada_job():
                n = ada["n"] - ADA_LAG
                ada["n"] += 1
                if n >= 0:
                    l, j = divmod(n, 3 * D // CW)
                    out_copy(adac[:, l, 2 * j:2 * j + 2], 2)

            for dst, src in ((rowsA[0:8, :], r8(a["norm1_g"][0])), (rowsA[8:16, :], r8(a["norm2_g"][0])),
                             (rowsA[16:17, :], a["kv_norm_g"]), (rowsA[17:25, :], r8(a["c_2"][0]))):
                act.dma_start(dst, src).then_inc(S["rows_loaded"], 16)
            act.dma_start(relw, a["rel_bias"]).then_inc(S["rel_loaded"], 16)
            act.dma_start(reltab, a["bucket_of_distance"]).then_inc(S["rel_loaded"], 16)
            act.wait_ge(S["x_loaded"], 32)
            sumsq()
            roots(1, small[:, 2:4])
            act.wait_ge(B.free, B.upto("colA"))
            step(f(csil[:, :], colA[:, 17:25], ACT.Tanh, scale=0.5), S["csil_tanh"])
            for tt in range(TT):
                b = A.take(act)
                step(f(ckv[:, tt, :], b[:, 0:RANK], ACT.Copy))
                step(f(pT[:, 0, tt, :], b[:, 0:RANK], ACT.Square, accum_out=small[:, 4 + tt:5 + tt]), A.free)
            out_copy(kiT, T)
            b = A.take(act)
            step(f(wi, b[:, 0:16].rearrange("p (t h) -> p t h", t=TT), ACT.Copy, scale=IDX_SCALE), A.free)
            roots(2, small[:, 6:8])
            act.wait_ge(S["sp_wanted"], 1)
            step(f(labs, labs, ACT.Exp, scale=-1.0), S["sp_ready"])
            for dst in (qT, qiT):
                for m in range(4):
                    out_copy(dst[:, m, :], T)
                    if m % 2:
                        ada_job()
            for tt in range(TT):
                ns = (tt + 1) * P
                for h in range(HEADS):
                    k = tt * HEADS + h
                    b = A.take(act)
                    if k >= 2:
                        act.wait_ge(S["relu_used"], k - 1)
                    step(f(relu[:, k % 2, 0:ns], b[:, 0:ns], ACT.Relu), A.free)
            for m in range(4):
                out_copy(kvT[:, m, :], T)
            for tt in range(TT):
                out_copy(vnat[:, tt, :], 512)
            for m in range(4):
                out_copy(guT[:, m, :], T, ACT.Gelu_apprx_tanh)
                if m % 2:
                    ada_job()
            for j in range(2):
                for tt in range(TT):
                    out_copy(gv[:, tt, j * CW:(j + 1) * CW], CW, ACT.Gelu_apprx_tanh)
                ada_job()
            out_copy(wsT, 512)
            roots(3, small[:, 12:14])
            gates = [(tga, m) for m in range(KB)] + [(tgb, m) for m in range(KB)]

            def gate_job():
                if gates:
                    t, m = gates.pop(0)
                    out_copy(t[:, m, :], T, ACT.Tanh, scale=0.5)
                    if m % 2:
                        ada_job()

            for h in range(HEADS + 1):
                gate_job()
                if h < HEADS:
                    for tt in range(TT):
                        ns = (tt + 1) * P
                        k = 2 * h + tt
                        act.wait_ge(S["sc_ready"], k + 1)
                        if k >= 4:
                            act.wait_ge(A.done, A.upto(f"pT{h - 2}"))
                        step(f(prob[h % 2][tt][:, 0:ns], sc[:, tt, 0:ns], ACT.Exp, bias=rt[:, tt:tt + 1],
                               accum_out=rt[:, 2 + tt:3 + tt]), S["p_ready"])
                gate_job()
                if h >= 1:
                    g = h - 1
                    o = (g % 2) * 64
                    b = A.take(act)
                    step(f(pT[:, g % 2, :, :], b[:, 0:384].rearrange("p (s q) -> p s q", s=3), ACT.Copy), A.free)
                    b = A.take(act)
                    step(f(oaT[o:o + 64, g // 2, :], b[o:o + 64, 0:T], ACT.Copy), A.free)
            for _ in range(8):
                ada_job()
            load_root_table()
            sumsq([(B.free, B.upto(f"xo3{tt}")) for tt in range(TT)])
            roots(4, small[:, 2:4])
            act.wait_ge(S["exp_wanted"], 1)
            step(f(rt[:, 8:8 + TT * EG], rt[:, 8:8 + TT * EG], ACT.Exp), S["exp_ready"])
            act.wait_ge(S["exp_wanted"], 2)
            step(f(rt[:, 32:32 + TT * EPG], rt[:, 32:32 + TT * EPG], ACT.Exp), S["exp_ready"])
            for _ in range(ADA_LAG):
                ada_job()
            act.wait_ge(S["most_ready"], 1)
            fullest = act.value_load(most[0:1, 0:1], min_val=0, max_val=T)

            def gathered(p, q):
                for hf in range(2):
                    act.wait_ge(S["gather_done"], p * 2 + (hf + 1))
                    f(hgT[:, 4 * hf:4 * hf + 4, :], psum[hf][:, :].rearrange("p (b s) -> p b s", b=4), ACT.Copy) \
                        .then_inc(S["gather_ready"], 1)
                act.wait_ge(S["combT_done"], p + 1)
                f(combT[:, q, :], psum[2][:, 0:T], ACT.Copy).then_inc(S["combT_ready"], 1)

            def pair(p, q):
                act.wait_ge(S["gu_done"], p * 2 + 2)
                f(thgs, psum[3][:, 0:FF], ACT.Tanh, scale=0.5).then_inc(S["tanh_gate"], 1)
                act.wait_ge(S["heT_done"], p + 1)
                f(heTs, psum[3][:, 0:2 * P].rearrange("p (b s) -> p b s", b=2), ACT.Copy).then_inc(S["heT_ready"], 1)
                if not isinstance(p, int) or p + 1 < PAIRS:
                    gathered(p + 1, 1 - q)
                for hf in range(2):
                    if hf == 0:
                        act.wait_ge(S["down_half"], p + 1)
                    else:
                        act.wait_ge(S["down_done"], p * 8 + 8)
                    f(ye[:, hf * 512:(hf + 1) * 512], psum[5 + hf][:, :], ACT.Copy).then_inc(S["ye_ready"], 1)

            def gate_tanh(e, par):
                act.wait_ge(S["gu_done"], e + 1)
                if isinstance(e, int) and e < 2:
                    pass
                else:
                    act.wait_ge(S["he_ready"], e - 1)
                f(thg[:, par, :], psum[par][:, :], ACT.Tanh, scale=0.5).then_inc(S["tanh_gate"], 1)

            with act.If(fullest < SLOTS + 1):
                gathered(0, 0)
                for p in range(2):
                    pair(p, p % 2)
                with act.Fori(1, (PAIRS - 2) // 2) as i:
                    for j in range(2):
                        pair(i * 2 + j, j)
                for p in range(PAIRS - 2, PAIRS):
                    pair(p, p % 2)
            with act.Else():
                gate_tanh(0, 0)
                gate_tanh(1, 1)
                with act.Fori(1, EXPERTS // 2) as i:
                    for j in range(2):
                        gate_tanh(i * 2 + j, j)
            load_root_table()
            act.wait_ge(S["down_out"], 4 * EXPERTS)
            sumsq()
            roots(5, small[:, 2:4])
            act.wait_ge(S["xg_ready"], 2)
            for tt in range(TT):
                step(f(squares[:, tt, :], xn[:, tt, :], ACT.Square, accum_out=small[:, 8 + tt:9 + tt]), S["ssq_ready"])
            roots(6, small[:, 10:12])
            for l in range(LAYERS):
                if l == 0:
                    act.wait_ge(S["xg_ready"], 2)
                else:
                    sumsq([(S["tile0_done"], l), (S["layer_done"], l)])
                    roots(6 + 2 * l, small[:, 2:4])
                for hf in range(2):
                    out_copy(gateB[:, hf * 512:(hf + 1) * 512], 512)
                for m in range(KB):
                    out_copy(rxv[:, m, PAD:PAD + T], T)
                for h in range(KB):
                    b = A.take(act)
                    if h == 0:
                        act.wait_ge(S["mod_ready"], l + 1)
                    step(f(thr[:, h, :], b[:, 0:T], ACT.Tanh, scale=0.5, bias=hb[:, l, h:h + 1]))
                    step(f(thi[:, h, :], b[:, T:2 * T], ACT.Tanh, scale=0.5, bias=hb[:, l, KB + h:KB + h + 1]), A.free)
                for h in range(KB):
                    step(f(aa[:, h, :], thr[:, h, :], ACT.Exp, scale=n4[:, 1, h:h + 1], bias=n4[:, 1, h:h + 1]))
                    step(f(tl[:, h, :], thr[:, h, :], ACT.Tanh, scale=n4[:, 0, h:h + 1], bias=n4[:, 0, h:h + 1]),
                         S["rg_gate"])
                def silu_part(dst, th_dst, name):
                    for m in range(KB):
                        b = A.take(act)
                        step(f(dst[:, m, :], b[:, 0:T], ACT.Copy))
                        step(f(th_dst[:, m, :], b[:, 0:T], ACT.Tanh, scale=0.5), A.free)
                act.wait_ge(S["xn_ready"], 3 + l)
                act.wait_ge(B.free, B.upto(f"hTL{l}7"))
                silu_part(zr, mth, "rz")
                for m in range(KB):
                    out_copy(mxv[:, m, PAD:PAD + T], T)
                act.wait_ge(S["rg_root_wanted"], l + 1)
                step(f(tl[:, :, :], tl[:, :, :], ACT.Sqrt), S["rg_root"])
                for m in range(KB):
                    act.wait_ge(S["mconv_ready"], l * KB + m + 1)
                    step(f(mth[:, m, :], mc[:, m, :], ACT.Tanh, scale=0.5), S["mtanh_ready"])

                def out_gate(j):
                    for tt in range(TT):
                        out_copy(oth[:, tt, j * CW:(j + 1) * CW], CW, ACT.Tanh, scale=0.5)
                out_gate(0)
                out_gate(1)
                for h in range(MLH):
                    b = A.take(act)
                    step(f(mqT[:, 2 * h:2 * h + 2, :], b[:, :].rearrange("p (m t) -> p m t", m=2), ACT.Copy,
                           scale=0.5), A.free)
                for h in range(MLH):
                    b = A.take(act)
                    step(f(mkT[:, 2 * h:2 * h + 2, :], b[:, :].rearrange("p (m t) -> p m t", m=2), ACT.Copy,
                           scale=0.5), A.free)
                for tt in range(TT):
                    for hp in range(2):
                        b = A.take(act)
                        step(f(vaug[:, tt, 2 * hp:2 * hp + 2, 0:MLD], b[:, :].rearrange("p (h c) -> p h c", h=2),
                               ACT.Copy), A.free)
                for hp in range(2):
                    b = A.take(act)
                    step(f(knat[:, 2 * hp:2 * hp + 2, :], b[:, :].rearrange("p (h c) -> p h c", h=2), ACT.Copy,
                           scale=MLD ** -0.5), A.free)
                act.wait_ge(S["rg_done"], l + 1)
                for h in range(MLH):
                    b = A.take(act)
                    step(f(mvT[:, 2 * h:2 * h + 2, :], b[:, :].rearrange("p (m t) -> p m t", m=2), ACT.Copy), A.free)
                act.wait_ge(S["lf_wanted"], l + 1)
                step(f(rows[:, 2, :], rows[:, 2, :], ACT.Exp, scale=-1.0), S["lf_ready"])
                out_gate(2)
                out_gate(3)
                act.wait_ge(S["mc_ready"], l * KB + KB)
                z_left = list(range(KB))

                def z_job():
                    m = z_left.pop(0)
                    b = A.take(act)
                    step(f(zm[:, m, :], b[:, 0:T], ACT.Copy))
                    if m >= 2:
                        act.wait_ge(S["zm_ready"], l * KB + m - 1)
                    step(f(zth[m % 2], b[:, 0:T], ACT.Tanh, scale=0.5), A.free)

                act.wait_ge(S["row_wanted"], l + 1)
                step(f(rows[:, 6, 0:P], rows[:, 3, 0:P], ACT.Exp, bias=rsc[:, 0:1]), S["row_ready"])
                step(f(rows[:, 6, P:T], rows[:, 5, P:T], ACT.Exp, bias=rsc[:, 1:2]), S["row_ready"])
                step(f(rows[:, 2, :], rows[:, 2, :], ACT.Exp, scale=-1.0), S["row_ready"])
                z_job()
                z_job()
                for c in range(TT):
                    for h in range(MLH):
                        b = A.take(act)
                        k8 = l * 8 + c * MLH + h
                        if h >= 2:
                            act.wait_ge(B.free, B.upto(f"St{l}{c}{h - 2}"))
                        elif c == 1:
                            act.wait_ge(B.free, B.upto(f"St{l}0{h + 2}"))
                        step(f(ebuf[:, h % 2, :], b[:, 0:P], ACT.Exp), A.free)
                        if c == 1:
                            b = A.take(act)
                            act.wait_ge(B.free, B.upto(f"cols{l}"))
                            if h >= 2:
                                act.wait_ge(S["hh_ready"], k8 - 1)
                            step(f(inter[:, h % 2, :], b[:, 0:VW], ACT.Copy, scale=cols[:, 1, h:h + 1]), A.free)
                        if z_left:
                            z_job()
                    if c == 0:
                        for h in range(MLH):
                            for k in range(2):
                                out_copy(caug[:, h, k, :], VW)
                act.wait_ge(S["zm_ready"], (l + 1) * KB)
                step.skip(A.free, 8)
                A.got += 8
                for c in range(TT):
                    for h in range(MLH):
                        act.wait_ge(S["hh_ready"], l * 8 + c * MLH + h + 1)
                        step(f(mth[:, 0, :], hh[:, c, h * MLD:(h + 1) * MLD], ACT.Square,
                               accum_out=small[:, 16 + c * MLH + h:17 + c * MLH + h]), S["ssq_ready"])
                roots(7 + 2 * l, small[:, 24:32])
            sumsq([(S["tile0_done"], LAYERS), (S["layer_done"], LAYERS)])
            roots(6 + 2 * LAYERS, small[:, 2:4])

        @block.vector
        def _(v):
            step = Chain(v, s_dve)
            tsc, stt, tten = v.tensor_scalar, v.scalar_tensor_tensor, v.tensor_tensor
            roots_n = {"n": 0, "ssq": 0}

            def rstd(dst, src, scale):
                roots_n["n"] += 1
                step(tsc(dst, src, scale, EPS, ALU.mult, ALU.add), S["root_wanted"])
                v.wait_ge(S["root_ready"], roots_n["n"])
                step(v.reciprocal(dst, dst))

            def norm_x():
                roots_n["ssq"] += 2
                v.wait_ge(S["ssq_ready"], roots_n["ssq"])
                rstd(small[:, 2:4], small[:, 0:2], 1.0 / D)

            def take_hT(scale, shift=None):
                for kb in range(KB):
                    b = B.take(v)
                    if shift is None:
                        step(tsc(hT[:, kb, :], b[:, 0:T], scale[:, kb:kb + 1], None, ALU.mult), B.free)
                    else:
                        step(tsc(hT[:, kb, :], b[:, 0:T], scale[:, kb:kb + 1], shift[:, kb:kb + 1], ALU.mult, ALU.add),
                             B.free)

            def log1p(dst, e, y, t):
                step(tsc(t, e, 2.0, None, ALU.add))
                step(v.reciprocal(t, t))
                step(tten(y, e, t, ALU.mult))
                step(tten(t, y, y, ALU.mult))
                step(tsc(dst, t, LOG1P[0], None, ALU.mult))
                for c in LOG1P[1:]:
                    step(stt(dst, dst, c, t, ALU.add, ALU.mult))
                step(stt(dst, dst, 1.0, y, ALU.add, ALU.mult))
                step(tsc(dst, dst, 2.0, None, ALU.mult))

            norm_x()
            for tt in range(TT):
                ins = tsc(xn[:, tt, :], x[:, tt, :], small[:, 2 + tt:3 + tt], None, ALU.mult)
                step(ins, S["xn_ready"]) if tt == 1 else step(ins)
            b = B.take(v)
            step(v.tensor_copy(colA[:, 0:25], b[:, 0:25]), B.free)
            take_hT(colA[:, 0:8])
            v.wait_ge(S["csil_tanh"], 1)
            step(stt(csil[:, :], csil[:, :], 1.0, colA[:, 17:25], ALU.add, ALU.mult))
            step(tsc(csil[:, :], csil[:, :], 0.5, None, ALU.mult), S["csil_ready"])
            v.wait_ge(A.free, A.upto("ckv1"))
            rstd(small[:, 6:8], small[:, 4:6], 1.0 / RANK)
            for tt in range(TT):
                ins = tsc(ckv[:, tt, :], ckv[:, tt, :], small[:, 6 + tt:7 + tt], None, ALU.mult)
                step(ins, S["ckv_ready"]) if tt == 1 else step(ins)
            for l in range(LAYERS):
                b = B.take(v)
                step(v.tensor_copy(colL[:, l, :], b[:, 0:P]))
                step(v.tensor_copy(colM[:, l, :], b[:, P:P + 16]), B.free)
            step(tsc(lneg, colL[:, :, V_LAM:V_LAM + KB], -1.0, None, ALU.mult))
            step(tten(labs, lneg, colL[:, :, V_LAM:V_LAM + KB], ALU.max))
            step(tsc(hb[:, :, :], colL[:, :, V_BA:V_BA + 2 * KB], 0.5, None, ALU.mult), S["sp_wanted"])
            b = B.take(v)
            step(v.tensor_copy(relrow, b[0:HEADS, :]), B.free)
            v.wait_ge(A.free, A.upto("wi"))
            for tt in range(TT):
                ns = (tt + 1) * P
                for h in range(HEADS):
                    v.wait_ge(A.free, A.upto(f"idx{tt}{h}"))
                    k = tt * HEADS + h
                    r = relu[:, k % 2, 0:ns]
                    if h == 0:
                        step(tsc(idx[:, tt, 0:ns], r, wi[:, tt, h:h + 1], None, ALU.mult), S["relu_used"])
                    else:
                        step(stt(idx[:, tt, 0:ns], r, wi[:, tt, h:h + 1], idx[:, tt, 0:ns], ALU.mult, ALU.add),
                             S["relu_used"])
            b = B.take(v)
            step(tsc(cT, b[:, 0:T], colA[:, 16:17], None, ALU.mult), B.free)
            for tt in range(TT):
                ns = (tt + 1) * P
                v.wait_ge(S["idx_masked"], tt + 1)
                for r in range(TOPK // 8):
                    step(v.max(m8[:, :], idx[:, tt, 0:ns]))
                    step(v.match_replace(idx[:, tt, 0:ns], m8[:, :], idx[:, tt, 0:ns], TAKEN))
                step(tsc(maskb[:, tt, 0:ns], idx[:, tt, 0:ns], TAKEN, None, ALU.is_equal))
                step(tsc(maskb[:, tt, 0:ns], maskb[:, tt, 0:ns], -1.0, BIG, ALU.add, ALU.mult), S["sel_ready"])
            v.wait_ge(S["sp_ready"], 1)
            log1p(lsp, labs, ly, lt)
            step(stt(lsp, lneg, 0.0, lsp, ALU.max, ALU.add))
            v.wait_ge(A.free, A.upto("v11"))
            for tt in range(TT):
                step(v.bn_stats(vst[:, 0:6], gv[:, tt, :]))
                step(v.bn_aggr(vst[:, 8 + 2 * tt:10 + 2 * tt], vst[:, 0:6]))
                step(v.tensor_copy(small[:, 12 + tt:13 + tt], vst[:, 9 + 2 * tt:10 + 2 * tt]))
            rstd(small[:, 12:14], small[:, 12:14], 1.0)
            v.wait_ge(S["ln_loaded"], 48)
            for tt in range(TT):
                step(tsc(gv[:, tt, :], gv[:, tt, :], vst[:, 8 + 2 * tt:9 + 2 * tt], small[:, 12 + tt:13 + tt],
                         ALU.subtract, ALU.mult))
                step(tten(gv[:, tt, :], gv[:, tt, :], lng, ALU.mult))
                ins = tten(gv[:, tt, :], gv[:, tt, :], lnb, ALU.add)
                step(ins, S["vln_ready"]) if tt == 1 else step(ins)
            v.wait_ge(S["mask_ready"], 2)
            for h in range(HEADS):
                for tt in range(TT):
                    ns = (tt + 1) * P
                    k = 2 * h + tt
                    b = B.take(v)
                    if k >= 2:
                        v.wait_ge(S["p_ready"], k - 1)
                    step(stt(sc[:, tt, 0:ns], b[:, 0:ns], SCALE, maskb[:, tt, 0:ns], ALU.mult, ALU.add), B.free)
                    step(v.tensor_reduce(rt[:, tt:tt + 1], sc[:, tt, 0:ns], AX.X, ALU.max, negate=True), S["sc_ready"])
                for tt in range(TT):
                    ns = (tt + 1) * P
                    v.wait_ge(S["p_ready"], 2 * h + tt + 1)
                    step(v.reciprocal(rt[:, 4 + tt:5 + tt], rt[:, 2 + tt:3 + tt]))
                    pn = prob[h % 2][tt][:, 0:ns]
                    step(tsc(pn, pn, rt[:, 4 + tt:5 + tt], None, ALU.mult), S["prob_ready"])
            for g in range(GROUPS):
                b = B.take(v)
                step(tten(gmT[:, g, :], b[:, 0:T], guT[:, g, :], ALU.mult), B.free)
            ada = {"n": ADA_POOL}

            def ada_sums(count):
                for n in range(ada["n"], ada["n"] + count):
                    c = ada_chunks[n]
                    v.wait_ge(slot_full[c % RING], fill_value[c])
                    v.wait_ge(A.done, A.upto(f"ada{n - 3}"))
                    w, dst = full(ring[c % RING]), adasum[:, n % 3, :]
                    step(tsc(dst, w[:, 0, :], csil[:, 0:1], None, ALU.mult))
                    for kb in range(1, KB):
                        ins = stt(dst, w[:, kb, :], csil[:, kb:kb + 1], dst, ALU.mult, ALU.add)
                        step(ins, S["ada_summed_v"]) if kb == KB - 1 else step(ins)
                ada["n"] += count

            v.wait_ge(A.free, A.upto("g15"))
            for m in range(KB):
                b = B.take(v)
                step(stt(mtmp[:, 0, :], tga[:, m, :], 1.0, b[:, 0:T], ALU.add, ALU.mult), B.free)
                b = B.take(v)
                step(stt(mtmp[:, 1, :], tgb[:, m, :], 1.0, b[:, 0:T], ALU.add, ALU.mult), B.free)
                step(tten(mgT[:, m, :], mtmp[:, 0, :], mtmp[:, 1, :], ALU.add), S["mg_ready"])
                if m % 2 and m > 1:
                    ada_sums(1)
            for j in range(4):
                for tt in range(TT):
                    b = B.take(v)
                    xs = x[:, tt, j * CW:(j + 1) * CW]
                    step(stt(xs, b[:, 0:CW], 0.5, xs, ALU.mult, ALU.add), B.free)
                ada_sums((1, 1, 2, 0)[j])
            norm_x()
            v.wait_ge(S["norm2_loaded"], 16)
            for tt in range(TT):
                ins = stt(xg[:, tt, :], x[:, tt, :], small[:, 2 + tt:3 + tt], norm2, ALU.mult, ALU.mult)
                step(ins, S["xn_ready"]) if tt == 1 else step(ins)
            for kb in range(KB):
                b = B.take(v)
                step(v.tensor_copy(hT[:, kb, :], b[:, 0:T]), B.free)
            b = B.take(v)
            NR = EG + EXPERTS
            step(v.tensor_copy(logit[:, :, :], b[:, 0:TT * NR].rearrange("p (t n) -> p t n", t=TT)), B.free)
            v.wait_ge(S["const_ready"], 1)

            def each(t, n):
                return t.unsqueeze(2).broadcast_to([P, TT, n])

            def rt3(c, n):
                return rt[:, c:c + TT * n].rearrange("p (t n) -> p t n", t=TT)

            t1, p_group, second = rt[:, 0:2], rt[:, 2:4], rt[:, 4:6]
            eg, group = rt3(8, EG), rt3(16, EG)
            le, best, w8 = rt3(32, EPG), rt3(48, EPG), rt3(64, EPG)
            comb4 = comb[:, :, :].rearrange("p t (g k) -> p t g k", g=EG)

            def first_max(onehot, vals, n, t1):
                descs = desc[:, 0:n].unsqueeze(1).broadcast_to([P, TT, n])
                step(v.tensor_reduce(t1, vals, AX.X, ALU.max))
                step(tten(onehot, vals, each(t1, n), ALU.is_equal))
                step(tten(onehot, onehot, descs, ALU.mult))
                step(v.tensor_reduce(t1, onehot, AX.X, ALU.max))
                step(tten(onehot, descs, each(t1, n), ALU.is_equal))

            lg = logit[:, :, 0:EG]
            step(v.tensor_reduce(t1, lg, AX.X, ALU.max))
            step(tten(eg, lg, each(t1, EG), ALU.subtract), S["exp_wanted"])
            first_max(group, lg, EG, t1)
            step(tten(comb4, logit[:, :, EG:NR].rearrange("p t (g k) -> p t g k", g=EG),
                      group.unsqueeze(3).broadcast_to([P, TT, EG, EPG]), ALU.mult))
            step(v.tensor_reduce(le, comb4.rearrange("p t g k -> p t k g"), AX.X, ALU.add))
            step(v.tensor_reduce(t1, le, AX.X, ALU.max))
            step(tten(le, le, each(t1, EPG), ALU.subtract), S["exp_wanted"])
            v.wait_ge(S["exp_ready"], 1)
            step(v.tensor_reduce(p_group, eg, AX.X, ALU.add))
            step(v.reciprocal(p_group, p_group))
            v.wait_ge(S["exp_ready"], 2)
            first_max(best, le, EPG, t1)
            step(stt(le, best, -2.0, le, ALU.mult, ALU.add))
            step(v.tensor_reduce(second, le, AX.X, ALU.max))
            first_max(w8, le, EPG, t1)
            step(tsc(t1, second, 1.0, None, ALU.add))
            step(v.reciprocal(t1, t1))
            step(stt(t1, t1, 0.5, p_group, ALU.mult, ALU.mult))
            step(tten(w8, w8, each(second, EPG), ALU.mult))
            step(tten(w8, w8, best, ALU.add))
            step(tten(w8, w8, each(t1, EPG), ALU.mult))
            step(tten(comb4, w8.unsqueeze(2).broadcast_to([P, TT, EG, EPG]),
                      group.unsqueeze(3).broadcast_to([P, TT, EG, EPG]), ALU.mult))
            step(tsc(member[:, :, :], comb[:, :, :], 0.0, None, ALU.is_gt), S["routed"])
            b = B.take(v)
            step(v.tensor_reduce(rt[:, 0:1], b[:, 2 * EXPERTS:3 * EXPERTS], AX.X, ALU.max))
            step(v.tensor_copy(most[:, :], rt[:, 0:1]), S["most_ready"])
            step(tten(key[:, :, :], b[:, 0:2 * EXPERTS].rearrange("p (t e) -> p t e", t=TT), member[:, :, :],
                      ALU.mult))
            step(v.tensor_copy(slotno, b[:, 3 * EXPERTS:3 * EXPERTS + SLOTS]), B.free)

            def slots(p, q):
                if not isinstance(p, int) or p >= 2:
                    v.wait_ge(S["combT_done"], p - 1)
                for tt in range(TT):
                    for j in range(2):
                        e = p * 2 + j
                        es = slice(e, e + 1) if isinstance(e, int) else bass.ds(e, 1)
                        js = slice(j * SLOTS, (j + 1) * SLOTS)
                        tsc(pick[:, q, tt, js], slotno, key[:, tt, es], None, ALU.is_equal) \
                            .then_inc(S["slots_ready"], 1)
                        tsc(pickw[:, q, tt, js], slotno, key[:, tt, es], comb[:, tt, es], ALU.is_equal, ALU.mult) \
                            .then_inc(S["slots_ready"], 1)

            slots(0, 0)
            slots(1, 1)
            fullest = v.value_load(most[0:1, 0:1], min_val=0, max_val=T)

            def act_own(p):
                v.wait_ge(S["tanh_gate"], p + 1)
                stt(sg[:, 0:FF], thgs, 1.0, psum[3][:, 0:FF], ALU.add, ALU.mult).then_inc(S["silu_ready"], 1)
                v.wait_ge(S["silu_ready"], p + 1)
                tten(he, psum[3][:, FF:2 * FF], sg[:, 0:FF], ALU.mult).then_inc(S["he_ready"], 1)
                v.wait_ge(S["he_ready"], p + 1)

            def mix_add(p):
                for r in range(4):
                    v.wait_ge(S["mixed"], p * 4 + (r + 1))
                    if r == 0 and not (isinstance(p, int) and p == 0):
                        v.wait_ge(S["down_out"], p * 8)
                    xs = x[:, r // 2, (r % 2) * 512:(r % 2 + 1) * 512]
                    tten(xs, psum[MIX_BANKS[r]][:, :], xs, ALU.add).then_inc(S["down_out"], 2)

            def pair(p, q):
                act_own(p)
                if not isinstance(p, int) or p >= 1:
                    mix_add(p - 1)
                if not isinstance(p, int) or p + 2 < PAIRS:
                    slots(p + 2, q)

            def gu(e, par):
                v.wait_ge(S["tanh_gate"], e + 1)
                v.scalar_tensor_tensor(sg[:, :], thg[:, par, :], 1.0, psum[par][:, :], ALU.add, ALU.mult) \
                    .then_inc(S["silu_ready"], 1)
                v.wait_ge(S["silu_ready"], e + 1)
                v.tensor_tensor(heT[:, par, :, :], psum[2 + par][:, :].rearrange("p (b t) -> p b t", b=2),
                                sg[:, :].rearrange("p (b t) -> p b t", b=2), ALU.mult).then_inc(S["he_ready"], 1)
                v.wait_ge(S["he_ready"], e + 1)

            def down_add(e):
                for tt in range(TT):
                    for hf in range(2):
                        k = 2 * tt + hf
                        v.wait_ge(S["down_done"], e * 4 + (k + 1))
                        if k == 0 and not (isinstance(e, int) and e == 0):
                            v.wait_ge(S["down_out"], e * 4)
                        xs = x[:, tt, hf * 512:(hf + 1) * 512]
                        v.scalar_tensor_tensor(xs, psum[4 + k][:, :], comb[:, tt, bass.ds(e, 1)] if not isinstance(e, int)
                                               else comb[:, tt, e:e + 1], xs, ALU.mult, ALU.add) \
                            .then_inc(S["down_out"], 1)
            with v.If(fullest < SLOTS + 1):
                for p in range(2):
                    pair(p, p % 2)
                with v.Fori(1, (PAIRS - 2) // 2) as i:
                    for j in range(2):
                        pair(i * 2 + j, j)
                for p in range(PAIRS - 2, PAIRS):
                    pair(p, p % 2)
                mix_add(PAIRS - 1)
            with v.Else():
                def pair_all(p):
                    for par in range(2):
                        gu(p * 2 + par, par)
                    for par in range(2):
                        down_add(p * 2 + par)

                pair_all(0)
                with v.Fori(1, PAIRS) as i:
                    pair_all(i)
            v.wait_ge(S["down_out"], 4 * EXPERTS)
            def modulation(l):
                mod = adac[:, l, :]
                if l == 0:
                    v.wait_ge(A.free, A.upto(f"ada{ADA_CHUNKS - 1}"))
                step(tten(mod, mod, colL[:, l, V_ADA:V_ADA + 3 * KB], ALU.add))
                step(tten(gdiag, ident[:, :].unsqueeze(1).broadcast_to([P, KB, P]),
                          mod[:, 2 * KB:3 * KB].unsqueeze(2).broadcast_to([P, KB, P]), ALU.mult), S["cbc_ready"])
                step(stt(gs[:, :], mod[:, KB:2 * KB], 1.0, colL[:, l, V_NORM:V_NORM + KB], ALU.add, ALU.mult))
                step(tsc(n4[:, 0, :], lsp[:, l, :], 4.0, None, ALU.mult))
                step(tsc(n4[:, 1, :], lsp[:, l, :], -4.0, None, ALU.mult), S["mod_ready"])

            modulation(0)
            v.wait_ge(S["gfin_loaded"], 16)
            for tt in range(TT):
                step(tten(xn[:, tt, :], x[:, tt, :], gfin[:, :], ALU.mult), S["xg_ready"])
            norm_x()
            v.wait_ge(S["ssq_ready"], roots_n["ssq"] + 2)
            roots_n["ssq"] += 2
            step(tten(small[:, 8:10], small[:, 8:10], small[:, 2:4], ALU.mult))
            step(tten(small[:, 8:10], small[:, 8:10], small[:, 2:4], ALU.mult))
            rstd(small[:, 10:12], small[:, 8:10], 1.0 / D)
            for tt in range(TT):
                step(tsc(x[:, tt, :], xn[:, tt, :], small[:, 2 + tt:3 + tt], None, ALU.mult))
                ins = tsc(xn[:, tt, :], xn[:, tt, :], small[:, 2 + tt:3 + tt], small[:, 10 + tt:11 + tt],
                          ALU.mult, ALU.mult)
                step(ins, S["xn_ready"]) if tt == 1 else step(ins)

            for l in range(LAYERS):
                mod = adac[:, l, :]
                if l > 0:
                    modulation(l)
                    norm_x()
                    for tt in range(TT):
                        ins = tsc(xn[:, tt, :], x[:, tt, :], small[:, 2 + tt:3 + tt], None, ALU.mult)
                        step(ins, S["xn_ready"]) if tt == 1 else step(ins)
                take_hT(gs, mod)

                def conv(dst, src, wcol, bcol, m, signal):
                    step(tsc(dst[:, m, :], src[:, m, 0:T], wcol(0, m), bcol(m), ALU.mult, ALU.add))
                    for j in range(1, TAPS):
                        ins = stt(dst[:, m, :], src[:, m, j:j + T], wcol(j, m), dst[:, m, :], ALU.mult, ALU.add)
                        step(ins, signal) if j == TAPS - 1 else step(ins)
                if l == 0:
                    v.wait_ge(S["pads_ready"], 1)
                for m in range(KB):
                    v.wait_ge(A.free, A.upto(f"rx{l}{m}"))
                    conv(rxc, rxv, lambda j, m: colL[:, l, V_RCW + j * KB + m:V_RCW + j * KB + m + 1],
                         lambda m: colL[:, l, V_RCB + m:V_RCB + m + 1], m, S["conv_ready"])
                v.wait_ge(S["rg_gate"], KB * (l + 1))
                step(tten(thr[:, :, :], aa[:, :, :], aa[:, :, :], ALU.mult))
                step(stt(tl[:, :, :], thr[:, :, :], 1.0, tl[:, :, :], ALU.add, ALU.mult), S["rg_root_wanted"])
                step(stt(thi[:, :, :], thi[:, :, :], 1.0, rxc[:, :, :], ALU.add, ALU.mult))
                v.wait_ge(A.free, A.upto(f"rz{l}7"))
                step(stt(zr[:, :, :], mth[:, :, :], 1.0, zr[:, :, :], ALU.add, ALU.mult))
                for m in range(KB):
                    v.wait_ge(A.free, A.upto(f"mx{l}{m}"))
                    conv(mc, mxv, lambda j, m: colL[:, l, V_MCW + j * KB + m:V_MCW + j * KB + m + 1],
                         lambda m: colM[:, l, m:m + 1], m, S["mconv_ready"])
                for m in range(KB):
                    v.wait_ge(S["mtanh_ready"], l * KB + m + 1)
                    step(stt(mc[:, m, :], mth[:, m, :], 1.0, mc[:, m, :], ALU.add, ALU.mult), S["mc_ready"])
                v.wait_ge(S["rg_root"], l + 1)
                step(stt(thi[:, :, :], tl[:, :, :], 0.5, thi[:, :, :], ALU.mult, ALU.mult))
                for h in range(KB):
                    step(v.tensor_tensor_scan(thr[:, h, :], aa[:, h, :], thi[:, h, :], 0.0, ALU.mult, ALU.add))
                step(stt(thr[:, :, :], thr[:, :, :], 0.5, zr[:, :, :], ALU.mult, ALU.mult), S["rg_done"])
                v.wait_ge(S["gate_b_loaded"], 16 * 3 * LAYERS)
                b = B.take(v)
                for r in range(4):
                    step(v.tensor_copy(rows[:, r, :], b[32 * r:32 * r + MLH, 0:T]), B.free if r == 3 else None)
                for r in range(2):
                    step(stt(rows[:, r, :], rows[:, r, :], bif[:, l, r:r + 1], rows[:, 2 + r, :], ALU.add, ALU.add))
                step(tsc(rows[:, 2, :], rows[:, 1, :], -1.0, None, ALU.mult))
                step(tten(rows[:, 2, :], rows[:, 2, :], rows[:, 1, :], ALU.max), S["lf_wanted"])
                v.wait_ge(S["lf_ready"], l + 1)
                log1p(rows[:, 4, :], rows[:, 2, :], rows[:, 5, :], rows[:, 6, :])
                step(stt(rows[:, 1, :], rows[:, 1, :], 0.0, rows[:, 4, :], ALU.min, ALU.subtract))
                for c in range(TT):
                    cs = slice(c * P, (c + 1) * P)
                    step(v.tensor_tensor_scan(rows[:, 7, cs], onesr[:, :], rows[:, 1, cs], 0.0, ALU.mult, ALU.add))
                step(tten(rows[:, 3, :], rows[:, 0, :], rows[:, 7, :], ALU.subtract))
                for c in range(TT):
                    cs = slice(c * P, (c + 1) * P)
                    step(v.tensor_tensor_scan(rows[:, 4, cs], rows[:, 3, cs], rows[:, 3, cs],
                                              0.0 if c == 0 else rsc[:, 1:2], ALU.max, ALU.max))
                    if c == 0:
                        step(tten(rsc[:, 1:2], rows[:, 4, P - 1:P], rows[:, 7, P - 1:P], ALU.add))
                        step(tsc(rsc[:, 0:1], rows[:, 4, P - 1:P], -1.0, None, ALU.mult))
                step(tsc(rows[:, 5, :], rows[:, 4, :], -1.0, None, ALU.mult))
                step(tten(rows[:, 2, :], rows[:, 4, :], rows[:, 7, :], ALU.add), S["row_wanted"])
                v.wait_ge(A.free, A.upto(f"mo{l}31"))
                step(tsc(oth_t[:, :], oth_t[:, :], 1.0, None, ALU.add))
                z_left = list(range(KB))

                def z_job():
                    m = z_left.pop(0)
                    v.wait_ge(A.free, A.upto(f"mz{l}{m}"))
                    step(stt(zm[:, m, :], zth[m % 2], 1.0, zm[:, m, :], ALU.add, ALU.mult), S["zm_ready"])

                b = B.take(v)
                step(v.tensor_copy(cols[:, :, :], b[:, 0:16].rearrange("p (n h) -> p n h", n=4)), B.free)
                z_job()
                z_job()
                for h in range(MLH):
                    step(tsc(knat[:, h, :], knat[:, h, :], cols[:, 0, h:h + 1], None, ALU.mult), S["kw_ready"])
                for c in range(TT):
                    for h in range(MLH):
                        b = B.take(v)
                        v.wait_ge(A.free, A.upto(f"E{l}{c}{h}"))
                        step(stt(stb[:, h % 2, :], b[:, 0:P], MLD ** -0.5, ebuf[:, h % 2, :], ALU.mult, ALU.mult),
                             B.free)
                        b = B.take(v)
                        if c == 0:
                            step(v.tensor_copy(hn[:, :], b[:, 0:VW]), B.free)
                        else:
                            v.wait_ge(A.free, A.upto(f"in{l}{h}"))
                            step(tten(hn[:, :], b[:, 0:VW], inter[:, h % 2, :], ALU.add), B.free)
                        step(tsc(rt[:, 0:1], hn[:, MLD:VW], -1.0, None, ALU.mult))
                        step(tten(rt[:, 0:1], rt[:, 0:1], hn[:, MLD:VW], ALU.max))
                        step(tten(rt[:, 0:1], rt[:, 0:1], cols[:, 2 + c, h:h + 1], ALU.max))
                        step(v.reciprocal(rt[:, 1:2], rt[:, 0:1]))
                        step(stt(hh[:, c, h * MLD:(h + 1) * MLD], hn[:, 0:MLD], rt[:, 1:2],
                                 oth[:, c, h * MLD:(h + 1) * MLD], ALU.mult, ALU.mult), S["hh_ready"])
                        if z_left:
                            z_job()
                roots_n["ssq"] += 8
                v.wait_ge(S["ssq_ready"], roots_n["ssq"])
                rstd(small[:, 24:32], small[:, 16:24], 0.25 / MLD)
                step(tsc(small[:, 24:32], small[:, 24:32], 0.25, None, ALU.mult))
                for c in range(TT):
                    for h in range(MLH):
                        hv = hh[:, c, h * MLD:(h + 1) * MLD]
                        n = 24 + c * MLH + h
                        ins = tsc(hv, hv, small[:, n:n + 1], None, ALU.mult)
                        step(ins, S["hq_ready"]) if (c, h) == (1, MLH - 1) else step(ins)
                for m in range(KB):
                    b = B.take(v)
                    step(stt(ymT[:, m, :], b[:, 0:T], colM[:, l, 8 + m:9 + m], zm[:, m, :], ALU.mult, ALU.mult), B.free)
                for j in range(4):
                    for tt in range(TT):
                        n = A.upto(f"xo{l}{j}{tt}")
                        v.wait_ge(A.done, n)
                        cs = slice(j * CW, (j + 1) * CW)
                        tten(gated[:, tt, :], A.bank(n)[:, 0:CW], gateB[:, cs], ALU.mult).then_inc(A.free, 1)
                        v.wait_ge(A.free, n)
                        ins = tten(x[:, tt, cs], x[:, tt, cs], gated[:, tt, :], ALU.add)
                        step(ins, (S["tile0_done"], S["layer_done"])[tt] if j == 3 else None)
            norm_x()
            v.wait_ge(S["gfin_loaded"], 32)
            for tt in range(TT):
                step(stt(xn[:, tt, :], x[:, tt, :], small[:, 2 + tt:3 + tt], gfin[:, :], ALU.mult, ALU.mult),
                     S["layer_done"])

        @block.gpsimd
        def _(g):
            step = Chain(g, s_pool)
            step(g.memset(ident[:, :], 0.0))
            step(g.affine_select(out=ident[:, :], in_=ident[:, :], compare_op=ALU.not_equal, fill=1.0, base=0,
                                 pattern=[[-1, P]], channel_multiplier=1), S["ident_ready"])
            g.dma_start(norm2, bcast(a["norm2_g"][0], D)).then_inc(S["norm2_loaded"], 16)
            s = S["small_loaded"]
            NR = EG + EXPERTS
            g.dma_start(wi_w[:, :, :], cols_of(w_in, C_WI, 8)).then_inc(s, 16)
            g.dma_start(rt_w[:, :, 0:EG], cols_of(a["router_group_w"][0], 0, EG)).then_inc(s, 16)
            g.dma_start(rt_w[:, :, EG:NR], cols_of(a["router_expert_w"][0], 0, EXPERTS)).then_inc(s, 16)
            g.dma_start(rt_b[0:1, 0:EG], a["router_group_b"]).then_inc(s, 16)
            g.dma_start(rt_b[0:1, EG:NR], a["router_expert_b"]).then_inc(s, 16)
            g.dma_start(wuk, a["w_uk"][0].rearrange("r h d -> r (h d)")).then_inc(S["attn_loaded"], 16)
            g.dma_start(wuv, a["w_uv"][0].rearrange("r h d -> r (h d)")).then_inc(S["attn_loaded"], 16)
            g.dma_start(wsn, a["w_spatial"][0].rearrange("g i j -> i g j")).then_inc(S["ws_loaded"], 16)
            g.dma_start(lng, bcast(a["ln_v_g"][0], 512)).then_inc(S["ln_loaded"], 16)
            g.dma_start(lnb, bcast(a["ln_v_b"][0], 512)).then_inc(S["ln_loaded"], 16)
            g.dma_start(bsp[0:1, :], a["b_spatial"].rearrange("a g i -> a (g i)")).then_inc(S["ln_loaded"], 16)
            step(g.memset(anti[:, :], 0.0))
            step(g.affine_select(out=anti[:, :], in_=anti[:, :], compare_op=ALU.not_equal, fill=1.0 / SCALE,
                                 base=1 - P, pattern=[[1, P]], channel_multiplier=1))
            step(g.memset(later[:, :], 0.0))
            step(g.affine_select(out=later[:, :], in_=later[:, :], compare_op=ALU.is_ge, fill=-BIG, base=0,
                                 pattern=[[1, P]], channel_multiplier=-1))
            step(g.memset(ones[:, :], 1.0))
            step(g.memset(allone[:, :], 1.0))
            step(g.memset(upto, 1.0))
            step(g.affine_select(out=upto, in_=upto, compare_op=ALU.is_ge, fill=0.0, base=0, pattern=[[1, P]],
                                 channel_multiplier=-1))
            step(g.memset(onesr[:, :], 1.0))
            step(g.memset(sel4[:, :, :], 0.0))
            step(g.affine_select(out=sel4[:, :, :], in_=sel4[:, :, :], compare_op=ALU.not_equal, fill=1.0, base=0,
                                 pattern=[[-1, MLH], [0, P]], channel_multiplier=1))
            for k in range(EPG):
                step(g.memset(desc[:, k:k + 1], float(EPG - k)), S["const_ready"] if k == EPG - 1 else None)
            g.wait_ge(B.free, B.upto("relrow"))
            g.dma_start(relscr_ap, relrow).then_inc(S["relrow_stored"], 16)
            g.wait_ge(S["relrow_stored"], 16)
            g.dma_start(biasT, diag).then_inc(S["bias_loaded"], 16)
            g.wait_ge(S["ws_loaded"], 16)
            step(g.affine_select(out=wsn, in_=wsn, compare_op=ALU.is_ge, fill=0.0, base=0,
                                 pattern=[[0, GROUPS], [-1, P]], channel_multiplier=1), S["ws_masked"])
            ada = {"n": 0}

            def ada_sums(count):
                for n in range(ada["n"], ada["n"] + count):
                    c = ada_chunks[n]
                    g.wait_ge(slot_full[c % RING], fill_value[c])
                    if n >= 3:
                        g.wait_ge(A.done, A.upto(f"ada{n - 3}"))
                    w = full(ring[c % RING])
                    step(g.tensor_tensor(w, w, csil[:, :].unsqueeze(2).broadcast_to([P, KB, CW]), ALU.mult))
                    step(g.tensor_tensor(w[:, 0:4, :], w[:, 0:4, :], w[:, 4:8, :], ALU.add))
                    step(g.tensor_tensor(w[:, 0:2, :], w[:, 0:2, :], w[:, 2:4, :], ALU.add))
                    step(g.tensor_tensor(adasum[:, n % 3, :], w[:, 0, :], w[:, 1, :], ALU.add), S["ada_summed"])
                ada["n"] += count

            g.wait_ge(S["csil_ready"], 1)
            ada_sums(4)
            for tt in range(TT):
                ns = (tt + 1) * P
                g.wait_ge(S["relu_used"], (tt + 1) * HEADS)
                step(g.affine_select(out=idx[:, tt, 0:ns], in_=idx[:, tt, 0:ns], compare_op=ALU.is_ge, fill=MASKED,
                                     base=tt * P, pattern=[[-1, ns]], channel_multiplier=1), S["idx_masked"])
            ada_sums(2)
            for tt in range(TT):
                ns = (tt + 1) * P
                g.wait_ge(S["sel_ready"], tt + 1)
                step(g.affine_select(out=maskb[:, tt, 0:ns], in_=maskb[:, tt, 0:ns], compare_op=ALU.is_ge, fill=-BIG,
                                     base=tt * P, pattern=[[-1, ns]], channel_multiplier=1), S["mask_ready"])
            ada_sums(2)
            for l in range(LAYERS):
                g.dma_start(wif[:, l, :, :], a["ml_w_if_2"][l].rearrange("(k p) g -> p k g", p=P)) \
                    .then_inc(S["gate_b_loaded"], 16)
                for k in range(2):
                    g.dma_start(bif[:, l, k:k + 1], a["ml_b_if_2"][l, k * MLH:(k + 1) * MLH].rearrange("(h o) -> h o", o=1)) \
                        .then_inc(S["gate_b_loaded"], 16)
            g.wait_ge(S["vln_ready"], 1)
            g.dma_start(gfin[:, :], bcast(a["final_norm_g"], D)).then_inc(S["gfin_loaded"], 16)
            ada_sums(ADA_POOL - ada["n"])
            g.wait_ge(S["xg_ready"], 2)
            step(g.memset(rxv[:, :, 0:PAD], 0.0))
            step(g.memset(mxv[:, :, 0:PAD], 0.0))
            step(g.memset(vaug[:, :, :, MLD:VW], 1.0), S["pads_ready"])
            g.wait_ge(S["layer_done"], LAYERS)
            g.dma_start(gfin[:, :], bcast(a["final_g_2"], D)).then_inc(S["gfin_loaded"], 16)


def bucket_of_distance():
    n = np.maximum(T - 1 - np.arange(512), 0)
    exact = BUCKETS // 2
    nf = np.maximum(n, 1).astype(np.float32)
    large = exact + (np.log(nf / np.float32(exact)) / np.float32(np.log(128 / exact))
                     * np.float32(BUCKETS - exact)).astype(np.int32)
    bucket = np.where(n < exact, n, np.minimum(large, BUCKETS - 1))
    return (np.arange(BUCKETS)[:, None] == bucket[None, :]).astype(np.float32)


def kernel(**inputs):
    import concourse.bacc as bacc
    from concourse.bass_utils import run_bass_kernel_spmd

    nc = bacc.Bacc("TRN2", target_bir_lowering=False, num_devices=1)
    arrays, args = {}, {}
    for name, value in list(inputs.items()) + [("bucket_of_distance", bucket_of_distance())]:
        value = np.ascontiguousarray(value)
        arrays[f"in_{name}"] = value
        args[name] = nc.dram_tensor(f"in_{name}", value.shape, mybir.dt.from_np(value.dtype), kind="ExternalInput").ap()
    out = nc.dram_tensor("out", (1, T, D), F32, kind="ExternalOutput").ap()
    build(nc, args, out)
    result = run_bass_kernel_spmd(nc, [arrays], core_ids=[0])
    return result.results[0]["out"]
```
